# Optimizing a Trainium2 kernel written in Bass

```python
import math
import jax, jax.numpy as jnp
from jax import lax
import numpy as np

D_MODEL = 1024
BATCH = 1
SEQ = 1024
DEPTH = 1
DEC_BATCH = 8
DEC_SEQ = 1
PAST_LEN = 8192
PAGE_SIZE = 128

CONV_W = 1024
CONV_K_A = 3
SSM_INNER = 2 * D_MODEL
SSM_HEADDIM = 64
SSM_HEADS = SSM_INNER // SSM_HEADDIM
SSM_GROUPS = 4
SSM_STATE = 128
CONV_K_S = 4
SSM_XBC = SSM_INNER + 2 * SSM_GROUPS * SSM_STATE
SSD_CHUNK = 128
N_MEM = 256
MEM_HEADS = 4
MEM_HEADDIM = 256
ATTN_W = MEM_HEADS * MEM_HEADDIM
N_BRANCH = 3
EPS = 1e-6
IN_SPLIT_WIDTHS = (CONV_W, CONV_W, CONV_W, CONV_W, SSM_INNER, SSM_XBC, SSM_HEADS, ATTN_W, ATTN_W, N_BRANCH * D_MODEL)
D_IN_TOTAL = 4 * CONV_W + SSM_INNER + SSM_XBC + SSM_HEADS + 2 * ATTN_W + N_BRANCH * D_MODEL

kernel_name = "hybrid_shortconv_ssd_memattn_step"

def rmsnorm(x, w):
    xf = x.astype(jnp.float32)
    y = xf * lax.rsqrt(jnp.mean(xf * xf, axis=-1, keepdims=True) + EPS)
    return (y * w.astype(jnp.float32)).astype(x.dtype)

def gated_rmsnorm(y, z, w):
    bt, L, dd = y.shape
    g = (y * jax.nn.silu(z)).astype(jnp.float32).reshape(bt, L, SSM_GROUPS, dd // SSM_GROUPS)
    g = g * lax.rsqrt(jnp.mean(g * g, axis=-1, keepdims=True) + EPS)
    return (g.reshape(bt, L, dd) * w.astype(jnp.float32)).astype(y.dtype)

def causal_conv(u, buf, w, bias=None):
    k, c = w.shape
    full = jnp.concatenate([buf.astype(u.dtype), u], axis=1)
    y = lax.conv_general_dilated(full, w[:, None, :].astype(u.dtype), window_strides=(1,), padding='VALID',
                                 dimension_numbers=('NWC', 'WIO', 'NWC'), feature_group_count=c)
    if bias is not None:
        y = y + bias.astype(u.dtype)
    return y, full[:, -(k - 1):]

def ssd_scan(x, dt, a, b, c, h0):
    bt, L, H, P = x.shape
    G, N = b.shape[2], b.shape[3]
    HG = H // G
    q = SSD_CHUNK if L >= SSD_CHUNK else L
    nc = -(-L // q)
    pad = nc * q - L
    f32 = jnp.float32
    xf, bf, cf, dtf = x.astype(f32), b.astype(f32), c.astype(f32), dt.astype(f32)
    if pad:
        xf = jnp.pad(xf, ((0, 0), (0, pad), (0, 0), (0, 0)))
        bf = jnp.pad(bf, ((0, 0), (0, pad), (0, 0), (0, 0)))
        cf = jnp.pad(cf, ((0, 0), (0, pad), (0, 0), (0, 0)))
        dtf = jnp.pad(dtf, ((0, 0), (0, pad), (0, 0)))
    xf = xf.reshape(bt, nc, q, G, HG, P)
    dtf = dtf.reshape(bt, nc, q, G, HG)
    bf = bf.reshape(bt, nc, q, G, N)
    cf = cf.reshape(bt, nc, q, G, N)
    da = dtf * a.astype(f32).reshape(G, HG)
    cs = jnp.cumsum(da, axis=2)
    xdt = xf * dtf[..., None]
    seg = cs[:, :, :, None] - cs[:, :, None, :]
    mask = jnp.tril(jnp.ones((q, q), dtype=bool))[:, :, None, None]
    lmat = jnp.exp(jnp.where(mask, seg, -jnp.inf))
    scores = jnp.einsum('bclgn,bcsgn->bclsg', cf, bf)
    y_diag = jnp.einsum('bclsgh,bcsghp->bclghp', scores[..., None] * lmat, xdt)
    decay = jnp.exp(cs[:, :, -1:] - cs)
    st = jnp.einsum('bclgn,bclghp->bcghpn', bf, xdt * decay[..., None])
    total = jnp.exp(cs[:, :, -1])

    def step(h, inp):
        tot, s = inp
        return tot[..., None, None] * h + s, h

    h_init = h0.astype(f32).reshape(bt, G, HG, P, N)
    h_fin, h_prev = lax.scan(step, h_init, (jnp.moveaxis(total, 1, 0), jnp.moveaxis(st, 1, 0)))
    h_prev = jnp.moveaxis(h_prev, 0, 1)
    y_off = jnp.einsum('bclgn,bcghpn->bclghp', cf, h_prev) * jnp.exp(cs)[..., None]
    y = (y_diag + y_off).reshape(bt, nc * q, H, P)[:, :L]
    return y.astype(x.dtype), h_fin.reshape(bt, H, P, N).astype(h0.dtype)

def mem_kv(mem, mem_norm_w, w_mem_kv):
    bt = mem.shape[0]
    kv = rmsnorm(mem, mem_norm_w) @ w_mem_kv
    k, v = jnp.split(kv, 2, axis=-1)
    return (k.reshape(bt, N_MEM, MEM_HEADS, MEM_HEADDIM), v.reshape(bt, N_MEM, MEM_HEADS, MEM_HEADDIM))

def mem_attention(q, k, v):
    s = jnp.einsum('blhd,bmhd->bhlm', q, k).astype(jnp.float32) * (1.0 / math.sqrt(MEM_HEADDIM))
    p = jax.nn.softmax(s, axis=-1).astype(v.dtype)
    return jnp.einsum('bhlm,bmhd->blhd', p, v)

def mixer_layer(x, mk, mv, buf_a, buf_s, h0, norm_w, w_in, conv_a_w, w_a_out, conv_s_w, conv_s_b,
                dt_bias, a_log, d_skip, ssm_norm_w, w_s_out, w_m_out, w_o):
    bt, L, _ = x.shape
    u = rmsnorm(x, norm_w)
    proj = u @ w_in
    idx = [int(i) for i in np.cumsum(IN_SPLIT_WIDTHS)[:-1]]
    cb, cc, ch, cz, sz, sxbc, sdt, mq, mz, gr = jnp.split(proj, idx, axis=-1)
    conv_out, new_buf_a = causal_conv(cc * ch, buf_a, conv_a_w)
    y_a = (jax.nn.silu(cz) * cb * conv_out) @ w_a_out
    xbc, new_buf_s = causal_conv(sxbc, buf_s, conv_s_w, conv_s_b)
    xbc = jax.nn.silu(xbc)
    xs, bm, cm = jnp.split(xbc, [SSM_INNER, SSM_INNER + SSM_GROUPS * SSM_STATE], axis=-1)
    xs = xs.reshape(bt, L, SSM_HEADS, SSM_HEADDIM)
    bm = bm.reshape(bt, L, SSM_GROUPS, SSM_STATE)
    cm = cm.reshape(bt, L, SSM_GROUPS, SSM_STATE)
    dt = jax.nn.softplus(sdt.astype(jnp.float32) + dt_bias.astype(jnp.float32))
    a = -jnp.exp(a_log.astype(jnp.float32))
    y, h_new = ssd_scan(xs, dt, a, bm, cm, h0)
    y = y + d_skip[:, None].astype(y.dtype) * xs
    y_s = gated_rmsnorm(y.reshape(bt, L, SSM_INNER), sz, ssm_norm_w) @ w_s_out
    o = mem_attention(mq.reshape(bt, L, MEM_HEADS, MEM_HEADDIM), mk, mv)
    y_m = (jax.nn.silu(mz) * o.reshape(bt, L, ATTN_W)) @ w_m_out
    g = jax.nn.sigmoid(gr.astype(jnp.float32)).astype(x.dtype).reshape(bt, L, N_BRANCH, D_MODEL)
    merged = g[:, :, 0] * y_a + g[:, :, 1] * y_s + g[:, :, 2] * y_m
    return x + merged @ w_o, new_buf_a, new_buf_s, h_new

def setup_inputs(seed: int = 0) -> dict:
    key = jax.random.key(seed)
    ks = jax.random.split(key, 24)

    def nrm(k, shape, scale):
        return jax.random.normal(k, shape, jnp.float32) * scale

    dt0 = jnp.exp(jax.random.uniform(ks[14], (DEPTH, SSM_HEADS)) * (math.log(0.1) - math.log(0.001)) + math.log(0.001))
    return {
        "x_prompt": nrm(ks[0], (BATCH, SEQ, D_MODEL), 1.0),
        "x_sample": nrm(ks[1], (DEC_BATCH, DEC_SEQ, D_MODEL), 1.0),
        "mem_prompt": nrm(ks[2], (BATCH, N_MEM, D_MODEL), 1.0),
        "state_conv_a": nrm(ks[3], (DEPTH, DEC_BATCH, CONV_K_A - 1, CONV_W), 1.0),
        "state_conv_s": nrm(ks[4], (DEPTH, DEC_BATCH, CONV_K_S - 1, SSM_XBC), 1.0),
        "state_ssm": nrm(ks[5], (DEPTH, DEC_BATCH, SSM_HEADS, SSM_HEADDIM, SSM_STATE), 0.1),
        "cache_mem_k": nrm(ks[6], (DEPTH, DEC_BATCH, N_MEM, MEM_HEADS, MEM_HEADDIM), 1.0),
        "cache_mem_v": nrm(ks[7], (DEPTH, DEC_BATCH, N_MEM, MEM_HEADS, MEM_HEADDIM), 1.0),
        "norm_w": 1.0 + nrm(ks[8], (DEPTH, D_MODEL), 0.02),
        "w_in": nrm(ks[9], (DEPTH, D_MODEL, D_IN_TOTAL), D_MODEL ** -0.5),
        "conv_a_w": nrm(ks[10], (DEPTH, CONV_K_A, CONV_W), CONV_K_A ** -0.5),
        "w_a_out": nrm(ks[11], (DEPTH, CONV_W, D_MODEL), CONV_W ** -0.5),
        "conv_s_w": nrm(ks[12], (DEPTH, CONV_K_S, SSM_XBC), CONV_K_S ** -0.5),
        "conv_s_b": nrm(ks[13], (DEPTH, SSM_XBC), 0.01),
        "dt_bias": dt0 + jnp.log(-jnp.expm1(-dt0)),
        "a_log": jnp.log(jax.random.uniform(ks[15], (DEPTH, SSM_HEADS), minval=1.0, maxval=16.0)),
        "d_skip": 1.0 + nrm(ks[16], (DEPTH, SSM_HEADS), 0.1),
        "ssm_norm_w": 1.0 + nrm(ks[17], (DEPTH, SSM_INNER), 0.02),
        "w_s_out": nrm(ks[18], (DEPTH, SSM_INNER, D_MODEL), SSM_INNER ** -0.5),
        "mem_norm_w": 1.0 + nrm(ks[19], (DEPTH, D_MODEL), 0.02),
        "w_mem_kv": nrm(ks[20], (DEPTH, D_MODEL, 2 * ATTN_W), D_MODEL ** -0.5),
        "w_m_out": nrm(ks[21], (DEPTH, ATTN_W, D_MODEL), ATTN_W ** -0.5),
        "w_o": nrm(ks[22], (DEPTH, D_MODEL, D_MODEL), D_MODEL ** -0.5),
        "final_norm_w": 1.0 + nrm(ks[23], (D_MODEL,), 0.02),
    }

def reference(x_prompt, x_sample, mem_prompt, state_conv_a, state_conv_s, state_ssm, cache_mem_k, cache_mem_v,
              norm_w, w_in, conv_a_w, w_a_out, conv_s_w, conv_s_b, dt_bias, a_log, d_skip, ssm_norm_w,
              w_s_out, mem_norm_w, w_mem_kv, w_m_out, w_o, final_norm_w):
    bp = x_prompt.shape[0]
    dtp = x_prompt.dtype
    x = x_prompt
    pa, ps, ph, pk, pv = [], [], [], [], []
    for l in range(DEPTH):
        mk, mv = mem_kv(mem_prompt, mem_norm_w[l], w_mem_kv[l])
        buf_a = jnp.zeros((bp, CONV_K_A - 1, CONV_W), dtp)
        buf_s = jnp.zeros((bp, CONV_K_S - 1, SSM_XBC), dtp)
        h0 = jnp.zeros((bp, SSM_HEADS, SSM_HEADDIM, SSM_STATE), dtp)
        x, na, ns, nh = mixer_layer(x, mk, mv, buf_a, buf_s, h0, norm_w[l], w_in[l], conv_a_w[l], w_a_out[l],
                                    conv_s_w[l], conv_s_b[l], dt_bias[l], a_log[l], d_skip[l], ssm_norm_w[l],
                                    w_s_out[l], w_m_out[l], w_o[l])
        pa.append(na); ps.append(ns); ph.append(nh); pk.append(mk); pv.append(mv)
    y_prompt = rmsnorm(x, final_norm_w)
    x = x_sample
    sa, ss, sh = [], [], []
    for l in range(DEPTH):
        x, na, ns, nh = mixer_layer(x, cache_mem_k[l], cache_mem_v[l], state_conv_a[l], state_conv_s[l],
                                    state_ssm[l], norm_w[l], w_in[l], conv_a_w[l], w_a_out[l],
                                    conv_s_w[l], conv_s_b[l], dt_bias[l], a_log[l], d_skip[l], ssm_norm_w[l],
                                    w_s_out[l], w_m_out[l], w_o[l])
        sa.append(na); ss.append(ns); sh.append(nh)
    y_sample = rmsnorm(x, final_norm_w)
    return (y_prompt, y_sample,
            jnp.stack(pa), jnp.stack(ps), jnp.stack(ph), jnp.stack(pk), jnp.stack(pv),
            jnp.stack(sa), jnp.stack(ss), jnp.stack(sh))


_drawn_inputs = setup_inputs


def setup_inputs(seed=0):
    import zlib

    import numpy as np

    out = dict(_drawn_inputs(seed))
    spreads = {}
    factors = {'conv_s_b': 3.329,
     'ssm_norm_w': 18.113,
     'mem_norm_w': 7.974,
     'final_norm_w': 8.469,
     'cache_mem_k': 7.621,
     'cache_mem_v': 5.921}
    for name, (base, spread) in spreads.items():
        noise = np.random.default_rng([zlib.crc32(name.encode()), seed]).standard_normal(out[name].shape)
        drawn = base * np.exp(spread * noise) if base else spread * noise
        out[name] = __import__('jax').numpy.asarray(drawn.astype(out[name].dtype))
    for name, factor in factors.items():
        out[name] = (out[name] * factor).astype(out[name].dtype)
    return out
```

```python
from contextlib import ExitStack

import concourse.bass as bass
from concourse import mybir

ALU = mybir.AluOpType
ACT = mybir.ActivationFunctionType
AX = mybir.AxisListType
F32 = mybir.dt.float32
F32R = mybir.dt.float32r

P = 128
D = 1024
SEQ = 1024
NB = 8
T = SEQ + NB
KT = D // P
NP = 3
PC = T // NP
INNER = 2 * D
HEADS, HD = 32, 64
GROUPS, HG = 4, 8
NS = 128
XBC = INNER + 2 * GROUPS * NS
KS, KA = 4, 3
CH = 128
NCH = SEQ // CH
NM, MH, MD = 256, 4, 256
EPS = 1e-6
ZT, XT = INNER // P, XBC // P
O_CB, O_CC, O_CH, O_CZ, O_SZ = 0, D, 2 * D, 3 * D, 4 * D
O_XBC = O_SZ + INNER
O_DT = O_XBC + XBC
O_MQ = O_DT + HEADS
O_MZ = O_MQ + D
O_G = O_MZ + D
C_SW, C_SB, C_NW = 0, KS * XT, KS * XT + XT
C_AW = C_NW + KT
C_SN = C_AW + KA * KT
C_MN = C_SN + ZT
NPAR = C_MN + KT
TAIL_S, TAIL_A = KS - 1 + NB, KA - 1 + NB
LOG1P_TERMS = 9


def build(nc, I, O):
    dram = lambda n, s: nc.dram_tensor(n, s, F32, kind="Internal").ap()
    s_xbc = dram("s_xbc", (XBC, T))
    s_z = dram("s_z", (INNER, T))
    s_q = dram("s_q", (D, T))
    s_mz = dram("s_mz", (D, T))
    s_g = dram("s_g", (3 * D, T))
    s_a = dram("s_a", (D, T))
    s_y = dram("s_y", (INNER, T))
    s_o = dram("s_o", (D, T))
    s_cs = dram("s_cs", (HEADS, SEQ))
    s_dd = dram("s_dd", (HEADS, 2, NB))
    s_bc = dram("s_bc", (NCH, 2, NB, P))
    s_kt = dram("s_kt", (D, NM))
    s_qd = dram("s_qd", (KT * NB, P))

    w_in = I["w_in"][0].rearrange("(k p) n -> p k n", p=P)
    w_kv = I["w_mem_kv"][0].rearrange("(k p) n -> p k n", p=P)

    with ExitStack() as ctx:
        used = [0]

        def sb(name, shape, dt=F32):
            n = 1
            for s in shape[1:]:
                n *= s
            used[0] += 4 * n
            return ctx.enter_context(nc.sbuf_tensor(name, shape, dt))

        def sem(name):
            return ctx.enter_context(nc.semaphore(name))

        acc = ctx.enter_context(nc.psum_tensor("acc", [P, NP, 512], F32))
        pm = [ctx.enter_context(nc.psum_tensor(f"pm{i}", [P, 512], F32)) for i in range(5)]
        uhi = sb("uhi", [P, KT, T], F32R)
        ulo = sb("ulo", [P, KT, T], F32R)
        raw = [sb(f"raw{r}", [P, KT, P]) for r in range(3)]
        whi = [sb(f"whi{r}", [P, KT, P], F32R) for r in range(3)]
        wlo = [sb(f"wlo{r}", [P, KT, P], F32R) for r in range(3)]
        stage = [sb(f"stage{r}", [P, T]) for r in range(3)]
        ident = sb("ident", [P, P])
        tri = sb("tri", [P, P])
        ones = sb("ones", [P, P])
        negh = sb("negh", [P, 1])
        epsc = sb("epsc", [P, 1])
        par = sb("par", [P, NPAR])
        hist_s = sb("hist_s", [P, XT, NB, KS - 1])
        hist_a = sb("hist_a", [P, KT, NB, KA - 1])
        tail_s = sb("tail_s", [P, XT, TAIL_S])
        tail_a = sb("tail_a", [P, KT, TAIL_A])
        cs_tok = sb("cs_tok", [P, NCH * HEADS])
        dt_tok = sb("dt_tok", [P, NCH * HEADS])
        dskip = sb("dskip", [P, HEADS])
        ARENA = 22096
        with nc.sbuf_tensor("mhi", [P, KT, NM], F32R) as mhi, nc.sbuf_tensor("mlo", [P, KT, NM], F32R) as mlo:
            pass
        arena = sb("arena", [P, ARENA])

        M0 = 2 * KT * NM
        cursor = [M0]

        def view(*shape, at=None):
            n = 1
            for s in shape:
                n *= s
            if at is None:
                at = cursor[0]
            cursor[0] = at + n
            assert cursor[0] <= ARENA, (cursor[0], shape)
            v = arena[:, at:at + n]
            if len(shape) == 2:
                v = v.rearrange("p (a b) -> p a b", b=shape[1])
            if len(shape) == 3:
                v = v.rearrange("p (a b c) -> p a b c", b=shape[1], c=shape[2])
            return v

        w_loaded = [sem(f"w_loaded{r}") for r in range(3)]
        w_high = [sem(f"w_high{r}") for r in range(3)]
        w_split = [sem(f"w_split{r}") for r in range(3)]
        ready = [sem(f"ready{p}") for p in range(NP - 1)]
        done = [sem(f"done{r}") for r in range(3)]
        evac = [sem(f"evac{p}") for p in range(NP)]
        stored = [sem(f"stored{r}") for r in range(3)]

        const_ready = sem("const_ready")

        paced = sem("paced")
        pace = [0]

        def settle(e, times=1):
            pace[0] += times
            e.sem_inc(paced, 1)

        def load_w(sp, t, src):
            sp.wait_ge(w_split[t[1]], t[0] + 1)
            settle(sp)
            sp.dma_start(raw[t[1]][:], src).then_inc(w_loaded[t[1]], 16)

        def split_w(pool, t):
            q, r = t[0], t[1]
            pool.wait_ge(w_loaded[r], (q + 1) * 16)
            pool.wait_ge(done[r], q + 1)
            settle(pool)
            pool.tensor_scalar(whi[r][:], raw[r][:], 1.0, 0.0, ALU.mult, ALU.add).then_inc(w_high[r], 1)
            pool.wait_ge(w_high[r], q + 1)
            pool.tensor_tensor(wlo[r][:], raw[r][:], whi[r][:].bitcast(F32), ALU.subtract).then_inc(w_split[r], 1)

        def dense(pe, t, hi, lo, pieces=((0, 0), (1, PC), (2, 2 * PC)), n=PC, acts=None):
            q, r, full, total = t
            pe.wait_ge(w_split[r], q + 1 + 1)
            for p, c0 in pieces:
                pe.wait_ge(evac[p], (total if p == NP - 1 else full) + 1)
                if acts:
                    pe.wait_ge(acts[0], acts[1] + p + 1)
                for k in range(KT):
                    for s, (w, a) in enumerate(((whi, hi), (wlo, hi), (whi, lo))):
                        mm = pe.matmul(acc[:, p, 0:n], w[r][:, k, :], a[:, k, c0:c0 + n],
                                       start=k == 0 and s == 0, stop=k == KT - 1 and s == 2)
                mm.then_inc(done[r] if p == NP - 1 else ready[p], 1)

        def piece_ready(e, t, p):
            if p == NP - 1:
                e.wait_ge(done[t[1]], t[0] + 1 + 1)
            else:
                e.wait_ge(ready[p], t[2] + 1)

        def read_out(act, t, out, func, scale=1.0):
            for p in range(NP):
                piece_ready(act, t, p)
                act.activation(out[:, p * PC:(p + 1) * PC], acc[:, p, 0:PC], func, scale=scale).then_inc(evac[p], 1)

        def evacuated(e, t):
            for p in range(NP):
                e.wait_ge(evac[p], ((t[3] if p == NP - 1 else t[2]) + 1) + 1)

        def to_dram(act, t, use, dst, func, scale=1.0):
            r = t[1]
            act.wait_ge(stored[r], use * 16 + 1)
            read_out(act, t, stage[r], func, scale)
            evacuated(act, t)
            act.dma_start(dst, stage[r][:]).then_inc(stored[r], 16)

        xbc_tile = lambda i, r: (i, r, i * 3 + r, i * 3 + r)
        z_tile = lambda i, r: (i + XT // 3, r, i * 3 + XT + r, i * 3 + XT + r)
        QL, FL = XT // 3 + 5, XT + 15
        last_z, dt_tile, kv0 = (QL, 0, FL, FL), (QL, 1, FL + 1, FL + 1), (QL, 2, None, FL + 2)
        kv_tile = lambda i, r: (i + QL + 1, r, None, i * 3 + FL + 3 + r)
        QM, FM, TM = QL + 6, FL + 2, FL + 18
        main_tile = lambda c, m: (c * 3 + QM + m // 3, m % 3, c * 9 + FM + m, c * 9 + TM + m)

        xbc_src = lambda j: w_in[:, :, bass.ds(j * P + O_XBC, P)]
        z_src = lambda j: w_in[:, :, bass.ds(j * P + O_SZ, P)]
        kv_src = lambda j: w_kv[:, :, bass.ds(j * P, P)]
        MAIN = (O_CC, O_CH, O_CZ, O_CB, O_MQ, O_MZ, O_G, O_G + D, O_G + 2 * D)
        rows = lambda d, j: d[bass.ds(j * P, P), :]

        rows_in = [sem(f"rows_in{b}") for b in range(2)]
        par_in, hist_in, small_in = sem("par_in"), sem("hist_in"), sem("small_in")
        square_done, root_done, rs_done = sem("square_done"), sem("root_done"), sem("rs_done")
        normed = [sem(f"normed{b}") for b in range(2)]
        turned, u_high, u_split = sem("turned"), sem("u_high"), sem("u_split")
        par_turned, par_copied = sem("par_turned"), sem("par_copied")
        xr = [view(D), view(D)]
        xn = [view(D), view(D)]
        nwb, mwb = view(D), view(D)
        junk = view(D)
        par_rows = view(2, P)
        hrow_s, hrow_a = view(XBC), view(D)
        ssq, root, rs = view(16), view(16), view(16)
        NROW = SEQ // P + 1 + NM // P
        def row_tile(a):
            if a < SEQ // P:
                return P, I["x_prompt"][0, a * P:(a + 1) * P, :], a * P
            if a == SEQ // P:
                return NB, I["x_sample"][:, 0, :], SEQ
            a -= SEQ // P + 1
            return P, I["mem_prompt"][0, a * P:(a + 1) * P, :], a * P
        xp = view(T + KS - 1, at=M0 + 15900)
        cv = view(T)
        dtb, alog = view(1), view(1)
        conv = [sem(f"conv{k}") for k in range(KS)]
        silu_done, tails_kept, pads_ready = sem("silu_done"), sem("tails_kept"), sem("pads_ready")

        kv_t = view(2 * KT, NM, at=M0)
        kv_tok = view(2, 2, D)
        kv_saved = sem("kv_saved")
        pre_turned, pre_copied = sem("pre_turned"), sem("pre_copied")
        DT0 = M0 + 8192
        dtv = view(T, at=DT0)
        absv, expo, zz, csv = view(T), view(T), view(T), view(T)
        da, resets = absv, zz
        aneg, dd = view(1), view(2, NB)
        dt_step, dt_abs, dt_exp, a_exp = sem("dt_step"), sem("dt_abs"), sem("dt_exp"), sem("a_exp")
        dt_ready, cs_ready, dd_exp, dd_ready, cs_saved = sem("dt_ready"), sem("cs_ready"), sem("dd_exp"), sem("dd_ready"), sem("cs_saved")
        bcx, bcr = view(8, NB), view(P)
        bcx_in, bc_saved, dec_in = (sem(n) for n in ("bcx_in", "bc_saved", "dec_in"))
        SEG = ((0, 1), (2, 3), (4, 5), (6, 7, 8))
        xg = [view(6, CH, at=0 if b == 0 else None) for b in range(2)]
        zg = [view(4, CH) for b in range(2)]
        csb = [view(HG, CH) for b in range(2)]
        xt, bt, scm = view(512), view(CH), view(CH)
        xdt, xdd = view(512), view(512)
        seg, mm_ = view(HG, CH), view(HG, CH)
        yv, gy, gyn, yT = view(512), view(512), view(512), view(4, CH)
        hT_at = ARENA - GROUPS * 512
        sa, sm = view(3, HG), view(3, HG)
        ss2, rt2, rs2, nw2, var2 = view(1), view(1), view(1), view(1), view(1)
        cc, zc, av = view(T), view(T), view(T)
        hb = view(T + KA - 1)
        bcd = view(2, NB, P)
        sd, sd2 = view(NB, P), view(NB, P)
        dec_x, dec_z, dec_xdt, dec_y, dec_sq = (view(ZT, NB) for _ in range(5))
        dec_dd = view(ZT, 2, NB)
        dec_skip = view(ZT)
        dec_ms, dec_rs, dec_nw = view(GROUPS, NB), view(GROUPS, NB), view(GROUPS, NB)
        assert cursor[0] <= hT_at, (cursor[0], hT_at)
        hT = view(GROUPS, 512, at=hT_at)
        bcd_in, sd_in, sd_step, sd_saved, dec_ready = sem("bcd_in"), sem("sd_in"), sem("sd_step"), sem("sd_saved"), sem("dec_ready")
        ssm_in = I["state_ssm"][0].rearrange("b h p n -> (h p) b n")
        ssm_out = O["s_ssm"][0].rearrange("b h p n -> (h p) b n")
        group_in = [sem(f"group_in{b}") for b in range(2)]
        summed = [sem(f"summed{b}") for b in range(2)]
        x_turned, b_ready, z_turned, x_copied = sem("x_turned"), sem("b_ready"), sem("z_turned"), sem("x_copied")
        args_ready, sm_ready, seg_ready, e_ready = sem("args_ready"), sem("sm_ready"), sem("seg_ready"), sem("e_ready")
        bt_ready, sc_ready, xdt_ready, xdd_ready, m_ready = (sem(n) for n in ("bt_ready", "sc_ready", "xdt_ready", "xdd_ready", "m_ready"))
        y_step, gy_ready, h_scaled, h_added = sem("y_step"), sem("gy_ready"), sem("h_scaled"), sem("h_added")
        sq2_done, rt2_done, rs2_step, gyn_ready = sem("sq2_done"), sem("rt2_done"), sem("rs2_step"), sem("gyn_ready")
        y_turned, y_out, y_stored = sem("y_turned"), sem("y_out"), sem("y_stored")
        hb_pad, tails_a_kept, a_conv, a_gate, a_ready = (
            sem(n) for n in ("hb_pad", "tails_a_kept", "a_conv", "a_gate", "a_ready"))
        STAGED = (XT // 3 + 6, XT // 3 + 5, XT // 3 + 5)
        def staged(c, m):
            return c * 2 + STAGED[m % 3] + (m >= 6)
        def bcast(v, n):
            return v.unsqueeze(2).to_broadcast([P, v.shape[1], n])
        def heads(v):
            return v.rearrange("p (h d) -> p h d", h=HG)
        def group_before(e, c, g):
            if g % 2:
                e.wait_ge(summed[0], c * 2 + g // 2 + 1 + 1)
            else:
                e.wait_ge(summed[1], c * 2 + g // 2 + 1)
        PASSES = 5
        SLOT2 = 2
        def out_tile(b, i, r):
            n = i * 2 + (b * KT + r)
            return i + (QM + 24 + b * 4), r, n + (FM + 72), n + (TM + 72)
        OUT_W = [I[w][0].rearrange("(k p) n -> p k n", p=P) for w in ("w_a_out", "w_s_out", "w_m_out", "w_o")]
        out_w = lambda b: (OUT_W[0], OUT_W[1][:, 0:KT], OUT_W[1][:, KT:], OUT_W[2], OUT_W[3])[b]
        GATE = (0, 1, 1, 2)
        tiles_of = lambda d: d.rearrange("(t p) n -> p t n", p=P)
        ACTS = (tiles_of(s_a), tiles_of(s_y)[:, 0:KT], tiles_of(s_y)[:, KT:], tiles_of(s_o))
        merged = view(KT, T, at=0)
        ra = [view(KT, PC) for _ in range(2)]
        R0 = cursor[0]
        aq, ak, avv, amz = view(2, 512), view(2, NM), view(2, MD), view(2, 512)
        pt, ptT = view(4, NM), view(2, 512)
        R1 = cursor[0]
        dk = view(2, D)
        dq = view(D)
        assert cursor[0] <= ARENA, cursor[0]
        pso = view(16, P, at=6144)
        small_at = [0]
        def small(*shape):
            n = 1
            for x in shape:
                n *= x
            v = stage[2][:, small_at[0]:small_at[0] + n]
            small_at[0] += n
            assert small_at[0] <= T
            return v.rearrange("p (a b) -> p a b", b=shape[-1]) if len(shape) == 2 else (
                v if len(shape) == 1 else v.rearrange("p (a b c) -> p a b c", b=shape[1], c=shape[2]))
        qx, qrow = small(KT, NB), small(P)
        amx, anx, asum, arec = small(4), small(4), small(4), small(4)
        sde = small(2, 4)
        sds = small(2, NB, 4)
        dmx, dnx, dsum, drec = small(1), small(1), small(1), small(1)
        dp = small(2, P)
        dpT = small(2, NB * 4)
        mzd, od = small(KT, NB), small(KT, NB)
        fss, frt, frs, fvar, fnw = small(9), small(9), small(9), small(9), small(9)
        SEMS = """h_final h_copied h_saved dec_sq_done dec_summed dec_root dec_step dec_saved qx_in qx_turned qx_copied q_saved
            act_high act_split att_in qk_done att_step att_exp p_turned p_copied pv_done
            att_ready att_saved sam_in sam_read sam_kept sds_turned sam_step sam_exp dp_turned dp_copied
            v_in v_used mzd_in od_ready od_saved tail_turned tail_copied tail_saved copied_dram fw_in row_turned row_sum row_sq
            row_root row_step row_out""".split()
        S = {n: sem(n) for n in SEMS}
        act_in = [sem(f"act_in{b}") for b in range(2)]
        gate_in = [sem(f"gate_in{r}") for r in range(2)]
        merge_done = [sem(f"merge_done{r}") for r in range(2)]
        row_in = [sem(f"row_in{r}") for r in range(2)]
        row_saved = [sem(f"row_saved{r}") for r in range(2)]
        trow_s, trow_a = view(XBC, at=R0), view(D)
        xf = [view(D, at=R0 - 2 * KT * PC)] + [view(D)]
        rr = [view(D) for _ in range(2)]
        fw, fjunk = view(D), view(D)
        TAILS = [(tail_s, trow_s, TAIL_S, n, n) for n in range(6)] + [(tail_a, trow_a, TAIL_A, n, n + 6) for n in range(2)]
        def last_piece(e, b, p):
            if p < NP - 1:
                e.wait_ge(ready[p], FM + 72 + b * KT)
            elif b == 0:
                e.wait_ge(done[2], QM + 24 + 1)
            else:
                e.wait_ge(done[1], QM + 24 + b * 4 + 1)
        OPENED = (*w_split, *done, *evac, *conv, tails_kept, *stored, silu_done, *summed, gy_ready, y_turned, y_stored, a_ready,
                  tails_a_kept, a_conv, sm_ready, m_ready, gyn_ready, sd_step, sd_saved, y_out, *merge_done,
                  *(S[n] for n in ("att_saved", "att_exp", "p_turned", "pv_done", "sam_read", "sam_kept", "v_used",
                                   "att_ready", "p_copied")))

        block = ctx.enter_context(nc.Block())

        @block.sync
        def _(sp):
            for v, (r0, n) in {"conv_s_w": (C_SW, KS * XT), "conv_s_b": (C_SB, XT), "norm_w": (C_NW, KT)}.items():
                src = I[v].rearrange("a (t p) -> (a t) p", p=P) if v != "conv_s_w" else I[v][0].rearrange("k (t p) -> (k t) p", p=P)
                sp.dma_start(par_rows[r0:r0 + n, 0, :], src).then_inc(par_in, 16)
            for v, (r0, n) in {"conv_a_w": (0, KA * KT), "ssm_norm_w": (KA * KT, ZT), "mem_norm_w": (KA * KT + ZT, KT)}.items():
                src = I[v].rearrange("a (t p) -> (a t) p", p=P) if v != "conv_a_w" else I[v][0].rearrange("k (t p) -> (k t) p", p=P)
                sp.dma_start(par_rows[r0:r0 + n, 1, :], src).then_inc(par_in, 16)
            sp.dma_start(nwb, I["norm_w"].to_broadcast([P, D])).then_inc(small_in, 16)
            sp.dma_start(mwb, I["mem_norm_w"].to_broadcast([P, D])).then_inc(small_in, 16)
            sp.dma_start(dskip[:], I["d_skip"].to_broadcast([P, HEADS])).then_inc(small_in, 16)
            sp.dma_start(dtb[0:HEADS, :], I["dt_bias"].rearrange("a h -> h a")).then_inc(small_in, 16)
            sp.dma_start(alog[0:HEADS, :], I["a_log"].rearrange("a h -> h a")).then_inc(small_in, 16)
            sp.dma_start(hrow_s[0:NB * (KS - 1), :], I["state_conv_s"][0].rearrange("b k c -> (b k) c")).then_inc(hist_in, 16)
            sp.dma_start(hrow_a[0:NB * (KA - 1), :], I["state_conv_a"][0].rearrange("b k c -> (b k) c")).then_inc(hist_in, 16)
            for a in range(NROW):
                n, src, _ = row_tile(a)
                if a >= 2:
                    sp.wait_ge(normed[a % 2], a // 2)
                sp.dma_start(xr[a % 2][0:n, :], src).then_inc(rows_in[a % 2], 16)
            with sp.Fori(0, XT // 3) as i:
                for r in range(3):
                    load_w(sp, xbc_tile(i, r), xbc_src(i * 3 + r))
            with sp.Fori(0, 5) as i:
                for r in range(3):
                    load_w(sp, z_tile(i, r), z_src(i * 3 + r))
            load_w(sp, last_z, w_in[:, :, O_SZ + 15 * P:O_SZ + 16 * P])
            load_w(sp, dt_tile, w_in[:, :, O_DT:O_DT + P])
            load_w(sp, kv0, w_kv[:, :, 0:P])
            with sp.Fori(0, 5) as i:
                for r in range(3):
                    load_w(sp, kv_tile(i, r), kv_src(i * 3 + r + 1))
            sp.wait_ge(cs_ready, 1)
            sp.dma_start(s_cs, csv[0:HEADS, 0:SEQ]).then_inc(cs_saved, 16)
            sp.wait_ge(dd_ready, 2)
            sp.dma_start(s_dd, dd[0:HEADS, :, :]).then_inc(cs_saved, 16)
            sp.wait_ge(evac[NP - 1], TM + 1)
            sp.dma_start(s_kt.rearrange("(t p) m -> p t m", p=P), kv_t[:, 0:KT, :]).then_inc(kv_saved, 16)
            for r in range(3):
                sp.wait_ge(stored[r], 16 * (XT // 3) + 1)
            sp.dma_start(bcx, s_xbc[INNER:, SEQ:].rearrange("(t p) b -> p t b", p=P)).then_inc(bcx_in, 16)
            sp.wait_ge(pre_copied, 3)
            for c in range(NCH):
                for s in range(2):
                    r0 = (s * GROUPS + c // 2) * NB
                    sp.dma_start(s_bc[c, s], bcr[r0:r0 + NB, :]).then_inc(bc_saved, 16)
            sp.wait_ge(pre_copied, 11)
            for s, dst in enumerate(("p_mem_k", "p_mem_v")):
                sp.dma_start(O[dst][0, 0].rearrange("(a m) h d -> m a (h d)", m=P), kv_tok[:, s, :, :]).then_inc(kv_saved, 16)
            xbc_t = s_xbc.rearrange("(t p) n -> p t n", p=P)
            z_t = s_z.rearrange("(t p) n -> p t n", p=P)
            sp.wait_ge(kv_saved, 48)
            sp.wait_ge(cs_saved, 32)
            sp.wait_ge(bc_saved, 16 * 16)
            sp.wait_ge(pre_turned, 1)
            for r in range(3):
                sp.wait_ge(stored[r], 16 * STAGED[r] + 1)
            sp.dma_start(dec_x, s_xbc[0:INNER, SEQ:].rearrange("(t p) b -> p t b", p=P)).then_inc(dec_in, 16)
            sp.dma_start(dec_z, s_z[:, SEQ:].rearrange("(t p) b -> p t b", p=P)).then_inc(dec_in, 16)
            for e in range(2):
                part = slice(e * HD, (e + 1) * HD)
                sp.dma_start(dec_dd[part, :, :, :], s_dd[e::2].unsqueeze(0).to_broadcast([HD, ZT, 2, NB])).then_inc(dec_in, 16)
            with sp.Fori(0, NCH) as c:
                for g in range(GROUPS):
                    b, u = g % 2, c * 2 + g // 2
                    sp.wait_ge(summed[b], u + 1)
                    settle(sp)
                    tok = bass.ds(c * CH, CH)
                    sp.dma_start(xg[b][:, 0:4, :], xbc_t[:, 4 * g:4 * g + 4, tok]).then_inc(group_in[b], 16)
                    sp.dma_start(xg[b][:, 4:6, :], xbc_t[:, ZT + g::GROUPS, tok]).then_inc(group_in[b], 16)
                    sp.dma_start(zg[b], z_t[:, 4 * g:4 * g + 4, tok]).then_inc(group_in[b], 16)
                    sp.dma_start(csb[b], s_cs[g * HG:(g + 1) * HG, tok].unsqueeze(0).to_broadcast([P, HG, CH])).then_inc(group_in[b], 16)
                    for m in SEG[g]:
                        load_w(sp, main_tile(c, m), w_in[:, :, bass.ds(c * P + MAIN[m], P)])
                    if g % 2 == 0:
                        if g == 0:
                            sp.wait_ge(sd_step, c * 10 + 1)
                            settle(sp)
                            sp.dma_start(bcd, s_bc[bass.ds(c, 1)].rearrange("a s b n -> a (s b) n").to_broadcast([P, 2 * NB, P])
                                         .rearrange("p (s b) n -> p s b n", s=2)).then_inc(bcd_in, 16)
                        sp.wait_ge(sd_saved, (c * 2 + g // 2) * 16 + 1)
                        settle(sp)
                        sp.wait_ge(sd_step, (c * 2 + g // 2) * 5 + 1)
                        settle(sp)
                        sp.dma_start(sd, ssm_in[bass.ds((c * 2 + g // 2) * P, P)]).then_inc(sd_in, 16)
            sp.dma_start(O["s_conv_s"][0, :, 0:KS - 2, :], I["state_conv_s"][0, :, 1:KS - 1, :]).then_inc(S["copied_dram"], 16)
            sp.dma_start(O["s_conv_a"][0, :, 0:KA - 2, :], I["state_conv_a"][0, :, 1:KA - 1, :]).then_inc(S["copied_dram"], 16)
            for r in range(3):
                sp.wait_ge(stored[r], 16 * (16 + STAGED[r]) + 1)
            sp.dma_start(qx, s_q[:, SEQ:].rearrange("(t p) b -> p t b", p=P)).then_inc(S["qx_in"], 16)
            def sp_tiles(b, i):
                for r in range(SLOT2):
                    load_w(sp, out_tile(b, i, r), out_w(b)[:, :, bass.ds((i * 2 + r) * P, P)])
                    if b < 4:
                        n = i * 2 + (b * KT + r)
                        for p in range(NP):
                            sp.wait_ge(evac[p], (n + ((TM if p == NP - 1 else FM) + 71)) + 1)
                            settle(sp)
                        if b:
                            sp.wait_ge(merge_done[r], i + (b - 1) * 4 + 1)
                            settle(sp)
                        sp.dma_start(stage[r][:], s_g[bass.ds((i * 2 + r) * P + GATE[b] * D, P), :]).then_inc(gate_in[r], 16)
            def load_att(i, half):
                u = i + half * 4
                sp.wait_ge(S["att_saved"], u * 16 + 1)
                settle(sp)
                tok = slice(half * 512, half * 512 + 512)
                head = lambda d: d[bass.ds(i * MD, MD), :].rearrange("(t p) n -> p t n", p=P)
                sp.dma_start(aq, head(s_q)[:, :, tok]).then_inc(S["att_in"], 16)
                sp.dma_start(ak, head(s_kt)).then_inc(S["att_in"], 16)
                sp.dma_start(amz, head(s_mz)[:, :, tok]).then_inc(S["att_in"], 16)
                sp.dma_start(avv, O["p_mem_v"][0, 0].rearrange("(a m) h d -> m a (h d)", m=P)[:, :, bass.ds(i * MD, MD)]).then_inc(S["att_in"], 16)
            sp.wait_ge(S["h_copied"], 4)
            sp.dma_start(O["p_ssm"][0, 0].rearrange("h p n -> (h p) n").rearrange("(t q) n -> q t n", q=P), pso).then_inc(S["h_saved"], 16)
            sp.wait_ge(S["dec_step"], 5)
            sp.dma_start(s_y[:, SEQ:].rearrange("(t p) b -> p t b", p=P), dec_y).then_inc(S["dec_saved"], 16)
            sp.wait_ge(S["qx_copied"], 1)
            sp.dma_start(s_qd, qrow[0:64, :]).then_inc(S["q_saved"], 16)
            sp.wait_ge(S["dec_saved"], 16)
            sp.wait_ge(S["q_saved"], 16)
            sp.wait_ge(S["h_saved"], 16)
            with sp.Fori(0, 4) as i:
                sp_tiles(0, i)
                load_att(i, 0)
            with sp.Fori(0, 4) as i:
                sp_tiles(1, i)
                load_att(i, 1)
                for e in range(2):
                    k = i * 2 + e
                    sp.wait_ge(S["sam_read"], k * 8 + 1)
                    settle(sp)
                    sp.wait_ge(S["sam_kept"], k + 1)
                    settle(sp)
                    sp.dma_start(dk, I["cache_mem_k"][0, bass.ds(k, 1)].rearrange("c (a m) h d -> m (c a) (h d)", m=P)).then_inc(S["sam_in"], 16)
                    sp.dma_start(dq.rearrange("p (t n) -> p t n", n=P),
                                 s_qd.rearrange("(t b) n -> b t n", b=NB)[bass.ds(k, 1)].to_broadcast([P, KT, P])).then_inc(S["sam_in"], 16)
            sp.wait_ge(S["tail_copied"], 8)
            for src, dst in ((trow_s[0:KS - 1, :], O["p_conv_s"][0, 0]), (trow_s[KS - 1:TAIL_S, :], O["s_conv_s"][0, :, KS - 2, :]),
                             (trow_a[0:KA - 1, :], O["p_conv_a"][0, 0]), (trow_a[KA - 1:TAIL_A, :], O["s_conv_a"][0, :, KA - 2, :])):
                sp.dma_start(dst, src).then_inc(S["tail_saved"], 16)
            sp.dma_start(mzd, s_mz[:, SEQ:].rearrange("(t p) b -> p t b", p=P)).then_inc(S["mzd_in"], 16)
            sp.wait_ge(S["sam_read"], 65)
            with sp.Fori(0, 4) as i:
                sp_tiles(2, i)
                for e in range(2):
                    k = i * 2 + e
                    sp.wait_ge(S["v_used"], k + 1)
                    settle(sp)
                    sp.dma_start(dk, I["cache_mem_v"][0, bass.ds(k, 1)].rearrange("c (a m) h d -> m (c a) (h d)", m=P)).then_inc(S["v_in"], 16)
            sp.wait_ge(S["od_ready"], 1)
            sp.dma_start(s_o[:, SEQ:].rearrange("(t p) b -> p t b", p=P), od).then_inc(S["od_saved"], 16)
            for b in (3, 4):
                with sp.Fori(0, 4) as i:
                    sp_tiles(b, i)
            sp.wait_ge(S["act_split"], 12)
            sp.wait_ge(S["tail_saved"], 64)
            sp.dma_start(fw, I["final_norm_w"].rearrange("(a n) -> a n", a=1).to_broadcast([P, D])).then_inc(S["fw_in"], 16)
            def final_rows(a):
                if a < NCH:
                    return P, I["x_prompt"][0, a * P:(a + 1) * P, :], O["y_prompt"][0, a * P:(a + 1) * P, :]
                return NB, I["x_sample"][:, 0, :], O["y_sample"][:, 0, :]
            for a in range(NCH + 1 + 2):
                if a < NCH + 1:
                    if a >= 2:
                        sp.wait_ge(S["row_sum"], 2 * (a - 1))
                    sp.dma_start(xf[a % 2][0:final_rows(a)[0], :], final_rows(a)[1]).then_inc(row_in[a % 2], 16)
                if a >= 2:
                    n, _, dst = final_rows(a - 2)
                    sp.wait_ge(S["row_out"], a - 1)
                    sp.dma_start(dst, rr[a % 2][0:n, :]).then_inc(row_saved[a % 2], 16)
            sp.wait_ge(row_saved[0], 16 * 5)
            sp.wait_ge(row_saved[1], 16 * 4)
            sp.wait_ge(S["copied_dram"], 32)
            sp.wait_ge(S["od_saved"], 16)

        @block.gpsimd
        def _(pool):
            for s in OPENED:
                pool.sem_inc(s, 1)
            pool.memset(ident[:], 0.0).then_inc(const_ready, 1)
            pool.memset(tri[:], 1.0).then_inc(const_ready, 1)
            pool.memset(ones[:], 1.0).then_inc(const_ready, 1)
            pool.memset(epsc[:], EPS).then_inc(const_ready, 1)
            pool.memset(negh[:], -0.5).then_inc(const_ready, 1)
            pool.memset(xp[:, 0:KS - 1], 0.0).then_inc(pads_ready, 1)
            pool.wait_ge(const_ready, 5)
            pool.affine_select(out=ident[:], in_=ident[:], compare_op=ALU.not_equal, fill=1.0, base=0,
                               pattern=[[-1, P]], channel_multiplier=1).then_inc(const_ready, 1)
            pool.affine_select(out=tri[:], in_=tri[:], compare_op=ALU.is_ge, fill=0.0, base=0,
                               pattern=[[1, P]], channel_multiplier=-1).then_inc(const_ready, 1)
            with pool.Fori(0, XT // 3) as i:
                for r in range(3):
                    split_w(pool, xbc_tile(i, r))
            with pool.Fori(0, 5) as i:
                for r in range(3):
                    split_w(pool, z_tile(i, r))
            for t in (last_z, dt_tile, kv0):
                split_w(pool, t)
            with pool.Fori(0, 5) as i:
                for r in range(3):
                    split_w(pool, kv_tile(i, r))
            with pool.Fori(0, NCH) as c:
                for m in range(9):
                    split_w(pool, main_tile(c, m))
            for b in range(PASSES):
                with pool.Fori(0, 4) as i:
                    for r in range(SLOT2):
                        split_w(pool, out_tile(b, i, r))

        @block.scalar
        def _(act):
            act.wait_ge(const_ready, 7)
            for a in range(NROW):
                n = row_tile(a)[0]
                act.wait_ge(rows_in[a % 2], 16 * (a // 2 + 1))
                if a:
                    act.wait_ge(square_done, a)
                act.activation(junk[0:n, :], xr[a % 2][0:n, :], ACT.Square, accum_out=ssq[0:n, a:a + 1]).then_inc(square_done, 1)
                act.wait_ge(square_done, a + 1)
                act.activation(root[0:n, a:a + 1], ssq[0:n, a:a + 1], ACT.Sqrt, scale=1.0 / D, bias=epsc[0:n, :]).then_inc(root_done, 1)
            act.wait_ge(pads_ready, 1)
            with act.Fori(0, XT // 3) as i:
                for r in range(3):
                    t = xbc_tile(i, r)
                    j = i * 3 + r
                    act.wait_ge(conv[KS - 1], j * 2 + 1)
                    act.wait_ge(tails_kept, j + 1)
                    read_out(act, t, xp[:, KS - 1:], ACT.Copy)
                    act.wait_ge(conv[KS - 1], (j + 1) * 2 + 1)
                    act.wait_ge(stored[r], i * 16 + 1)
                    act.activation(stage[r][:], cv[:, :], ACT.Silu).then_inc(silu_done, 1)
                    act.wait_ge(silu_done, j + 1 + 1)
                    act.dma_start(rows(s_xbc, j), stage[r][:]).then_inc(stored[r], 16)
            with act.Fori(0, 5) as i:
                for r in range(3):
                    to_dram(act, z_tile(i, r), i + XT // 3, rows(s_z, i * 3 + r), ACT.Silu)
            to_dram(act, last_z, XT // 3 + 5, s_z[15 * P:, :], ACT.Silu)
            act.wait_ge(u_split, 2 * NROW)
            act.wait_ge(par_turned, 1)
            def read_kv(t, n):
                piece_ready(act, t, NP - 1)
                act.activation(kv_t[:, n, :] if type(n) is int else kv_t[:, bass.ds(n, 1), :].rearrange("p a m -> p (a m)"),
                               acc[:, NP - 1, 0:NM], ACT.Copy).then_inc(evac[NP - 1], 1)
            read_kv(kv0, 0)
            evacuated(act, dt_tile)
            act.activation(absv[0:HEADS, :], dtv[0:HEADS, :], ACT.Abs).then_inc(dt_abs, 1)
            act.wait_ge(dt_abs, 1)
            act.activation(expo[0:HEADS, :], absv[0:HEADS, :], ACT.Exp, scale=-1.0).then_inc(dt_exp, 1)
            act.activation(aneg[0:HEADS, :], alog[0:HEADS, :], ACT.Exp).then_inc(a_exp, 1)
            with act.Fori(0, 5) as i:
                for r in range(3):
                    read_kv(kv_tile(i, r), i * 3 + r + 1)
            act.wait_ge(dt_ready, 1)
            act.activation(dd[0:HEADS, 0, :], da[0:HEADS, SEQ:], ACT.Exp).then_inc(dd_ready, 1)
            act.wait_ge(kv_saved, 48)
            act.wait_ge(cs_saved, 32)
            act.wait_ge(pre_turned, 1)
            def act_tile(c, m):
                t = main_tile(c, m)
                if m == 0:
                    act.wait_ge(tails_a_kept, c + 1)
                    read_out(act, t, cc, ACT.Copy)
                elif m == 2:
                    act.wait_ge(a_ready, c + 1)
                    read_out(act, t, zc, ACT.Silu)
                elif m == 3:
                    act.wait_ge(a_ready, c + 1 + 1)
                    act.dma_start(rows(s_a, c), stage[0][:]).then_inc(stored[0], 16)
                elif m == 4:
                    to_dram(act, t, staged(c, m), rows(s_q, c), ACT.Copy, MD ** -0.5)
                elif m == 5:
                    to_dram(act, t, staged(c, m), rows(s_mz, c), ACT.Silu)
                elif m >= 6:
                    to_dram(act, t, staged(c, m), s_g[bass.ds(c * P + (m - 6) * D, P), :], ACT.Sigmoid)
            with act.Fori(0, NCH) as c:
                for g in range(GROUPS):
                    n = c * 4 + g
                    act.wait_ge(x_turned, n + 1)
                    act.wait_ge(gy_ready, n + 1)
                    act.activation(xt, pm[0][:], ACT.Copy).then_inc(x_copied, 1)
                    act.wait_ge(args_ready, (n + 1) * 3)
                    act.activation(sm, sa, ACT.Exp).then_inc(sm_ready, 1)
                    act.wait_ge(seg_ready, (n + 1) * HG)
                    act.activation(seg, seg, ACT.Exp).then_inc(e_ready, 1)
                    act_tile(c, SEG[g][0])
                    act.wait_ge(gy_ready, n + 1 + 1)
                    act.wait_ge(y_turned, n + 1)
                    act.activation(gyn, gy, ACT.Square, accum_out=ss2).then_inc(sq2_done, 1)
                    act.wait_ge(sq2_done, n + 1)
                    act.activation(rt2, ss2, ACT.Sqrt, scale=1.0 / 512, bias=epsc[:]).then_inc(rt2_done, 1)
                    act.wait_ge(rs2_step, (n + 1) * 5)
                    act.activation(gyn, gy, ACT.Copy, scale=rs2).then_inc(gyn_ready, 1)
                    for m in SEG[g][1:]:
                        act_tile(c, m)
                    if g % 2:
                        k = c * 2 + g // 2
                        act.wait_ge(sd_step, k * 5 + 3 + 1)
                        act.dma_start(ssm_out[bass.ds(k * P, P)], sd).then_inc(sd_saved, 16)
                    act.wait_ge(y_turned, n + 1 + 1)
                    act.wait_ge(y_stored, n * 16 + 1)
                    for k in range(4):
                        act.activation(yT[:, k, :], pm[2][:, k * P:(k + 1) * P], ACT.Copy,
                                       scale=par[:, C_SN + 4 * g + k:C_SN + 4 * g + k + 1]).then_inc(y_out, 1)
                    act.wait_ge(y_out, (n + 1) * 4 + 1)
                    act.dma_start(s_y.rearrange("(t p) n -> p t n", p=P)[:, 4 * g:4 * g + 4, bass.ds(c * CH, CH)], yT).then_inc(y_stored, 16)
            act.wait_ge(y_stored, 16 * 32 + 1)
            act.wait_ge(sd_saved, 16 * 16 + 1)
            act.wait_ge(stored[0], 16 * (16 + STAGED[0]) + 1)
            act.wait_ge(stored[1], 16 * (16 + STAGED[1]) + 1)
            act.wait_ge(stored[2], 16 * (16 + STAGED[2]) + 1)
            act.wait_ge(gy_ready, 33)
            act.wait_ge(a_ready, NCH + 1)
            act.wait_ge(S["dec_sq_done"], 1)
            act.wait_ge(sd_step, 81)
            def load_acts(x):
                act.dma_start(ra[x % 2], ACTS[x // NP][:, :, (x % NP) * PC:(x % NP + 1) * PC]).then_inc(act_in[x % 2], 16)
            def high_parts(b):
                for p in range(NP):
                    x = b * NP + p
                    if b < 4:
                        act.wait_ge(act_in[x % 2], 16 * (x // 2 + 1))
                    elif p == 0:
                        act.wait_ge(merge_done[0], 3 * 4 + 1)
                        act.wait_ge(merge_done[1], 3 * 4 + 1)
                    last_piece(act, b, p)
                    cols = slice(p * PC, (p + 1) * PC)
                    act.activation(uhi[:, :, cols], ra[x % 2] if b < 4 else merged[:, :, cols], ACT.Copy).then_inc(S["act_high"], 1)
                    if x + 2 < 12:
                        act.wait_ge(S["act_split"], x + 1)
                        if x + 2 == 3:
                            act.wait_ge(S["dec_saved"], 16)
                        if x + 2 == 9:
                            act.wait_ge(S["att_saved"], 16 * 8 + 1)
                        if x + 2 == 11:
                            act.wait_ge(S["od_saved"], 16)
                        load_acts(x + 2)
            load_acts(0)
            load_acts(1)
            for n in range(4):
                act.wait_ge(S["h_final"], n + 1)
                act.activation(pso[:, 4 * n:4 * n + 4, :], pm[n][:, :].rearrange("p (a b) -> p a b", b=P), ACT.Copy).then_inc(S["h_copied"], 1)
            act.wait_ge(S["dec_step"], 3)
            act.activation(dec_rs, dec_ms, ACT.Sqrt).then_inc(S["dec_root"], 1)
            high_parts(0)
            def attend(i, half):
                u = i + half * 4
                act.wait_ge(S["att_step"], u * 5 + 3)
                act.wait_ge(S["p_turned"], u * 2 + 1)
                for k in range(4):
                    act.activation(pt[:, k, :], pm[k // 2][:, (k % 2) * NM:(k % 2 + 1) * NM], ACT.Exp, bias=anx[:, k:k + 1],
                                   accum_out=asum[:, k:k + 1]).then_inc(S["att_exp"], 1)
                for m in range(2):
                    act.wait_ge(S["p_turned"], u * 2 + m + 1 + 1)
                    act.wait_ge(S["pv_done"], u + 1)
                    act.activation(ptT[:, m, :], pm[2 + m][:], ACT.Copy).then_inc(S["p_copied"], 1)
            def save_att(i, half):
                u = i + half * 4
                act.wait_ge(S["att_ready"], (u + 1) * 2 + 1)
                act.dma_start(s_o[bass.ds(i * MD, MD), half * 512:half * 512 + 512].rearrange("(t p) n -> p t n", p=P), amz).then_inc(S["att_saved"], 16)
            for half in range(2):
                if half:
                    high_parts(1)
                with act.Fori(0, 4) as i:
                    attend(i, half)
                    save_att(i, half)
            act.wait_ge(S["sam_step"], 2)
            act.activation(dp[0:32, :, :], pm[0][0:32, 0:NM].rearrange("p (a b) -> p a b", b=P), ACT.Exp, bias=dnx[0:32, :],
                           accum_out=dsum[0:32, :]).then_inc(S["sam_exp"], 1)
            act.wait_ge(S["att_saved"], 16 * 8 + 1)
            for src, dst, n, q, x in TAILS:
                act.wait_ge(S["tail_turned"], x + 1)
                act.activation(dst[0:n, q * 512:(q + 1) * 512], pm[2 + x % 3][0:n, :], ACT.Copy).then_inc(S["tail_copied"], 1)
            high_parts(2)
            high_parts(3)
            high_parts(4)
            with act.Fori(0, 4) as i:
                for r in range(SLOT2):
                    t = out_tile(4, i, r)
                    for p in range(NP):
                        piece_ready(act, t, p)
                        out = merged[:, bass.ds(i * 2 + r, 1), p * PC:(p + 1) * PC].rearrange("p a n -> p (a n)")
                        act.wait_ge(S["act_split"], 15)
                        act.activation(out, acc[:, p, 0:PC], ACT.Copy).then_inc(evac[p], 1)
            for a in range(NCH + 1):
                n = P if a < NCH else NB
                act.wait_ge(S["row_sum"], 2 * (a + 1))
                if a:
                    act.wait_ge(S["row_sq"], a)
                act.activation(fjunk[0:n, :], rr[a % 2][0:n, :], ACT.Square, accum_out=fss[0:n, a:a + 1]).then_inc(S["row_sq"], 1)
                act.wait_ge(S["row_sq"], a + 1)
                act.activation(frt[0:n, a:a + 1], fss[0:n, a:a + 1], ACT.Sqrt, scale=1.0 / D, bias=epsc[0:n, :]).then_inc(S["row_root"], 1)

        @block.vector
        def _(dve):
            dve.wait_ge(small_in, 80)
            def norm_rows(a):
                n = row_tile(a)[0]
                b = a % 2
                dve.wait_ge(root_done, a + 1)
                dve.reciprocal(rs[0:n, a:a + 1], root[0:n, a:a + 1]).then_inc(rs_done, 1)
                dve.wait_ge(rs_done, a + 1)
                if a >= 2:
                    dve.wait_ge(turned, 2 * (a - 1))
                w = nwb if a <= SEQ // P else mwb
                dve.scalar_tensor_tensor(xn[b][0:n, :], xr[b][0:n, :], rs[0:n, a:a + 1], w[0:n, :],
                                         ALU.mult, ALU.mult).then_inc(normed[b], 1)
            def split_rows(a):
                n, _, c0 = row_tile(a)
                hi, lo = (uhi, ulo) if a <= SEQ // P else (mhi, mlo)
                for h in range(2):
                    dve.wait_ge(turned, 2 * a + h + 1)
                    src = pm[2 * (a % 2) + h][:, :].rearrange("p (k c) -> p k c", c=P)[:, :, 0:n]
                    dve.tensor_copy(hi[:, 4 * h:4 * h + 4, c0:c0 + n], src).then_inc(u_high, 1)
                    dve.wait_ge(u_high, 2 * a + h + 1)
                    dve.tensor_tensor(lo[:, 4 * h:4 * h + 4, c0:c0 + n], src,
                                      hi[:, 4 * h:4 * h + 4, c0:c0 + n].bitcast(F32), ALU.subtract).then_inc(u_split, 1)
            for a in range(NROW + 1):
                if a < NROW:
                    norm_rows(a)
                if a:
                    split_rows(a - 1)
            dve.wait_ge(par_turned, 1)
            dve.tensor_copy(par[:, 0:P], pm[4][:, 0:P]).then_inc(par_copied, 1)
            dve.tensor_copy(par[:, P:NPAR], pm[4][:, P:NPAR]).then_inc(par_copied, 1)
            for h in range(2):
                dve.tensor_copy(hist_s[:, 12 * h:12 * h + 12, :, :],
                                acc[:, h, 0:288].rearrange("p (t b k) -> p t b k", b=NB, k=KS - 1)).then_inc(par_copied, 1)
            dve.tensor_copy(hist_a[:, :, :, :],
                            acc[:, 2, 0:128].rearrange("p (t b k) -> p t b k", b=NB, k=KA - 1)).then_inc(par_copied, 1)
            dve.wait_ge(par_copied, 5)
            def col(c, j=None):
                return par[:, c:c + 1] if j is None else par[:, bass.ds(j + c, 1)]
            with dve.Fori(0, XT // 3) as i:
                for r in range(3):
                    t = xbc_tile(i, r)
                    j = i * 3 + r
                    evacuated(dve, t)
                    hist = hist_s[:, bass.ds(j, 1), :, :].rearrange("p a b k -> p (a b) k")
                    for k in range(KS):
                        now = xp[:, SEQ + KS - 1:] if k == KS - 1 else hist[:, :, k]
                        if k == 0:
                            dve.wait_ge(silu_done, j + 1)
                            dve.tensor_scalar(cv[:, 0:SEQ], xp[:, 0:SEQ], col(C_SW, j), col(C_SB, j), ALU.mult, ALU.add).then_inc(conv[0], 1)
                            dve.tensor_scalar(cv[:, SEQ:], now, col(C_SW, j), col(C_SB, j), ALU.mult, ALU.add).then_inc(conv[0], 1)
                            continue
                        w = col(C_SW + k * XT, j)
                        dve.wait_ge(conv[k - 1], (j + 1) * 2 + 1)
                        dve.scalar_tensor_tensor(cv[:, 0:SEQ], xp[:, k:k + SEQ], w, cv[:, 0:SEQ], ALU.mult, ALU.add).then_inc(conv[k], 1)
                        dve.scalar_tensor_tensor(cv[:, SEQ:], now, w, cv[:, SEQ:], ALU.mult, ALU.add).then_inc(conv[k], 1)
                    dve.tensor_copy(tail_s[:, bass.ds(j, 1), :].rearrange("p a b -> p (a b)"), xp[:, SEQ:]).then_inc(tails_kept, 1)
            dve.wait_ge(u_split, 2 * NROW)
            dve.wait_ge(par_turned, 1)
            H = slice(0, HEADS)
            for p in range(NP):
                piece_ready(dve, dt_tile, p)
                dve.tensor_scalar(dtv[H, p * PC:(p + 1) * PC], acc[H, p, 0:PC], dtb[H, :], None, ALU.add).then_inc(evac[p], 1)
            evacuated(dve, dt_tile)
            steps = [0]
            def step(ins):
                steps[0] += 1
                ins.then_inc(dt_step, 1)
                dve.wait_ge(dt_step, steps[0])
            dve.wait_ge(dt_exp, 1)
            step(dve.tensor_scalar(zz[H, :], expo[H, :], 2.0, None, ALU.add))
            step(dve.reciprocal(zz[H, :], zz[H, :]))
            step(dve.tensor_tensor(zz[H, :], zz[H, :], expo[H, :], ALU.mult))
            step(dve.tensor_tensor(expo[H, :], zz[H, :], zz[H, :], ALU.mult))
            step(dve.tensor_scalar(csv[H, :], expo[H, :], 1.0 / (2 * LOG1P_TERMS + 1), None, ALU.mult))
            for n in range(LOG1P_TERMS - 1, 0, -1):
                step(dve.scalar_tensor_tensor(csv[H, :], csv[H, :], 1.0 / (2 * n + 1), expo[H, :], ALU.add, ALU.mult))
            step(dve.scalar_tensor_tensor(csv[H, :], csv[H, :], 1.0, zz[H, :], ALU.add, ALU.mult))
            step(dve.tensor_scalar(dtv[H, :], dtv[H, :], 0.0, None, ALU.max))
            step(dve.scalar_tensor_tensor(dtv[H, :], csv[H, :], 2.0, dtv[H, :], ALU.mult, ALU.add))
            dve.wait_ge(a_exp, 1)
            step(dve.tensor_scalar(aneg[H, :], aneg[H, :], -1.0, None, ALU.mult))
            dve.tensor_scalar(da[H, :], dtv[H, :], aneg[H, :], None, ALU.mult).then_inc(dt_ready, 1)
            step(dve.memset(resets[H, :], 1.0))
            step(dve.memset(resets[H, 0:SEQ:CH], 0.0))
            dve.wait_ge(dt_ready, 1)
            dve.tensor_tensor_scan(csv[H, 0:SEQ], resets[H, 0:SEQ], da[H, 0:SEQ], 0.0, ALU.mult, ALU.add).then_inc(cs_ready, 1)
            dve.tensor_copy(dd[H, 1, :], dtv[H, SEQ:]).then_inc(dd_ready, 1)
            dve.wait_ge(pre_turned, 1)
            dve.tensor_copy(dt_tok[:], pm[0][:, 0:NCH * HEADS]).then_inc(pre_copied, 1)
            dve.tensor_copy(cs_tok[:], pm[0][:, NCH * HEADS:2 * NCH * HEADS]).then_inc(pre_copied, 1)
            dve.wait_ge(pre_turned, 2)
            dve.tensor_copy(bcr[0:64, :], pm[0][0:64, 0:P]).then_inc(pre_copied, 1)
            for n in range(8):
                s, m, h = n // 4, n // 2 % 2, n % 2
                dve.wait_ge(pre_turned, n + 3)
                dve.tensor_copy(kv_tok[:, s, m, h * 512:(h + 1) * 512], pm[1 + n % 4][:]).then_inc(pre_copied, 1)
            dve.wait_ge(kv_saved, 48)
            dve.wait_ge(cs_saved, 32)
            dve.wait_ge(pre_copied, 2)
            dve.memset(hT, 0.0).then_inc(h_added, 1)
            dve.memset(hb[:, 0:KA - 1], 0.0).then_inc(hb_pad, 1)
            dve.wait_ge(h_added, 1)
            dve.wait_ge(hb_pad, 1)
            dve.wait_ge(dec_in, 16 * 4)
            for e in range(2):
                part = slice(e * HD, (e + 1) * HD)
                dve.tensor_copy(dec_skip[part, :], dskip[part, e::2]).then_inc(dec_ready, 1)
            dve.tensor_tensor(dec_xdt, dec_x, dec_dd[:, :, 1, :], ALU.mult).then_inc(dec_ready, 1)
            dve.wait_ge(dec_ready, 3)
            def dve_tile(c, m):
                t = main_tile(c, m)
                if m == 1:
                    evacuated(dve, main_tile(c, 0))
                    for p in range(NP):
                        piece_ready(dve, t, p)
                        lo, hi = p * PC, (p + 1) * PC
                        dve.wait_ge(a_conv, c * 2 * KA + 1)
                        dve.wait_ge(tails_a_kept, c + 1)
                        dve.tensor_tensor(hb[:, KA - 1 + lo:KA - 1 + hi], acc[:, p, 0:PC], cc[:, lo:hi], ALU.mult).then_inc(evac[p], 1)
                    evacuated(dve, t)
                    dve.tensor_copy(tail_a[:, bass.ds(c, 1), :].rearrange("p a b -> p (a b)"), hb[:, SEQ:]).then_inc(tails_a_kept, 1)
                    hist = hist_a[:, bass.ds(c, 1), :, :].rearrange("p a b k -> p (a b) k")
                    dve.wait_ge(a_ready, c + 1)
                    for k in range(KA):
                        now = hb[:, SEQ + KA - 1:] if k == KA - 1 else hist[:, :, k]
                        w = col(C_AW + k * KT, c)
                        if k == 0:
                            dve.tensor_scalar(av[:, 0:SEQ], hb[:, 0:SEQ], w, None, ALU.mult).then_inc(a_conv, 1)
                            dve.tensor_scalar(av[:, SEQ:], now, w, None, ALU.mult).then_inc(a_conv, 1)
                            continue
                        dve.wait_ge(a_conv, (c * KA + k) * 2 + 1)
                        dve.scalar_tensor_tensor(av[:, 0:SEQ], hb[:, k:k + SEQ], w, av[:, 0:SEQ], ALU.mult, ALU.add).then_inc(a_conv, 1)
                        dve.scalar_tensor_tensor(av[:, SEQ:], now, w, av[:, SEQ:], ALU.mult, ALU.add).then_inc(a_conv, 1)
                elif m == 3:
                    evacuated(dve, main_tile(c, 2))
                    for p in range(NP):
                        piece_ready(dve, t, p)
                        part = zc[:, p * PC:(p + 1) * PC]
                        dve.tensor_tensor(part, part, acc[:, p, 0:PC], ALU.mult).then_inc(evac[p], 1)
                    evacuated(dve, t)
                    dve.wait_ge(a_conv, (c + 1) * 2 * KA + 1)
                    dve.wait_ge(stored[0], staged(c, m) * 16 + 1)
                    dve.tensor_tensor(stage[0][:], zc, av, ALU.mult).then_inc(a_ready, 1)
            with dve.Fori(0, NCH) as c:
                for g in range(GROUPS):
                    n, b, u = c * 4 + g, g % 2, c * 2 + g // 2
                    dve.wait_ge(group_in[b], (u + 1) * 64)
                    last = csb[b][:, :, CH - 1]
                    cs = cs_tok[:, bass.ds(c * HEADS + g * HG, HG)]
                    dve.wait_ge(sm_ready, n + 1)
                    dve.tensor_tensor(sa[:, 0, :], last, cs, ALU.subtract).then_inc(args_ready, 1)
                    dve.tensor_copy(sa[:, 1, :], cs).then_inc(args_ready, 1)
                    dve.tensor_copy(sa[:, 2, :], last).then_inc(args_ready, 1)
                    dve.wait_ge(m_ready, n + 1)
                    for h in range(HG):
                        dve.tensor_scalar(seg[:, h, :], csb[b][:, h, :], cs_tok[:, bass.ds(c * HEADS + g * HG + h, 1)], 0.0,
                                          ALU.subtract, ALU.min).then_inc(seg_ready, 1)
                    dve.wait_ge(b_ready, n + 1)
                    group_before(dve, c, g)
                    dve.tensor_copy(bt, pm[1][:, 0:P]).then_inc(bt_ready, 1)
                    dve.tensor_tensor(scm, pm[1][:, P:2 * P], tri[:], ALU.mult).then_inc(sc_ready, 1)
                    dve.wait_ge(x_copied, n + 1)
                    dve.tensor_tensor(heads(xdt), heads(xt), bcast(dt_tok[:, bass.ds(c * HEADS + g * HG, HG)], HD), ALU.mult).then_inc(xdt_ready, 1)
                    dve.wait_ge(sm_ready, n + 1 + 1)
                    dve.wait_ge(xdt_ready, n + 1)
                    dve.tensor_tensor(heads(xdd), heads(xdt), bcast(sm[:, 0, :], HD), ALU.mult).then_inc(xdd_ready, 1)
                    dve.wait_ge(e_ready, n + 1)
                    dve.wait_ge(sc_ready, n + 1)
                    dve.tensor_tensor(mm_, seg, scm.unsqueeze(1).to_broadcast([P, HG, CH]), ALU.mult).then_inc(m_ready, 1)
                    dve_tile(c, SEG[g][0])
                    dve.wait_ge(gyn_ready, n + 1)
                    dve.tensor_tensor(heads(gy), heads(xt), bcast(dskip[:, g * HG:(g + 1) * HG], HD), ALU.mult).then_inc(y_step, 1)
                    dve.wait_ge(summed[b], u + 1 + 1)
                    dve.tensor_tensor(heads(yv), heads(pm[3][:]), bcast(sm[:, 1, :], HD), ALU.mult).then_inc(y_step, 1)
                    dve.tensor_tensor(heads(hT[:, g, :]), heads(hT[:, g, :]), bcast(sm[:, 2, :], HD), ALU.mult).then_inc(h_scaled, 1)
                    dve.wait_ge(y_step, n * 4 + 2)
                    dve.tensor_tensor(yv, yv, pm[4][:], ALU.add).then_inc(y_step, 1)
                    dve.wait_ge(h_scaled, n + 1)
                    dve.tensor_tensor(hT[:, g, :], hT[:, g, :], pm[0][:], ALU.add).then_inc(h_added, 1)
                    dve.wait_ge(y_step, n * 4 + 3)
                    dve.tensor_tensor(yv, yv, gy, ALU.add).then_inc(y_step, 1)
                    dve.wait_ge(y_step, n * 4 + 4)
                    dve.wait_ge(z_turned, n + 1)
                    dve.tensor_tensor(gy, yv, pm[2][:], ALU.mult).then_inc(gy_ready, 1)
                    dve.wait_ge(rt2_done, n + 1)
                    dve.wait_ge(gyn_ready, n + 1)
                    dve.tensor_scalar(var2, ss2, 1.0 / 512, EPS, ALU.mult, ALU.add).then_inc(rs2_step, 1)
                    dve.reciprocal(rs2, rt2).then_inc(rs2_step, 1)
                    dve.wait_ge(rs2_step, n * 5 + 2)
                    dve.scalar_tensor_tensor(nw2, rs2, var2, rs2, ALU.mult, ALU.mult).then_inc(rs2_step, 1)
                    dve.wait_ge(rs2_step, n * 5 + 3)
                    dve.tensor_scalar(nw2, nw2, -0.5, 1.5, ALU.mult, ALU.add).then_inc(rs2_step, 1)
                    dve.wait_ge(rs2_step, n * 5 + 4)
                    dve.tensor_tensor(rs2, rs2, nw2, ALU.mult).then_inc(rs2_step, 1)
                    for m in SEG[g][1:]:
                        dve_tile(c, m)
                    if g % 2 == 0:
                        k = c * 2 + g // 2
                        if g == 0:
                            dve.wait_ge(bcd_in, (c + 1) * 16)
                        dve.wait_ge(sd_in, (k + 1) * 16)
                        dve.wait_ge(sd_step, k * 5 + 1)
                        tile = lambda v: v[:, bass.ds(k, 1)]
                        decay = dec_dd[:, bass.ds(k, 1), 0, :].rearrange("p a b -> p (a b)")
                        flat = lambda v: v[:, bass.ds(k, 1), :].rearrange("p a b -> p (a b)")
                        dve.tensor_tensor(sd2, bcd[:, 0, :, :], bcast(flat(dec_xdt), P), ALU.mult).then_inc(sd_step, 1)
                        dve.tensor_tensor(sd, sd, bcast(decay, P), ALU.mult).then_inc(sd_step, 1)
                        dve.wait_ge(sd_step, k * 5 + 2 + 1)
                        dve.tensor_tensor(sd, sd, sd2, ALU.add).then_inc(sd_step, 1)
                        dve.wait_ge(sd_step, k * 5 + 3 + 1)
                        dve.tensor_tensor(sd2, sd, bcd[:, 1, :, :], ALU.mult).then_inc(sd_step, 1)
                        dve.wait_ge(sd_step, k * 5 + 4 + 1)
                        dve.tensor_reduce(flat(dec_y), sd2, AX.X, ALU.add).then_inc(sd_step, 1)
            for e_ in (dec_in,):
                dve.wait_ge(e_, 64)
            dve.tensor_tensor(dec_sq, dec_x, bcast(dec_skip, NB), ALU.mult).then_inc(dec_ready, 1)
            dve.wait_ge(dec_ready, 4)
            dve.wait_ge(sd_step, 81)
            dve.tensor_tensor(dec_y, dec_y, dec_sq, ALU.add).then_inc(dec_ready, 1)
            dve.wait_ge(dec_ready, 5)
            dve.tensor_tensor(dec_y, dec_y, dec_z, ALU.mult).then_inc(dec_ready, 1)
            dve.wait_ge(dec_ready, 6)
            dve.tensor_tensor(dec_sq, dec_y, dec_y, ALU.mult).then_inc(S["dec_sq_done"], 1)
            dve.wait_ge(S["dec_summed"], 1)
            dve.tensor_reduce(dec_ms, pm[4][:, 0:P].rearrange("p (g t b) -> p g b t", g=GROUPS, b=NB), AX.X, ALU.add).then_inc(S["dec_step"], 1)
            dve.wait_ge(S["dec_step"], 1)
            dve.tensor_scalar(dec_ms, dec_ms, 1.0 / 512, EPS, ALU.mult, ALU.add).then_inc(S["dec_step"], 1)
            dve.wait_ge(S["dec_step"], 2)
            dve.tensor_scalar(dec_nw, dec_ms, -0.5, None, ALU.mult).then_inc(S["dec_step"], 1)
            dve.wait_ge(S["dec_root"], 1)
            dve.wait_ge(S["dec_step"], 3)
            dve.reciprocal(dec_rs, dec_rs).then_inc(S["dec_step"], 1)
            dve.wait_ge(S["dec_step"], 4)
            step(dve.tensor_tensor(dec_nw, dec_nw, dec_rs, ALU.mult))
            step(dve.tensor_tensor(dec_nw, dec_nw, dec_rs, ALU.mult))
            step(dve.tensor_scalar(dec_nw, dec_nw, 1.5, None, ALU.add))
            step(dve.tensor_tensor(dec_rs, dec_rs, dec_nw, ALU.mult))
            for g in range(GROUPS):
                step(dve.tensor_tensor(dec_y[:, 4 * g:4 * g + 4, :], dec_y[:, 4 * g:4 * g + 4, :],
                                       dec_rs[:, g:g + 1, :].to_broadcast([P, 4, NB]), ALU.mult))
            dve.tensor_tensor(dec_y, dec_y, bcast(par[:, C_SN:C_SN + ZT], NB), ALU.mult).then_inc(S["dec_step"], 1)
            dve.wait_ge(S["qx_turned"], 1)
            for r in range(3):
                dve.wait_ge(stored[r], 16 * (16 + STAGED[r]) + 1)
            dve.tensor_copy(qrow[0:64, :], pm[4][0:64, P:2 * P]).then_inc(S["qx_copied"], 1)
            dve.wait_ge(S["dec_saved"], 16)
            dve.wait_ge(S["h_final"], 4)
            dve.wait_ge(y_stored, 16 * 32 + 1)
            def low_parts(b):
                for p in range(NP):
                    x = b * NP + p
                    dve.wait_ge(S["act_high"], x + 1)
                    cols = slice(p * PC, (p + 1) * PC)
                    dve.tensor_tensor(ulo[:, :, cols], ra[x % 2] if b < 4 else merged[:, :, cols],
                                      uhi[:, :, cols].bitcast(F32), ALU.subtract).then_inc(S["act_split"], 1)
            def merge(b, i, r):
                t = out_tile(b, i, r)
                it = bass.ds(i * 2 + r, 1)
                dve.wait_ge(gate_in[r], (i + (b * 4 + 1)) * 16)
                for p in range(NP):
                    piece_ready(dve, t, p)
                    cols = slice(p * PC, (p + 1) * PC)
                    if b == 0:
                        if p == 0:
                            dve.wait_ge(S["h_saved"], 16)
                        out = merged[:, it, cols].rearrange("p a n -> p (a n)")
                    else:
                        out = stage[r][:, cols]
                    dve.tensor_tensor(out, stage[r][:, cols], acc[:, p, 0:PC], ALU.mult).then_inc(evac[p], 1)
                if b:
                    evacuated(dve, t)
                    whole = merged[:, it, :].rearrange("p a n -> p (a n)")
                    dve.tensor_tensor(whole, whole, stage[r][:], ALU.add).then_inc(merge_done[r], 1)
            def softmax(i, half):
                u = i + half * 4
                dve.wait_ge(S["qk_done"], u + 1)
                dve.wait_ge(S["att_exp"], u * 4 + 1)
                for k in range(2):
                    dve.tensor_reduce(amx[:, 2 * k:2 * k + 2], pm[k][:, :].rearrange("p (a b) -> p a b", b=NM), AX.X, ALU.max).then_inc(S["att_step"], 1)
                dve.wait_ge(S["att_step"], u * 5 + 2)
                dve.tensor_scalar(anx, amx, -1.0, None, ALU.mult).then_inc(S["att_step"], 1)
                dve.wait_ge(S["att_exp"], (u + 1) * 4 + 1)
                dve.reciprocal(arec, asum).then_inc(S["att_step"], 1)
                dve.wait_ge(S["att_step"], u * 5 + 4)
                dve.tensor_tensor(pt, pt, bcast(arec, NM), ALU.mult).then_inc(S["att_step"], 1)
            def gate_att(i, half):
                u = i + half * 4
                dve.wait_ge(S["pv_done"], u + 1 + 1)
                for d in range(2):
                    dve.tensor_tensor(amz[:, d, :], amz[:, d, :], pm[4 * (1 - d)][:], ALU.mult).then_inc(S["att_ready"], 1)
            def sample_scores(i):
                for e in range(2):
                    k = i * 2 + e
                    dve.wait_ge(S["sam_in"], (k + 1) * 32)
                    dve.wait_ge(S["sam_kept"], k + 1)
                    for a in range(2):
                        for h in range(MH):
                            ks = dk[:, a, h * MD:(h + 1) * MD]
                            dve.tensor_tensor_reduce(ks, ks, dq[:, h * MD:(h + 1) * MD], 1.0, 0.0, ALU.mult, ALU.add,
                                                     sde[:, a, h:h + 1]).then_inc(S["sam_read"], 1)
                    dve.wait_ge(S["sam_read"], (k + 1) * 8 + 1)
                    dve.tensor_copy(sds[:, :, bass.ds(k, 1), :].rearrange("p a b h -> p a (b h)"), sde).then_inc(S["sam_kept"], 1)
            low_parts(0)
            with dve.Fori(0, 4) as i:
                softmax(i, 0)
                merge(0, i, 0)
                merge(0, i, 1)
                gate_att(i, 0)
            low_parts(1)
            with dve.Fori(0, 4) as i:
                softmax(i, 1)
                merge(1, i, 0)
                merge(1, i, 1)
                gate_att(i, 1)
                sample_scores(i)
            dve.wait_ge(S["sds_turned"], 1)
            dve.tensor_reduce(dmx[0:32, :], pm[0][0:32, 0:NM], AX.X, ALU.max).then_inc(S["sam_step"], 1)
            dve.wait_ge(S["sam_step"], 1)
            dve.tensor_scalar(dnx[0:32, :], dmx[0:32, :], -1.0, None, ALU.mult).then_inc(S["sam_step"], 1)
            dve.wait_ge(S["sam_exp"], 1)
            dve.reciprocal(drec[0:32, :], dsum[0:32, :]).then_inc(S["sam_step"], 1)
            dve.wait_ge(S["sam_step"], 3)
            dve.tensor_scalar(dp[0:32, :, :], dp[0:32, :, :], drec[0:32, :], None, ALU.mult).then_inc(S["sam_step"], 1)
            dve.wait_ge(S["dp_turned"], 1)
            dve.tensor_copy(dpT, pm[1][:, 0:64].rearrange("p (a b) -> p a b", a=2)).then_inc(S["dp_copied"], 1)
            low_parts(2)
            with dve.Fori(0, 4) as i:
                merge(2, i, 0)
                merge(2, i, 1)
            dve.wait_ge(S["v_used"], 9)
            dve.wait_ge(S["mzd_in"], 16)
            dve.tensor_tensor(od, mzd, pm[3][:, 0:64].rearrange("p (b t) -> p t b", t=KT), ALU.mult).then_inc(S["od_ready"], 1)
            low_parts(3)
            with dve.Fori(0, 4) as i:
                merge(3, i, 0)
                merge(3, i, 1)
            low_parts(4)
            dve.wait_ge(S["fw_in"], 16)
            def final_out(a):
                n = P if a < NCH else NB
                q = slice(a, a + 1)
                dve.wait_ge(S["row_root"], a + 1)
                dve.tensor_scalar(fvar[0:n, q], fss[0:n, q], 1.0 / D, EPS, ALU.mult, ALU.add).then_inc(S["row_step"], 1)
                dve.reciprocal(frs[0:n, q], frt[0:n, q]).then_inc(S["row_step"], 1)
                dve.wait_ge(S["row_step"], a * 5 + 2)
                dve.scalar_tensor_tensor(fnw[0:n, q], frs[0:n, q], fvar[0:n, q], frs[0:n, q], ALU.mult, ALU.mult).then_inc(S["row_step"], 1)
                dve.wait_ge(S["row_step"], a * 5 + 3)
                dve.tensor_scalar(fnw[0:n, q], fnw[0:n, q], -0.5, 1.5, ALU.mult, ALU.add).then_inc(S["row_step"], 1)
                dve.wait_ge(S["row_step"], a * 5 + 4)
                dve.tensor_tensor(frs[0:n, q], frs[0:n, q], fnw[0:n, q], ALU.mult).then_inc(S["row_step"], 1)
                dve.wait_ge(S["row_step"], a * 5 + 5)
                v = rr[a % 2][0:n, :]
                dve.scalar_tensor_tensor(v, v, frs[0:n, q], fw[0:n, :], ALU.mult, ALU.mult).then_inc(S["row_out"], 1)
            for a in range(NCH + 2):
                if a < NCH + 1:
                    n = P if a < NCH else NB
                    dve.wait_ge(row_in[a % 2], 16 * (a // 2 + 1))
                    if a >= 2:
                        dve.wait_ge(row_saved[a % 2], 16 * (a // 2))
                    for h in range(2):
                        dve.wait_ge(S["row_turned"], 2 * a + h + 1)
                        half = slice(h * 512, (h + 1) * 512)
                        dve.tensor_tensor(rr[a % 2][0:n, half], xf[a % 2][0:n, half], pm[2 * (a % 2) + h][0:n, :], ALU.add).then_inc(S["row_sum"], 1)
                if a:
                    final_out(a - 1)

        @block.tensor
        def _(pe):
            pe.wait_ge(const_ready, 7)
            pe.wait_ge(par_in, 96)
            pe.transpose(pm[4][:, 0:P], par_rows[:, 0, :], ident[:])
            n1 = NPAR - P
            pe.transpose(pm[4][:, P:NPAR], par_rows[0:n1, 1, :], ident[0:n1, 0:n1])
            pe.wait_ge(hist_in, 32)
            for t in range(XT):
                pe.transpose(acc[:, t // 12, (t % 12) * 24:(t % 12) * 24 + 24], hrow_s[0:24, t * P:(t + 1) * P], ident[0:24, 0:24])
            for t in range(KT):
                tr = pe.transpose(acc[:, 2, t * 16:t * 16 + 16], hrow_a[0:16, t * P:(t + 1) * P], ident[0:16, 0:16])
            tr.then_inc(par_turned, 1)
            for a in range(NROW):
                n = row_tile(a)[0]
                pe.wait_ge(normed[a % 2], a // 2 + 1)
                for h in range(2):
                    if a >= 2:
                        pe.wait_ge(u_split, 2 * (a - 2) + h + 1)
                    for k in range(4):
                        tr = pe.transpose(pm[2 * (a % 2) + h][:, k * P:k * P + n], xn[a % 2][0:n, (4 * h + k) * P:(4 * h + k + 1) * P],
                                          ident[0:n, 0:n])
                    tr.then_inc(turned, 1)
            pe.wait_ge(u_split, 2 * NROW)
            pe.wait_ge(par_copied, 5)
            with pe.Fori(0, XT // 3) as i:
                for r in range(3):
                    dense(pe, xbc_tile(i, r), uhi, ulo)
            with pe.Fori(0, 5) as i:
                for r in range(3):
                    dense(pe, z_tile(i, r), uhi, ulo)
            dense(pe, last_z, uhi, ulo)
            dense(pe, dt_tile, uhi, ulo)
            KV_PIECE = ((NP - 1, 0),)
            dense(pe, kv0, mhi, mlo, KV_PIECE, NM)
            with pe.Fori(0, 5) as i:
                for r in range(3):
                    dense(pe, kv_tile(i, r), mhi, mlo, KV_PIECE, NM)
            pe.wait_ge(cs_ready, 1)
            for n, v in enumerate((dtv, csv)):
                for c in range(NCH):
                    tr = pe.transpose(pm[0][:, (n * NCH + c) * HEADS:(n * NCH + c + 1) * HEADS], v[0:HEADS, c * CH:(c + 1) * CH],
                                      ident[0:HEADS, 0:HEADS])
            tr.then_inc(pre_turned, 1)
            pe.wait_ge(bcx_in, 16)
            pe.wait_ge(pre_copied, 2)
            pe.transpose(pm[0][0:64, 0:P], bcx.rearrange("p t b -> p (t b)"), ident[:]).then_inc(pre_turned, 1)
            pe.wait_ge(evac[NP - 1], TM + 1)
            for n in range(8):
                s, m, h = n // 4, n // 2 % 2, n % 2
                if n >= 4:
                    pe.wait_ge(pre_copied, n)
                for k in range(4):
                    tr = pe.transpose(pm[1 + n % 4][:, k * P:(k + 1) * P], kv_t[:, s * KT + h * 4 + k, m * P:(m + 1) * P], ident[:])
                tr.then_inc(pre_turned, 1)
            pe.wait_ge(pre_copied, 2)
            pe.wait_ge(pre_copied, 11)
            with pe.Fori(0, NCH) as c:
                for g in range(GROUPS):
                    n, b, u = c * 4 + g, g % 2, c * 2 + g // 2
                    bg, cg = xg[b][:, 4, :], xg[b][:, 5, :]
                    pe.wait_ge(group_in[b], (u + 1) * 64)
                    pe.wait_ge(h_added, n + 1)
                    for k in range(4):
                        tr = pe.transpose(pm[0][:, k * P:(k + 1) * P], xg[b][:, k, :], ident[:])
                    tr.then_inc(x_turned, 1)
                    pe.transpose(pm[1][:, 0:P], bg, ident[:])
                    pe.matmul(pm[1][:, P:2 * P], bg, cg, start=True, stop=True).then_inc(b_ready, 1)
                    pe.wait_ge(y_out, n * 4 + 1)
                    for k in range(4):
                        tr = pe.transpose(pm[2][:, k * P:(k + 1) * P], zg[b][:, k, :], ident[:])
                    tr.then_inc(z_turned, 1)
                    dense(pe, main_tile(c, SEG[g][0]), uhi, ulo)
                    pe.wait_ge(m_ready, n + 1 + 1)
                    pe.wait_ge(xdd_ready, n + 1)
                    pe.wait_ge(bt_ready, n + 1)
                    pe.matmul(pm[3][:], cg, hT[:, g, :], start=True, stop=True)
                    for h in range(HG):
                        pe.matmul(pm[4][:, h * HD:(h + 1) * HD], mm_[:, h, :], xdt[:, h * HD:(h + 1) * HD], start=True, stop=True)
                    pe.matmul(pm[0][:], bt, xdd, start=True, stop=True).then_inc(summed[b], 1)
                    for m in SEG[g][1:]:
                        dense(pe, main_tile(c, m), uhi, ulo)
                    pe.wait_ge(gyn_ready, n + 1 + 1)
                    for k in range(4):
                        tr = pe.transpose(pm[2][:, k * P:(k + 1) * P], gyn[:, k * P:(k + 1) * P], ident[:])
                    tr.then_inc(y_turned, 1)
            pe.wait_ge(h_added, 33)
            pe.wait_ge(y_out, 129)
            pe.wait_ge(gyn_ready, 33)
            for n in range(4):
                for k in range(4):
                    tr = pe.transpose(pm[n][:, k * P:(k + 1) * P], hT[:, n, k * P:(k + 1) * P], ident[:])
                tr.then_inc(S["h_final"], 1)
            pe.wait_ge(S["dec_sq_done"], 1)
            pe.matmul(pm[4][:, 0:P], ones[:], dec_sq.rearrange("p t b -> p (t b)"), start=True, stop=True).then_inc(S["dec_summed"], 1)
            pe.wait_ge(S["qx_in"], 16)
            pe.wait_ge(S["dec_step"], 1)
            pe.transpose(pm[4][0:64, P:2 * P], qx.rearrange("p t b -> p (t b)"), ident[:]).then_inc(S["qx_turned"], 1)
            pe.wait_ge(S["h_copied"], 4)
            pe.wait_ge(S["qx_copied"], 1)
            def out_dense(b, i, r):
                dense(pe, out_tile(b, i, r), uhi, ulo, acts=(S["act_split"], b * NP))
            def scores(i, half):
                u = i + half * 4
                pe.wait_ge(S["att_in"], (u + 1) * 64)
                pe.wait_ge(S["att_ready"], u * 2 + 1)
                for k in range(4):
                    for d in range(2):
                        mm = pe.matmul(pm[k // 2][:, (k % 2) * NM:(k % 2 + 1) * NM], aq[:, d, k * P:(k + 1) * P], ak[:, d, :],
                                       start=d == 0, stop=d == 1)
                mm.then_inc(S["qk_done"], 1)
            def turn_probs(i, half):
                u = i + half * 4
                pe.wait_ge(S["att_step"], u * 5 + 5)
                pe.wait_ge(S["p_copied"], u * 2 + 1)
                for m in range(2):
                    for k in range(4):
                        tr = pe.transpose(pm[2 + m][:, k * P:(k + 1) * P], pt[:, k, m * P:(m + 1) * P], ident[:])
                    tr.then_inc(S["p_turned"], 1)
            def values(i, half):
                u = i + half * 4
                pe.wait_ge(S["p_copied"], (u + 1) * 2 + 1)
                for d in range(2):
                    for m in range(2):
                        mm = pe.matmul(pm[4 * (1 - d)][:], avv[:, m, d * P:(d + 1) * P], ptT[:, m, :], start=m == 0, stop=m == 1)
                mm.then_inc(S["pv_done"], 1)
            for half in range(2):
                with pe.Fori(0, 4) as i:
                    scores(i, half)
                    out_dense(half, i, 0)
                    turn_probs(i, half)
                    out_dense(half, i, 1)
                    values(i, half)
            pe.wait_ge(S["sam_kept"], 9)
            pe.wait_ge(S["att_ready"], 17)
            for m in range(2):
                tr = pe.transpose(pm[0][0:32, m * P:(m + 1) * P], sds[:, m, :, :].rearrange("p b h -> p (b h)"), ident[:])
            tr.then_inc(S["sds_turned"], 1)
            for src, dst, n, q, x in TAILS:
                if x >= 3:
                    pe.wait_ge(S["tail_copied"], x - 2)
                for k in range(4):
                    tr = pe.transpose(pm[2 + x % 3][0:n, k * P:(k + 1) * P], src[:, q * 4 + k, :], ident[:])
                tr.then_inc(S["tail_turned"], 1)
            pe.wait_ge(S["sam_step"], 4)
            for m in range(2):
                tr = pe.transpose(pm[1][:, m * 32:(m + 1) * 32], dp[0:32, m, :], ident[0:32, 0:32])
            tr.then_inc(S["dp_turned"], 1)
            pe.wait_ge(S["dp_copied"], 1)
            pe.wait_ge(S["tail_copied"], 8)
            with pe.Fori(0, 4) as i:
                for r in range(SLOT2):
                    out_dense(2, i, r)
                    k = i * 2 + r
                    pe.wait_ge(S["v_in"], (k + 1) * 16)
                    for t in range(KT):
                        for m in range(2):
                            mm = pe.matmul(pm[3][:, bass.ds(k * KT + t, 1)], dk[:, m, t * P:(t + 1) * P],
                                           dpT[:, m, bass.ds(k * 4 + t // 2, 1)], start=m == 0, stop=m == 1)
                    mm.then_inc(S["v_used"], 1)
            for b in (3, 4):
                with pe.Fori(0, 4) as i:
                    for r in range(SLOT2):
                        out_dense(b, i, r)
            for p in range(NP):
                pe.wait_ge(evac[p], ((TM if p == NP - 1 else FM) + 72 + 40) + 1)
            for a in range(NCH + 1):
                n = P if a < NCH else NB
                for h in range(2):
                    if a >= 2:
                        pe.wait_ge(S["row_sum"], 2 * (a - 2) + h + 1)
                    for k in range(4):
                        tr = pe.transpose(pm[2 * (a % 2) + h][0:n, k * P:(k + 1) * P], merged[:, 4 * h + k, a * P:a * P + n], ident[:])
                    tr.then_inc(S["row_turned"], 1)



INPUTS = ["x_prompt", "x_sample", "mem_prompt", "state_conv_a", "state_conv_s", "state_ssm", "cache_mem_k",
          "cache_mem_v", "norm_w", "w_in", "conv_a_w", "w_a_out", "conv_s_w", "conv_s_b", "dt_bias", "a_log",
          "d_skip", "ssm_norm_w", "w_s_out", "mem_norm_w", "w_mem_kv", "w_m_out", "w_o", "final_norm_w"]
OUTPUTS = {"y_prompt": (1, SEQ, D), "y_sample": (NB, 1, D), "p_conv_a": (1, 1, KA - 1, D),
           "p_conv_s": (1, 1, KS - 1, XBC), "p_ssm": (1, 1, HEADS, HD, NS), "p_mem_k": (1, 1, NM, MH, MD),
           "p_mem_v": (1, 1, NM, MH, MD), "s_conv_a": (1, NB, KA - 1, D), "s_conv_s": (1, NB, KS - 1, XBC),
           "s_ssm": (1, NB, HEADS, HD, NS)}


def kernel(**inputs):
    import numpy as np
    import concourse.bacc as bacc
    from concourse.bass_utils import run_bass_kernel_spmd

    nc = bacc.Bacc("TRN2", target_bir_lowering=False, num_devices=1)
    arrays, ins, outs = {}, {}, {}
    for name in INPUTS:
        a = np.ascontiguousarray(inputs[name])
        arrays[f"in_{name}"] = a
        ins[name] = nc.dram_tensor(f"in_{name}", a.shape, F32, kind="ExternalInput").ap()
    for name, shape in OUTPUTS.items():
        outs[name] = nc.dram_tensor(f"out_{name}", shape, F32, kind="ExternalOutput").ap()
    build(nc, ins, outs)
    r = run_bass_kernel_spmd(nc, [arrays], core_ids=[0])
    return tuple(r.results[0][f"out_{name}"] for name in OUTPUTS)
```

```python
from contextlib import ExitStack

import concourse.bass as bass
from concourse import mybir

ALU = mybir.AluOpType
ACT = mybir.ActivationFunctionType
AX = mybir.AxisListType
F32 = mybir.dt.float32
F32R = mybir.dt.float32r

P = 128
D = 1024
SEQ = 1024
NB = 8
T = SEQ + NB
KT = D // P
NP = 3
PC = T // NP
INNER = 2 * D
HEADS, HD = 32, 64
GROUPS, HG = 4, 8
NS = 128
XBC = INNER + 2 * GROUPS * NS
KS, KA = 4, 3
CH = 128
NCH = SEQ // CH
NM, MH, MD = 256, 4, 256
EPS = 1e-6
ZT, XT = INNER // P, XBC // P
O_CB, O_CC, O_CH, O_CZ, O_SZ = 0, D, 2 * D, 3 * D, 4 * D
O_XBC = O_SZ + INNER
O_DT = O_XBC + XBC
O_MQ = O_DT + HEADS
O_MZ = O_MQ + D
O_G = O_MZ + D
C_SW, C_SB, C_NW = 0, KS * XT, KS * XT + XT
C_AW = C_NW + KT
C_SN = C_AW + KA * KT
C_MN = C_SN + ZT
NPAR = C_MN + KT
TAIL_S, TAIL_A = KS - 1 + NB, KA - 1 + NB
LOG1P_TERMS = 9


def build(nc, I, O):
    dram = lambda n, s: nc.dram_tensor(n, s, F32, kind="Internal").ap()
    s_xbc = dram("s_xbc", (XBC, T))
    s_z = dram("s_z", (INNER, T))
    s_q = dram("s_q", (D, T))
    s_mz = dram("s_mz", (D, T))
    s_g = dram("s_g", (3 * D, T))
    s_a = dram("s_a", (D, T))
    s_y = dram("s_y", (INNER, T))
    s_o = dram("s_o", (D, T))
    s_cs = dram("s_cs", (HEADS, SEQ))
    s_dd = dram("s_dd", (HEADS, 2, NB))
    s_bc = dram("s_bc", (NCH, 2, NB, P))
    s_kt = dram("s_kt", (D, NM))
    s_qd = dram("s_qd", (KT * NB, P))

    w_in = I["w_in"][0].rearrange("(k p) n -> p k n", p=P)
    w_kv = I["w_mem_kv"][0].rearrange("(k p) n -> p k n", p=P)

    with ExitStack() as ctx:
        used = [0]

        def sb(name, shape, dt=F32):
            n = 1
            for s in shape[1:]:
                n *= s
            used[0] += 4 * n
            return ctx.enter_context(nc.sbuf_tensor(name, shape, dt))

        def sem(name):
            return ctx.enter_context(nc.semaphore(name))

        acc = ctx.enter_context(nc.psum_tensor("acc", [P, NP, 512], F32))
        pm = [ctx.enter_context(nc.psum_tensor(f"pm{i}", [P, 512], F32)) for i in range(5)]
        uhi = sb("uhi", [P, KT, T], F32R)
        ulo = sb("ulo", [P, KT, T], F32R)
        raw, whi, wlo = [], [], []
        for r in range(3):
            if r == 2:
                with nc.sbuf_tensor("slot2", [P, 3 * KT * P], F32) as slot2:
                    pass
                with nc.sbuf_tensor("wo_lo_b", [P, 3, D], F32R) as wo_lo_b:
                    pass
            raw.append(sb(f"raw{r}", [P, KT, P]))
            whi.append(sb(f"whi{r}", [P, KT, P], F32R))
            wlo.append(sb(f"wlo{r}", [P, KT, P], F32R))
        stage = [sb(f"stage{r}", [P, T]) for r in range(3)]
        ident = sb("ident", [P, P])
        tri = sb("tri", [P, P])
        ones = sb("ones", [P, P])
        epsc = sb("epsc", [P, 1])
        par = sb("par", [P, NPAR])
        hist_s = sb("hist_s", [P, XT, NB, KS - 1])
        hist_a = sb("hist_a", [P, KT, NB, KA - 1])
        tail_s = sb("tail_s", [P, XT, TAIL_S])
        tail_a = sb("tail_a", [P, KT, TAIL_A])
        cs_tok = sb("cs_tok", [P, NCH * HEADS])
        dt_tok = sb("dt_tok", [P, NCH * HEADS])
        dskip = sb("dskip", [P, HEADS])
        ARENA = 22096
        with nc.sbuf_tensor("mhi", [P, KT, NM], F32R) as mhi, nc.sbuf_tensor("mlo", [P, KT, NM], F32R) as mlo:
            pass
        WO_A, WO_GAP = KT * T, 2 * KT * PC - 5 * D
        with nc.sbuf_tensor("below", [P, WO_A], F32), nc.sbuf_tensor("wo_hi_a", [P, 5, D], F32R) as wo_hi_a, \
                nc.sbuf_tensor("wo_lo_a", [P, 5, D], F32R) as wo_lo_a, nc.sbuf_tensor("between", [P, WO_GAP], F32), \
                nc.sbuf_tensor("wo_hi_b", [P, 3, D], F32R) as wo_hi_b:
            pass
        arena = sb("arena", [P, ARENA])

        M0 = 2 * KT * NM
        cursor = [M0]

        def view(*shape, at=None):
            n = 1
            for s in shape:
                n *= s
            if at is None:
                at = cursor[0]
            cursor[0] = at + n
            assert cursor[0] <= ARENA, (cursor[0], shape)
            v = arena[:, at:at + n]
            if len(shape) == 2:
                v = v.rearrange("p (a b) -> p a b", b=shape[1])
            if len(shape) == 3:
                v = v.rearrange("p (a b c) -> p a b c", b=shape[1], c=shape[2])
            return v

        w_loaded = [sem(f"w_loaded{r}") for r in range(3)]
        w_high = [sem(f"w_high{r}") for r in range(3)]
        w_split = [sem(f"w_split{r}") for r in range(3)]
        ready = [sem(f"ready{p}") for p in range(NP - 1)]
        done = [sem(f"done{r}") for r in range(3)]
        evac = [sem(f"evac{p}") for p in range(NP)]
        stored = [sem(f"stored{r}") for r in range(3)]

        const_ready = sem("const_ready")

        paced = sem("paced")
        pace = [0]

        def settle(e, times=1):
            pace[0] += times
            e.sem_inc(paced, 1)

        def load_w(sp, t, src):
            sp.wait_ge(w_split[t[1]], t[0] + 1)
            settle(sp)
            sp.dma_start(raw[t[1]][:], src).then_inc(w_loaded[t[1]], 16)

        def split_w(pool, t):
            q, r = t[0], t[1]
            pool.wait_ge(w_loaded[r], (q + 1) * 16)
            pool.wait_ge(done[r], q + 1)
            settle(pool)
            pool.tensor_scalar(whi[r][:], raw[r][:], 1.0, 0.0, ALU.mult, ALU.add).then_inc(w_high[r], 1)
            pool.wait_ge(w_high[r], q + 1)
            pool.tensor_tensor(wlo[r][:], raw[r][:], whi[r][:].bitcast(F32), ALU.subtract).then_inc(w_split[r], 1)

        def product(pe, t, out, hi, lo, c0, n):
            r = t[1]
            for k in range(KT):
                for s, (w, a) in enumerate(((whi, hi), (wlo, hi), (whi, lo))):
                    mm = pe.matmul(out, w[r][:, k, :], a[:, k, c0:c0 + n], start=k == 0 and s == 0, stop=k == KT - 1 and s == 2)
            return mm

        def dense(pe, t, acts=None):
            q, r, n = t
            pe.wait_ge(w_split[r], q + 1 + 1)
            for p in range(NP):
                pe.wait_ge(evac[p], n + 1)
                if acts:
                    pe.wait_ge(acts[0], acts[1] + p + 1)
                product(pe, t, acc[:, p, 0:PC], uhi, ulo, p * PC, PC).then_inc(done[r] if p == NP - 1 else ready[p], 1)

        def piece_ready(e, t, p):
            if p == NP - 1:
                e.wait_ge(done[t[1]], t[0] + 1 + 1)
            else:
                e.wait_ge(ready[p], t[2] + 1)

        def read_out(act, t, out, func, scale=1.0):
            for p in range(NP):
                piece_ready(act, t, p)
                act.activation(out[:, p * PC:(p + 1) * PC], acc[:, p, 0:PC], func, scale=scale).then_inc(evac[p], 1)

        def evacuated(e, t):
            for p in range(NP):
                e.wait_ge(evac[p], t[2] + 1 + 1)

        def to_dram(act, t, use, dst, func, scale=1.0):
            r = t[1]
            act.wait_ge(stored[r], use * 16 + 1)
            read_out(act, t, stage[r], func, scale)
            evacuated(act, t)
            act.dma_start(dst, stage[r][:]).then_inc(stored[r], 16)

        xbc_tile = lambda i, r: (i, r, i * 3 + r)
        Q1 = XT // 3
        dt_tile, z_first = (Q1, 0, XT), [(Q1, 1, XT + 1), (Q1, 2, XT + 2)]
        mixed_tile = lambda i, j: (i * 2 + Q1 + 1 + j // 3, j % 3, None if j % 3 else i * 2 + XT + 3 + j // 3)
        late_z = lambda i, r: (i + Q1 + 9, r, i * 3 + XT + 11 + r)
        QM, FM = Q1 + 11, XT + 1 + ZT
        main_tile = lambda c, m: (c * 3 + QM + m // 3, m % 3, c * 9 + FM + m)

        xbc_src = lambda j: w_in[:, :, bass.ds(j * P + O_XBC, P)]
        z_src = lambda j: w_in[:, :, bass.ds(j * P + O_SZ, P)]
        kv_src = lambda j: w_kv[:, :, bass.ds(j * P, P)]
        MAIN = (O_CC, O_CH, O_CZ, O_CB, O_MQ, O_MZ, O_G, O_G + D, O_G + 2 * D)
        rows = lambda d, j: d[bass.ds(j * P, P), :]

        rows_in = [sem(f"rows_in{b}") for b in range(2)]
        par_in, hist_in, small_in = sem("par_in"), sem("hist_in"), sem("small_in")
        square_done, root_done, rs_done = sem("square_done"), sem("root_done"), sem("rs_done")
        normed = [sem(f"normed{b}") for b in range(2)]
        turned, u_high, u_split = sem("turned"), sem("u_high"), sem("u_split")
        par_turned, par_copied = sem("par_turned"), sem("par_copied")
        xr = [view(D), view(D)]
        xn = [view(D), view(D)]
        nwb, mwb = view(D), view(D)
        junk = view(D)
        par_rows = view(2, P)
        hrow_s, hrow_a = view(XBC), view(D)
        ssq, root, rs = view(16), view(16), view(16)
        NROW = SEQ // P + 1 + NM // P
        def row_tile(a):
            if a < SEQ // P:
                return P, I["x_prompt"][0, a * P:(a + 1) * P, :], a * P
            if a == SEQ // P:
                return NB, I["x_sample"][:, 0, :], SEQ
            a -= SEQ // P + 1
            return P, I["mem_prompt"][0, a * P:(a + 1) * P, :], a * P
        xp = view(T + KS - 1, at=M0 + 15900)
        cv = view(T)
        dtb, alog = view(1), view(1)
        conv = [sem(f"conv{k}") for k in range(KS)]
        silu_done, tails_kept, pads_ready = sem("silu_done"), sem("tails_kept"), sem("pads_ready")

        kv_t = view(2 * KT, NM, at=M0)
        kv_tok = view(2, 2, D)
        kv_saved = sem("kv_saved")
        kv_evac = [sem(f"kv_evac{b}") for b in range(2)]
        KV_BANK = {1: 0, 2: 1, 4: 0, 5: 1}
        z_of = lambda i, j: i * 2 + 2 + j // 3
        kv_of = lambda i, j: i * 4 + (j - 1 if j < 3 else j - 2)
        pre_turned, pre_copied = sem("pre_turned"), sem("pre_copied")
        DT0 = M0 + 8192
        dtv = view(T, at=DT0)
        absv, expo, zz, csv = view(T), view(T), view(T), view(T)
        da, resets = absv, zz
        aneg, dd = view(1), view(2, NB)
        dt_step, dt_abs, dt_exp = sem("dt_step"), sem("dt_abs"), sem("dt_exp")
        dt_ready, cs_ready, dd_exp, dd_ready, cs_saved = sem("dt_ready"), sem("cs_ready"), sem("dd_exp"), sem("dd_ready"), sem("cs_saved")
        bcx, bcr = view(8, NB), view(P)
        bcx_in, bc_saved, dec_in = (sem(n) for n in ("bcx_in", "bc_saved", "dec_in"))
        SEG = ((0, 1), (2, 3), (4, 5), (6, 7, 8))
        xg = [view(6, CH, at=0 if b == 0 else None) for b in range(2)]
        zg = [view(4, CH) for b in range(2)]
        csb = [view(HG, CH) for b in range(2)]
        xt, bt, scm = view(512), view(CH), view(CH)
        xdt, xdd = view(512), view(512)
        seg, mm_ = view(HG, CH), view(HG, CH)
        yv, gy, gyn, yT = view(512), view(512), view(512), view(4, CH)
        sa, sm = view(3, HG), view(3, HG)
        ss2, rt2, rs2, nw2, var2 = view(1), view(1), view(1), view(1), view(1)
        dec_x, dec_z, dec_xdt, dec_y, dec_sq = (view(ZT, NB) for _ in range(5))
        dec_dd = view(ZT, 2, NB)
        dec_skip = view(ZT)
        dec_ms, dec_rs, dec_nw = view(GROUPS, NB), view(GROUPS, NB), view(GROUPS, NB)
        hT = view(GROUPS, 512)
        FIRST = cursor[0]
        cc, zc, av = view(T), view(T), view(T)
        hb = view(T + KA - 1)
        bcd = view(2, NB, P)
        sd, sd2 = view(NB, P), view(NB, P)
        bcd_in, sd_in, sd_step, sd_saved, dec_ready = sem("bcd_in"), sem("sd_in"), sem("sd_step"), sem("sd_saved"), sem("dec_ready")
        ssm_in = I["state_ssm"][0].rearrange("b h p n -> (h p) b n")
        ssm_out = O["s_ssm"][0].rearrange("b h p n -> (h p) b n")
        group_in = [sem(f"group_in{b}") for b in range(2)]
        summed = [sem(f"summed{b}") for b in range(2)]
        x_turned, b_ready, z_turned, x_copied = sem("x_turned"), sem("b_ready"), sem("z_turned"), sem("x_copied")
        args_ready, sm_ready, seg_ready, e_ready = sem("args_ready"), sem("sm_ready"), sem("seg_ready"), sem("e_ready")
        bt_ready, sc_ready, xdt_ready, xdd_ready, m_ready = (sem(n) for n in ("bt_ready", "sc_ready", "xdt_ready", "xdd_ready", "m_ready"))
        y_step, gy_ready, h_scaled, h_added = sem("y_step"), sem("gy_ready"), sem("h_scaled"), sem("h_added")
        sq2_done, rt2_done, rs2_step, gyn_ready = sem("sq2_done"), sem("rt2_done"), sem("rs2_step"), sem("gyn_ready")
        y_turned, y_out, y_stored = sem("y_turned"), sem("y_out"), sem("y_stored")
        tails_a_kept, a_conv, a_ready = (
            sem(n) for n in ("tails_a_kept", "a_conv", "a_ready"))
        STAGED = (Q1 + 10, Q1 + 3, Q1 + 3)
        def staged(c, m):
            return c * 2 + STAGED[m % 3] + (m >= 6)
        def bcast(v, n):
            return v.unsqueeze(2).to_broadcast([P, v.shape[1], n])
        def heads(v):
            return v.rearrange("p (h d) -> p h d", h=HG)
        def group_before(e, c, g):
            if g % 2:
                e.wait_ge(summed[0], c * 2 + g // 2 + 1 + 1)
            else:
                e.wait_ge(summed[1], c * 2 + g // 2 + 1)
        PASSES = 4
        SLOT2 = 2
        def out_tile(b, i, r):
            n = i * 2 + (b * KT + r)
            return i + (QM + 24 + b * 4), r, n + (FM + 72)
        OUT_W = [I[w][0].rearrange("(k p) n -> p k n", p=P) for w in ("w_a_out", "w_s_out", "w_m_out")]
        out_w = lambda b: (OUT_W[0], OUT_W[1][:, 0:KT], OUT_W[1][:, KT:], OUT_W[2])[b]
        GATE = (0, 1, 1, 2)
        tiles_of = lambda d: d.rearrange("(t p) n -> p t n", p=P)
        ACTS = (tiles_of(s_a), tiles_of(s_y)[:, 0:KT], tiles_of(s_y)[:, KT:], tiles_of(s_o))
        merged = view(KT, T, at=0)
        A0 = cursor[0]
        aq, ak, avv, amz = view(2, 512), view(2, NM), view(2, MD), view(2, 512)
        pt, ptT = view(4, NM), view(2, 512)
        piece_at = cursor[0]
        piece_buf = [view(KT, PC) for _ in range(2)]
        piece_buf.append(slot2[:, 0:KT * PC].rearrange("p (k n) -> p k n", n=PC))
        K0 = cursor[0]
        dk = view(2, D)
        dq = view(D)
        qx = view(KT, NB)
        assert qx.shape and cursor[0] <= ARENA, cursor[0]
        first_buf = [view(KT, PC, at=FIRST + p * KT * PC) for p in range(NP)]
        acts_buf = lambda b, p: first_buf[p] if b == 0 else piece_buf[p]
        pso = view(16, P, at=6144)
        trow_s, trow_a = view(XBC, at=A0), view(D)
        vv = [(dk[:, 0, :], dk[:, 1, :]), (view(D), dq)]
        wo_raw = [view(D, at=piece_at + k * D) for k in range(5)] + [slot2[:, k * D:(k + 1) * D] for k in range(3)]
        wo_lo = [wo_lo_a[:, k, :] for k in range(5)] + [wo_lo_b[:, k, :] for k in range(3)]
        wo_hi = [wo_hi_a[:, k, :] for k in range(5)] + [wo_hi_b[:, k, :] for k in range(3)]
        assert (A0, piece_at, K0) == (WO_A, WO_A + 5 * D, WO_A + 10 * D + WO_GAP)
        xf = [view(D, at=0), view(D)]
        rr = [view(D), view(D)]
        fw, fjunk = view(D), view(D)
        small_at = [0]
        def small(*shape):
            n = 1
            for x in shape:
                n *= x
            v = stage[2][:, small_at[0]:small_at[0] + n]
            small_at[0] += n
            assert small_at[0] <= T
            return v.rearrange("p (a b) -> p a b", b=shape[-1]) if len(shape) == 2 else (
                v if len(shape) == 1 else v.rearrange("p (a b c) -> p a b c", b=shape[1], c=shape[2]))
        qrow = small(P)
        amx, anx, asum, arec = small(4), small(4), small(4), small(4)
        sde = small(2, 4)
        sds = small(2, NB, 4)
        dmx, dnx, dsum, drec = small(1), small(1), small(1), small(1)
        dp = small(2, P)
        dpT = small(2, NB * 4)
        mzd = small(KT, NB)
        fss, frt, frs, fvar, fnw = small(9), small(9), small(9), small(9), small(9)
        SEMS = """h_final h_copied h_saved dec_sq_done dec_summed dec_root dec_step dec_saved qx_in qx_turned qx_copied q_saved
            act_high act_split qk_in att_in qk_done att_step att_exp p_turned p_copied pv_done
            att_ready att_saved sam_in sam_read sam_kept sds_turned sam_step sam_exp dp_turned dp_copied
            v_scaled v_used mzd_in od_ready tail_turned tail_copied tail_saved copied_dram
            last_merged wo_high wo_split row_done row_sum row_sq row_root row_step row_out""".split()
        S = {n: sem(n) for n in SEMS}
        act_in = [sem(f"act_in{p}") for p in range(NP)]
        v_in = [sem(f"v_in{b}") for b in range(2)]
        wo_in = sem("wo_in")
        gate_in = [sem(f"gate_in{r}") for r in range(2)]
        merge_done = [sem(f"merge_done{r}") for r in range(2)]
        row_saved = [sem(f"row_saved{r}") for r in range(2)]
        TAILS = [(tail_s, trow_s, TAIL_S, n, n) for n in range(6)] + [(tail_a, trow_a, TAIL_A, n, n + 6) for n in range(2)]
        def load_v(e, k, b):
            src = I["cache_mem_v"][0, bass.ds(k, 1)].rearrange("c (a m) h d -> a m (c h d)", m=P)
            for a in range(2):
                e.dma_start(vv[b][a], src[a]).then_inc(v_in[b], 16)
        def last_piece(e, b, p):
            if p < NP - 1:
                e.wait_ge(ready[p], FM + 72 + b * KT)
            elif b == 0:
                e.wait_ge(done[2], QM + 24 + 1)
            else:
                e.wait_ge(done[1], QM + 24 + b * 4 + 1)
        OPENED = (*kv_evac, *w_split, *done, *evac, *conv, tails_kept, *stored, silu_done, *summed, gy_ready, y_turned, y_stored, a_ready,
                  tails_a_kept, a_conv, sm_ready, m_ready, gyn_ready, sd_step, sd_saved, y_out, *merge_done,
                  *(S[n] for n in ("att_saved", "att_exp", "p_turned", "pv_done", "qk_done", "sam_read", "sam_kept", "v_used",
                                   "att_ready", "p_copied")))


        block = ctx.enter_context(nc.Block())

        @block.sync
        def _(sp):
            for v, (r0, n) in {"conv_s_w": (C_SW, KS * XT), "conv_s_b": (C_SB, XT), "norm_w": (C_NW, KT)}.items():
                src = I[v].rearrange("a (t p) -> (a t) p", p=P) if v != "conv_s_w" else I[v][0].rearrange("k (t p) -> (k t) p", p=P)
                sp.dma_start(par_rows[r0:r0 + n, 0, :], src).then_inc(par_in, 16)
            for v, (r0, n) in {"conv_a_w": (0, KA * KT), "ssm_norm_w": (KA * KT, ZT), "mem_norm_w": (KA * KT + ZT, KT)}.items():
                src = I[v].rearrange("a (t p) -> (a t) p", p=P) if v != "conv_a_w" else I[v][0].rearrange("k (t p) -> (k t) p", p=P)
                sp.dma_start(par_rows[r0:r0 + n, 1, :], src).then_inc(par_in, 16)
            sp.dma_start(nwb, I["norm_w"].to_broadcast([P, D])).then_inc(small_in, 16)
            sp.dma_start(mwb, I["mem_norm_w"].to_broadcast([P, D])).then_inc(small_in, 16)
            sp.dma_start(dskip[:], I["d_skip"].to_broadcast([P, HEADS])).then_inc(small_in, 16)
            sp.dma_start(dtb[0:HEADS, :], I["dt_bias"].rearrange("a h -> h a")).then_inc(small_in, 16)
            sp.dma_start(alog[0:HEADS, :], I["a_log"].rearrange("a h -> h a")).then_inc(small_in, 16)
            sp.dma_start(hrow_s[0:NB * (KS - 1), :], I["state_conv_s"][0].rearrange("b k c -> (b k) c")).then_inc(hist_in, 16)
            sp.dma_start(hrow_a[0:NB * (KA - 1), :], I["state_conv_a"][0].rearrange("b k c -> (b k) c")).then_inc(hist_in, 16)
            for a in range(NROW):
                n, src, _ = row_tile(a)
                if a >= 2:
                    sp.wait_ge(normed[a % 2], a // 2)
                sp.dma_start(xr[a % 2][0:n, :], src).then_inc(rows_in[a % 2], 16)
            with sp.Fori(0, XT // 3) as i:
                for r in range(3):
                    load_w(sp, xbc_tile(i, r), xbc_src(i * 3 + r))
            load_w(sp, dt_tile, w_in[:, :, O_DT:O_DT + P])
            for n in range(2):
                load_w(sp, z_first[n], w_in[:, :, O_SZ + n * P:O_SZ + (n + 1) * P])
            with sp.Fori(0, 4) as i:
                for j in range(6):
                    load_w(sp, mixed_tile(i, j), kv_src(kv_of(i, j)) if j % 3 else z_src(z_of(i, j)))
            with sp.Fori(0, 2) as i:
                for r in range(3):
                    load_w(sp, late_z(i, r), z_src(i * 3 + 10 + r))
            sp.wait_ge(cs_ready, 1)
            sp.dma_start(s_cs, csv[0:HEADS, 0:SEQ]).then_inc(cs_saved, 16)
            sp.wait_ge(dd_ready, 2)
            sp.dma_start(s_dd, dd[0:HEADS, :, :]).then_inc(cs_saved, 16)
            for b in range(2):
                sp.wait_ge(kv_evac[b], KT + 1)
            sp.dma_start(s_kt.rearrange("(t p) m -> p t m", p=P), kv_t[:, 0:KT, :]).then_inc(kv_saved, 16)
            sp.wait_ge(pre_copied, 10)
            for s, dst in enumerate(("p_mem_k", "p_mem_v")):
                sp.dma_start(O[dst][0, 0].rearrange("(a m) h d -> m a (h d)", m=P), kv_tok[:, s, :, :]).then_inc(kv_saved, 16)
            sp.wait_ge(pre_copied, 11)
            for c in range(NCH):
                for s in range(2):
                    r0 = (s * GROUPS + c // 2) * NB
                    sp.dma_start(s_bc[c, s], bcr[r0:r0 + NB, :]).then_inc(bc_saved, 16)
            xbc_t = s_xbc.rearrange("(t p) n -> p t n", p=P)
            z_t = s_z.rearrange("(t p) n -> p t n", p=P)
            def sample_inputs():
                sp.dma_start(dec_x, s_xbc[0:INNER, SEQ:].rearrange("(t p) b -> p t b", p=P)).then_inc(dec_in, 16)
                for e in range(2):
                    part = slice(e * HD, (e + 1) * HD)
                    sp.dma_start(dec_dd[part, :, :, :], s_dd[e::2].unsqueeze(0).to_broadcast([HD, ZT, 2, NB])).then_inc(dec_in, 16)
            sp.wait_ge(kv_saved, 48)
            sp.wait_ge(cs_saved, 32)
            sample_inputs()
            sp.wait_ge(bc_saved, 16 * 16)
            for r, n in enumerate((Q1 + 8, Q1 + 1, Q1 + 1)):
                sp.wait_ge(stored[r], 16 * n + 1)
            with sp.Fori(0, NCH) as c:
                for g in range(GROUPS):
                    b, u = g % 2, c * 2 + g // 2
                    sp.wait_ge(summed[b], u + 1)
                    settle(sp)
                    if g == 2:
                        for r in range(3):
                            sp.wait_ge(stored[r], 16 * STAGED[r] + 1)
                    tok = bass.ds(c * CH, CH)
                    sp.dma_start(xg[b][:, 0:4, :], xbc_t[:, 4 * g:4 * g + 4, tok]).then_inc(group_in[b], 16)
                    sp.dma_start(xg[b][:, 4:6, :], xbc_t[:, ZT + g::GROUPS, tok]).then_inc(group_in[b], 16)
                    sp.dma_start(zg[b], z_t[:, 4 * g:4 * g + 4, tok]).then_inc(group_in[b], 16)
                    sp.dma_start(csb[b], s_cs[g * HG:(g + 1) * HG, tok].unsqueeze(0).to_broadcast([P, HG, CH])).then_inc(group_in[b], 16)
                    for m in SEG[g]:
                        load_w(sp, main_tile(c, m), w_in[:, :, bass.ds(c * P + MAIN[m], P)])
                    if g % 2 == 0:
                        if g == 0:
                            sp.wait_ge(sd_step, c * 10 + 1)
                            settle(sp)
                            sp.dma_start(bcd, s_bc[bass.ds(c, 1)].rearrange("a s b n -> a (s b) n").to_broadcast([P, 2 * NB, P])
                                         .rearrange("p (s b) n -> p s b n", s=2)).then_inc(bcd_in, 16)
                        sp.wait_ge(sd_saved, (c * 2 + g // 2) * 16 + 1)
                        settle(sp)
                        sp.wait_ge(sd_step, (c * 2 + g // 2) * 5 + 1)
                        settle(sp)
                        sp.dma_start(sd, ssm_in[bass.ds((c * 2 + g // 2) * P, P)]).then_inc(sd_in, 16)
            sp.dma_start(O["s_conv_s"][0, :, 0:KS - 2, :], I["state_conv_s"][0, :, 1:KS - 1, :]).then_inc(S["copied_dram"], 16)
            sp.dma_start(O["s_conv_a"][0, :, 0:KA - 2, :], I["state_conv_a"][0, :, 1:KA - 1, :]).then_inc(S["copied_dram"], 16)
            sp.dma_start(dec_z, s_z[:, SEQ:].rearrange("(t p) b -> p t b", p=P)).then_inc(dec_in, 16)
            def first_acts(p):
                sp.dma_start(first_buf[p], ACTS[0][:, :, p * PC:(p + 1) * PC]).then_inc(act_in[p], 16)
            sp.wait_ge(a_ready, NCH + 1)
            sp.wait_ge(stored[0], 16 * (15 + STAGED[0]) + 1)
            first_acts(0)
            sp.wait_ge(sd_step, 81)
            first_acts(1)
            sp.wait_ge(sd_saved, 16 * 16 + 1)
            first_acts(2)
            def load_gate(b, i, r):
                n = i * 2 + (b * KT + r)
                for p in range(NP):
                    sp.wait_ge(evac[p], n + (FM + 71) + 1)
                    settle(sp)
                if b:
                    sp.wait_ge(merge_done[r], i + (b - 1) * 4 + 1)
                    settle(sp)
                sp.dma_start(stage[r][:], s_g[bass.ds((i * 2 + r) * P + GATE[b] * D, P), :]).then_inc(gate_in[r], 16)
            def sp_tile(b, i, r):
                load_w(sp, out_tile(b, i, r), out_w(b)[:, :, bass.ds((i * 2 + r) * P, P)])
                if (b, r) == (0, 0) and type(i) is int:
                    sp.wait_ge(stored[1], 16 * (15 + STAGED[1]) + 1)
                    sp.dma_start(qx, s_q[:, SEQ:].rearrange("(t p) b -> p t b", p=P)).then_inc(S["qx_in"], 16)
                    load_w(sp, out_tile(0, 0, 1), out_w(0)[:, :, P:2 * P])
                    for s in range(3):
                        sp.wait_ge(stored[s], 16 * (16 + STAGED[s]) + 1)
                load_gate(b, i, r)
            head = lambda d, i: d[bass.ds(i * MD, MD), :].rearrange("(t p) n -> p t n", p=P)
            def load_qk(i, half):
                u = i + half * 4
                sp.wait_ge(S["qk_done"], u + 1)
                settle(sp)
                sp.dma_start(aq, head(s_q, i)[:, :, half * 512:half * 512 + 512]).then_inc(S["qk_in"], 16)
                sp.dma_start(ak, head(s_kt, i)).then_inc(S["qk_in"], 16)
            def load_att(i, half):
                u = i + half * 4
                sp.wait_ge(S["pv_done"], u + 1)
                settle(sp)
                sp.dma_start(avv, O["p_mem_v"][0, 0].rearrange("(a m) h d -> m a (h d)", m=P)[:, :, bass.ds(i * MD, MD)]).then_inc(S["att_in"], 16)
                sp.wait_ge(S["att_saved"], u * 16 + 1)
                settle(sp)
                sp.dma_start(amz, head(s_mz, i)[:, :, half * 512:half * 512 + 512]).then_inc(S["att_in"], 16)
            sp_tile(0, 0, 0)
            sp.wait_ge(y_turned, 33)
            load_qk(0, 0)
            load_gate(0, 0, 1)
            sp.wait_ge(S["h_copied"], 4)
            sp.dma_start(O["p_ssm"][0, 0].rearrange("h p n -> (h p) n").rearrange("(t q) n -> q t n", q=P), pso).then_inc(S["h_saved"], 16)
            sp.wait_ge(S["dec_step"], 5)
            sp.dma_start(s_y[:, SEQ:].rearrange("(t p) b -> p t b", p=P), dec_y).then_inc(S["dec_saved"], 16)
            sp.wait_ge(y_stored, 16 * 32 + 1)
            sp.wait_ge(S["dec_saved"], 16)
            load_att(0, 0)
            sp.wait_ge(S["qx_copied"], 1)
            sp.dma_start(s_qd, qrow[0:64, :]).then_inc(S["q_saved"], 16)
            sp.wait_ge(S["h_saved"], 16)
            sp.dma_start(mzd, s_mz[:, SEQ:].rearrange("(t p) b -> p t b", p=P)).then_inc(S["mzd_in"], 16)
            for half in range(2):
                with sp.Fori(1 - half, 4) as i:
                    sp_tile(half, i, 0)
                    load_qk(i, half)
                    sp_tile(half, i, 1)
                    load_att(i, half)
            for r in range(2):
                sp_tile(2, 0, r)
            sp.wait_ge(S["sam_read"], 65)
            load_v(sp, 0, 0)
            sp.wait_ge(S["att_saved"], 16 * 8 + 1)
            load_v(sp, 1, 1)
            for src, dst, x in ((trow_s[0:KS - 1, :], O["p_conv_s"][0, 0], 6), (trow_s[KS - 1:TAIL_S, :], O["s_conv_s"][0, :, KS - 2, :], 6),
                                (trow_a[0:KA - 1, :], O["p_conv_a"][0, 0], 8), (trow_a[KA - 1:TAIL_A, :], O["s_conv_a"][0, :, KA - 2, :], 8)):
                sp.wait_ge(S["tail_copied"], x)
                sp.dma_start(dst, src).then_inc(S["tail_saved"], 16)
            with sp.Fori(1, 4) as i:
                for r in range(SLOT2):
                    sp_tile(2, i, r)
            for r in range(2):
                sp_tile(3, 0, r)
            sp.wait_ge(S["act_split"], 12)
            for k in range(KT):
                sp.dma_start(wo_raw[k], I["w_o"][0, k * P:(k + 1) * P, :]).then_inc(wo_in, 16)
            with sp.Fori(1, 4) as i:
                for r in range(2):
                    sp_tile(3, i, r)
            sp.wait_ge(S["act_split"], 15)
            sp.dma_start(fw, I["final_norm_w"].rearrange("(a n) -> a n", a=1).to_broadcast([P, D])).then_inc(small_in, 16)
            def final_rows(a):
                if a < NCH:
                    return P, I["x_prompt"][0, a * P:(a + 1) * P, :], O["y_prompt"][0, a * P:(a + 1) * P, :]
                return NB, I["x_sample"][:, 0, :], O["y_sample"][:, 0, :]
            for a in range(NCH + 1 + 2):
                if a < NCH + 1:
                    if a >= 2:
                        sp.wait_ge(S["row_sum"], 2 * (a - 1))
                    sp.dma_start(xf[a % 2][0:final_rows(a)[0], :], final_rows(a)[1]).then_inc(rows_in[a % 2], 16)
                if a >= 2:
                    n, _, dst = final_rows(a - 2)
                    sp.wait_ge(S["row_out"], a - 1)
                    sp.dma_start(dst, rr[a % 2][0:n, :]).then_inc(row_saved[a % 2], 16)
            sp.wait_ge(row_saved[0], 16 * 5)
            sp.wait_ge(row_saved[1], 16 * 4)
            sp.wait_ge(S["copied_dram"], 32)
            sp.wait_ge(S["tail_saved"], 64)

        @block.gpsimd
        def _(pool):
            for s in OPENED:
                pool.sem_inc(s, 1)
            pool.memset(ident[:], 0.0).then_inc(const_ready, 1)
            pool.memset(tri[:], 1.0).then_inc(const_ready, 1)
            pool.memset(ones[:], 1.0).then_inc(const_ready, 1)
            pool.memset(epsc[:], EPS).then_inc(const_ready, 1)
            pool.memset(xp[:, 0:KS - 1], 0.0).then_inc(pads_ready, 1)
            pool.wait_ge(const_ready, 4)
            pool.affine_select(out=ident[:], in_=ident[:], compare_op=ALU.not_equal, fill=1.0, base=0,
                               pattern=[[-1, P]], channel_multiplier=1).then_inc(const_ready, 1)
            pool.affine_select(out=tri[:], in_=tri[:], compare_op=ALU.is_ge, fill=0.0, base=0,
                               pattern=[[1, P]], channel_multiplier=-1).then_inc(const_ready, 1)
            with pool.Fori(0, XT // 3) as i:
                for r in range(3):
                    split_w(pool, xbc_tile(i, r))
            for t in (dt_tile, *z_first):
                split_w(pool, t)
            with pool.Fori(0, 4) as i:
                for j in range(6):
                    split_w(pool, mixed_tile(i, j))
            with pool.Fori(0, 2) as i:
                for r in range(3):
                    split_w(pool, late_z(i, r))
            with pool.Fori(0, NCH) as c:
                for m in range(9):
                    split_w(pool, main_tile(c, m))
            for b in range(PASSES - 1):
                with pool.Fori(0, 4) as i:
                    for r in range(SLOT2):
                        split_w(pool, out_tile(b, i, r))
            def split_wo(k):
                pool.wait_ge(wo_in, 16 * KT)
                if k == 0:
                    pool.wait_ge(S["tail_saved"], 64)
                    pool.wait_ge(S["v_used"], 9)
                pool.tensor_scalar(wo_hi[k], wo_raw[k], 1.0, 0.0, ALU.mult, ALU.add).then_inc(S["wo_high"], 1)
                pool.wait_ge(S["wo_high"], k + 1)
                pool.tensor_tensor(wo_lo[k], wo_raw[k], wo_hi[k].bitcast(F32), ALU.subtract).then_inc(S["wo_split"], 1)
            for n in range(KT):
                split_w(pool, out_tile(3, n // 2, n % 2))
                if n >= 2:
                    split_wo(n - 2)
            split_wo(6)
            split_wo(7)

        @block.scalar
        def _(act):
            act.wait_ge(const_ready, 6)
            for a in range(NROW):
                n = row_tile(a)[0]
                act.wait_ge(rows_in[a % 2], 16 * (a // 2 + 1))
                if a:
                    act.wait_ge(square_done, a)
                act.activation(junk[0:n, :], xr[a % 2][0:n, :], ACT.Square, accum_out=ssq[0:n, a:a + 1]).then_inc(square_done, 1)
                act.wait_ge(square_done, a + 1)
                act.activation(root[0:n, a:a + 1], ssq[0:n, a:a + 1], ACT.Sqrt, scale=1.0 / D, bias=epsc[0:n, :]).then_inc(root_done, 1)
            act.wait_ge(pads_ready, 1)
            with act.Fori(0, XT // 3) as i:
                for r in range(3):
                    t = xbc_tile(i, r)
                    j = i * 3 + r
                    act.wait_ge(conv[KS - 1], j * 2 + 1)
                    act.wait_ge(tails_kept, j + 1)
                    read_out(act, t, xp[:, KS - 1:], ACT.Copy)
                    act.wait_ge(conv[KS - 1], (j + 1) * 2 + 1)
                    act.wait_ge(stored[r], i * 16 + 1)
                    act.activation(stage[r][:], cv[:, :], ACT.Silu).then_inc(silu_done, 1)
                    act.wait_ge(silu_done, j + 1 + 1)
                    act.dma_start(rows(s_xbc, j), stage[r][:]).then_inc(stored[r], 16)
            act.wait_ge(u_split, 2 * NROW)
            act.wait_ge(par_turned, 1)
            evacuated(act, dt_tile)
            act.activation(absv[0:HEADS, :], dtv[0:HEADS, :], ACT.Abs).then_inc(dt_abs, 1)
            act.wait_ge(dt_abs, 1)
            act.activation(expo[0:HEADS, :], absv[0:HEADS, :], ACT.Exp, scale=-1.0).then_inc(dt_exp, 1)
            act.activation(aneg[0:HEADS, :], alog[0:HEADS, :], ACT.Exp).then_inc(dt_exp, 1)
            for n in range(2):
                to_dram(act, z_first[n], Q1, s_z[n * P:(n + 1) * P, :], ACT.Silu)
            for r in range(3):
                act.wait_ge(stored[r], 16 * Q1 + 1)
            act.dma_start(bcx, s_xbc[INNER:, SEQ:].rearrange("(t p) b -> p t b", p=P)).then_inc(bcx_in, 16)
            with act.Fori(0, 4) as i:
                for j in range(6):
                    t = mixed_tile(i, j)
                    if j % 3 == 0:
                        to_dram(act, t, i * 2 + Q1 + j // 3, rows(s_z, z_of(i, j)), ACT.Silu)
                    else:
                        b = KV_BANK[j]
                        act.wait_ge(done[t[1]], t[0] + 1 + 1)
                        act.activation(kv_t[:, bass.ds(kv_of(i, j), 1), :].rearrange("p a m -> p (a m)"), pm[3 + b][:, 0:NM],
                                       ACT.Copy).then_inc(kv_evac[b], 1)
            act.wait_ge(dt_ready, 1)
            act.activation(dd[0:HEADS, 0, :], da[0:HEADS, SEQ:], ACT.Exp).then_inc(dd_ready, 1)
            with act.Fori(0, 2) as i:
                for r in range(3):
                    to_dram(act, late_z(i, r), i + (Q1 + 8 if r == 0 else Q1 + 1), rows(s_z, i * 3 + 10 + r), ACT.Silu)
            act.wait_ge(kv_saved, 48)
            act.wait_ge(cs_saved, 32)
            act.wait_ge(pre_turned, 1)
            def act_tile(c, m):
                t = main_tile(c, m)
                if m == 0:
                    act.wait_ge(tails_a_kept, c + 1)
                    read_out(act, t, cc, ACT.Copy)
                elif m == 2:
                    act.wait_ge(a_ready, c + 1)
                    read_out(act, t, zc, ACT.Silu)
                elif m == 3:
                    act.wait_ge(a_ready, c + 1 + 1)
                    act.dma_start(rows(s_a, c), stage[0][:]).then_inc(stored[0], 16)
                elif m == 4:
                    to_dram(act, t, staged(c, m), rows(s_q, c), ACT.Copy, MD ** -0.5)
                elif m == 5:
                    to_dram(act, t, staged(c, m), rows(s_mz, c), ACT.Silu)
                elif m >= 6:
                    to_dram(act, t, staged(c, m), s_g[bass.ds(c * P + (m - 6) * D, P), :], ACT.Sigmoid)
            with act.Fori(0, NCH) as c:
                for g in range(GROUPS):
                    n = c * 4 + g
                    act.wait_ge(x_turned, n + 1)
                    act.wait_ge(gy_ready, n + 1)
                    act.activation(xt, pm[0][:], ACT.Copy).then_inc(x_copied, 1)
                    act.wait_ge(args_ready, (n + 1) * 3)
                    act.activation(sm, sa, ACT.Exp).then_inc(sm_ready, 1)
                    act.wait_ge(seg_ready, (n + 1) * HG)
                    act.activation(seg, seg, ACT.Exp).then_inc(e_ready, 1)
                    act_tile(c, SEG[g][0])
                    if g % 2:
                        k = c * 2 + g // 2
                        act.wait_ge(sd_step, k * 5 + 3 + 1)
                        act.dma_start(ssm_out[bass.ds(k * P, P)], sd).then_inc(sd_saved, 16)
                    act.wait_ge(gy_ready, n + 1 + 1)
                    act.wait_ge(y_turned, n + 1)
                    act.activation(gyn, gy, ACT.Square, accum_out=ss2).then_inc(sq2_done, 1)
                    act.wait_ge(sq2_done, n + 1)
                    act.activation(rt2, ss2, ACT.Sqrt, scale=1.0 / 512, bias=epsc[:]).then_inc(rt2_done, 1)
                    act.wait_ge(rs2_step, (n + 1) * 5)
                    act.activation(gyn, gy, ACT.Copy, scale=rs2).then_inc(gyn_ready, 1)
                    for m in SEG[g][1:]:
                        act_tile(c, m)
                    act.wait_ge(y_turned, n + 1 + 1)
                    act.wait_ge(y_stored, n * 16 + 1)
                    for k in range(4):
                        act.activation(yT[:, k, :], pm[2][:, k * P:(k + 1) * P], ACT.Copy,
                                       scale=par[:, C_SN + 4 * g + k:C_SN + 4 * g + k + 1]).then_inc(y_out, 1)
                    act.wait_ge(y_out, (n + 1) * 4 + 1)
                    act.dma_start(s_y.rearrange("(t p) n -> p t n", p=P)[:, 4 * g:4 * g + 4, bass.ds(c * CH, CH)], yT).then_inc(y_stored, 16)
            def high_part(b, p):
                if b < 4:
                    act.wait_ge(act_in[p], 16 * (b + 1))
                else:
                    act.wait_ge(merge_done[0], 3 * 4 + 1)
                    act.wait_ge(merge_done[1], 3 * 4 - 1 + 1)
                    act.wait_ge(S["last_merged"], p + 1)
                if (b, p) == (3, 2):
                    act.wait_ge(S["od_ready"], 1)
                last_piece(act, b, p)
                cols = slice(p * PC, (p + 1) * PC)
                act.activation(uhi[:, :, cols], acts_buf(b, p) if b < 4 else merged[:, :, cols], ACT.Copy).then_inc(S["act_high"], 1)
            def load_acts(b):
                act.wait_ge(S["act_split"], 3 * b)
                for p in range(NP):
                    if (b, p) == (1, 2):
                        act.wait_ge(S["dec_saved"], 16)
                    c1 = SEQ if (b, p) == (3, 2) else (p + 1) * PC
                    act.dma_start(acts_buf(b, p)[:, :, 0:c1 - p * PC], ACTS[b][:, :, p * PC:c1]).then_inc(act_in[p], 16)
            high_part(0, 0)
            act.wait_ge(gy_ready, 33)
            for n in range(4):
                act.wait_ge(S["h_final"], n + 1)
                act.activation(pso[:, 4 * n:4 * n + 4, :], pm[n + (n > 1)][:, :].rearrange("p (a b) -> p a b", b=P), ACT.Copy).then_inc(S["h_copied"], 1)
                if n % 2:
                    high_part(0, n // 2 + 1)
            act.wait_ge(S["dec_step"], 3)
            act.activation(dec_rs, dec_ms, ACT.Sqrt).then_inc(S["dec_root"], 1)
            act.wait_ge(y_stored, 16 * 32 + 1)
            load_acts(1)
            def exp_scores(i, half):
                u = i + half * 4
                act.wait_ge(S["att_step"], u * 5 + 3)
                act.wait_ge(S["p_turned"], u * 2 + 1)
                for k in range(4):
                    act.activation(pt[:, k, :], pm[k // 2][:, (k % 2) * NM:(k % 2 + 1) * NM], ACT.Exp, bias=anx[:, k:k + 1],
                                   accum_out=asum[:, k:k + 1]).then_inc(S["att_exp"], 1)
            def copy_probs(i, half):
                u = i + half * 4
                for m in range(2):
                    act.wait_ge(S["p_turned"], u * 2 + m + 1 + 1)
                    act.wait_ge(S["pv_done"], u + 1)
                    act.activation(ptT[:, m, :], pm[2 + m][:], ACT.Copy).then_inc(S["p_copied"], 1)
            def save_att(i, half):
                u = i + half * 4
                act.wait_ge(S["att_ready"], (u + 1) * 2 + 1)
                act.dma_start(s_o[bass.ds(i * MD, MD), half * 512:half * 512 + 512].rearrange("(t p) n -> p t n", p=P), amz).then_inc(S["att_saved"], 16)
            def load_sample(k):
                act.wait_ge(S["sam_read"], k * 8 + 1)
                settle(act)
                act.dma_start(dk, I["cache_mem_k"][0, bass.ds(k, 1)].rearrange("c (a m) h d -> m (c a) (h d)", m=P)).then_inc(S["sam_in"], 16)
                act.dma_start(dq.rearrange("p (t n) -> p t n", n=P),
                              s_qd.rearrange("(t b) n -> b t n", b=NB)[bass.ds(k, 1)].to_broadcast([P, KT, P])).then_inc(S["sam_in"], 16)
            with act.Fori(0, 3) as i:
                exp_scores(i, 0)
                copy_probs(i, 0)
                save_att(i, 0)
            exp_scores(3, 0)
            copy_probs(3, 0)
            for p in range(NP):
                high_part(1, p)
            save_att(3, 0)
            act.wait_ge(S["q_saved"], 16)
            load_acts(2)
            with act.Fori(0, 3) as i:
                load_sample(i * 2)
                exp_scores(i, 1)
                copy_probs(i, 1)
                load_sample(i * 2 + 1)
                save_att(i, 1)
            load_sample(6)
            exp_scores(3, 1)
            copy_probs(3, 1)
            load_sample(7)
            for p in range(NP):
                high_part(2, p)
            save_att(3, 1)
            act.wait_ge(S["att_saved"], 16 * 8 + 1)
            load_acts(3)
            act.wait_ge(S["sam_step"], 2)
            act.activation(dp[0:32, :, :], pm[0][0:32, 0:NM].rearrange("p (a b) -> p a b", b=P), ACT.Exp, bias=dnx[0:32, :],
                           accum_out=dsum[0:32, :]).then_inc(S["sam_exp"], 1)
            for src, dst, n, q, x in TAILS:
                act.wait_ge(S["tail_turned"], x + 1)
                act.activation(dst[0:n, q * 512:(q + 1) * 512], pm[2 + x % 3][0:n, :], ACT.Copy).then_inc(S["tail_copied"], 1)
            with act.Fori(1, 4) as i:
                for r in range(2):
                    act.wait_ge(S["v_used"], i * 2 + (r - 1) + 1)
                    settle(act)
                    load_v(act, i * 2 + r, r)
            for b in (3, 4):
                for p in range(NP):
                    high_part(b, p)
            act.wait_ge(S["act_split"], 15)
            for a in range(NCH + 1):
                n = P if a < NCH else NB
                act.wait_ge(S["row_sum"], 2 * (a + 1))
                if a:
                    act.wait_ge(S["row_sq"], a)
                act.activation(fjunk[0:n, :], rr[a % 2][0:n, :], ACT.Square, accum_out=fss[0:n, a:a + 1]).then_inc(S["row_sq"], 1)
                act.wait_ge(S["row_sq"], a + 1)
                act.activation(frt[0:n, a:a + 1], fss[0:n, a:a + 1], ACT.Sqrt, scale=1.0 / D, bias=epsc[0:n, :]).then_inc(S["row_root"], 1)

        @block.vector
        def _(dve):
            dve.wait_ge(small_in, 80)
            def norm_rows(a):
                n = row_tile(a)[0]
                b = a % 2
                dve.wait_ge(root_done, a + 1)
                dve.reciprocal(rs[0:n, a:a + 1], root[0:n, a:a + 1]).then_inc(rs_done, 1)
                dve.wait_ge(rs_done, a + 1)
                if a >= 2:
                    dve.wait_ge(turned, 2 * (a - 1))
                w = nwb if a <= SEQ // P else mwb
                dve.scalar_tensor_tensor(xn[b][0:n, :], xr[b][0:n, :], rs[0:n, a:a + 1], w[0:n, :],
                                         ALU.mult, ALU.mult).then_inc(normed[b], 1)
            def split_rows(a):
                n, _, c0 = row_tile(a)
                hi, lo = (uhi, ulo) if a <= SEQ // P else (mhi, mlo)
                for h in range(2):
                    dve.wait_ge(turned, 2 * a + h + 1)
                    src = pm[2 * (a % 2) + h][:, :].rearrange("p (k c) -> p k c", c=P)[:, :, 0:n]
                    dve.tensor_copy(hi[:, 4 * h:4 * h + 4, c0:c0 + n], src).then_inc(u_high, 1)
                    dve.wait_ge(u_high, 2 * a + h + 1)
                    dve.tensor_tensor(lo[:, 4 * h:4 * h + 4, c0:c0 + n], src,
                                      hi[:, 4 * h:4 * h + 4, c0:c0 + n].bitcast(F32), ALU.subtract).then_inc(u_split, 1)
            for a in range(NROW + 1):
                if a < NROW:
                    norm_rows(a)
                if a:
                    split_rows(a - 1)
            dve.wait_ge(par_turned, 1)
            dve.tensor_copy(par[:, 0:P], pm[4][:, 0:P]).then_inc(par_copied, 1)
            dve.tensor_copy(par[:, P:NPAR], pm[4][:, P:NPAR]).then_inc(par_copied, 1)
            for h in range(2):
                dve.tensor_copy(hist_s[:, 12 * h:12 * h + 12, :, :],
                                acc[:, h, 0:288].rearrange("p (t b k) -> p t b k", b=NB, k=KS - 1)).then_inc(par_copied, 1)
            dve.tensor_copy(hist_a[:, :, :, :],
                            acc[:, 2, 0:128].rearrange("p (t b k) -> p t b k", b=NB, k=KA - 1)).then_inc(par_copied, 1)
            dve.wait_ge(par_copied, 5)
            def col(c, j=None):
                return par[:, c:c + 1] if j is None else par[:, bass.ds(j + c, 1)]
            with dve.Fori(0, XT // 3) as i:
                for r in range(3):
                    t = xbc_tile(i, r)
                    j = i * 3 + r
                    evacuated(dve, t)
                    hist = hist_s[:, bass.ds(j, 1), :, :].rearrange("p a b k -> p (a b) k")
                    for k in range(KS):
                        now = xp[:, SEQ + KS - 1:] if k == KS - 1 else hist[:, :, k]
                        if k == 0:
                            dve.wait_ge(silu_done, j + 1)
                            dve.tensor_scalar(cv[:, 0:SEQ], xp[:, 0:SEQ], col(C_SW, j), col(C_SB, j), ALU.mult, ALU.add).then_inc(conv[0], 1)
                            dve.tensor_scalar(cv[:, SEQ:], now, col(C_SW, j), col(C_SB, j), ALU.mult, ALU.add).then_inc(conv[0], 1)
                            continue
                        w = col(C_SW + k * XT, j)
                        dve.wait_ge(conv[k - 1], (j + 1) * 2 + 1)
                        dve.scalar_tensor_tensor(cv[:, 0:SEQ], xp[:, k:k + SEQ], w, cv[:, 0:SEQ], ALU.mult, ALU.add).then_inc(conv[k], 1)
                        dve.scalar_tensor_tensor(cv[:, SEQ:], now, w, cv[:, SEQ:], ALU.mult, ALU.add).then_inc(conv[k], 1)
                    dve.tensor_copy(tail_s[:, bass.ds(j, 1), :].rearrange("p a b -> p (a b)"), xp[:, SEQ:]).then_inc(tails_kept, 1)
            dve.wait_ge(u_split, 2 * NROW)
            dve.wait_ge(par_turned, 1)
            H = slice(0, HEADS)
            for p in range(NP):
                piece_ready(dve, dt_tile, p)
                dve.tensor_scalar(dtv[H, p * PC:(p + 1) * PC], acc[H, p, 0:PC], dtb[H, :], None, ALU.add).then_inc(evac[p], 1)
            evacuated(dve, dt_tile)
            steps = [0]
            def step(ins):
                steps[0] += 1
                ins.then_inc(dt_step, 1)
                dve.wait_ge(dt_step, steps[0])
            dve.wait_ge(dt_exp, 1)
            step(dve.tensor_scalar(zz[H, :], expo[H, :], 2.0, None, ALU.add))
            step(dve.reciprocal(zz[H, :], zz[H, :]))
            step(dve.tensor_tensor(zz[H, :], zz[H, :], expo[H, :], ALU.mult))
            step(dve.tensor_tensor(expo[H, :], zz[H, :], zz[H, :], ALU.mult))
            step(dve.tensor_scalar(csv[H, :], expo[H, :], 1.0 / (2 * LOG1P_TERMS + 1), None, ALU.mult))
            for n in range(LOG1P_TERMS - 1, 0, -1):
                step(dve.scalar_tensor_tensor(csv[H, :], csv[H, :], 1.0 / (2 * n + 1), expo[H, :], ALU.add, ALU.mult))
            step(dve.scalar_tensor_tensor(csv[H, :], csv[H, :], 1.0, zz[H, :], ALU.add, ALU.mult))
            step(dve.tensor_scalar(dtv[H, :], dtv[H, :], 0.0, None, ALU.max))
            step(dve.scalar_tensor_tensor(dtv[H, :], csv[H, :], 2.0, dtv[H, :], ALU.mult, ALU.add))
            dve.wait_ge(dt_exp, 2)
            step(dve.tensor_scalar(aneg[H, :], aneg[H, :], -1.0, None, ALU.mult))
            dve.tensor_scalar(da[H, :], dtv[H, :], aneg[H, :], None, ALU.mult).then_inc(dt_ready, 1)
            step(dve.memset(resets[H, :], 1.0))
            step(dve.memset(resets[H, 0:SEQ:CH], 0.0))
            dve.wait_ge(dt_ready, 1)
            dve.tensor_tensor_scan(csv[H, 0:SEQ], resets[H, 0:SEQ], da[H, 0:SEQ], 0.0, ALU.mult, ALU.add).then_inc(cs_ready, 1)
            dve.tensor_copy(dd[H, 1, :], dtv[H, SEQ:]).then_inc(dd_ready, 1)
            dve.wait_ge(pre_turned, 1)
            dve.tensor_copy(dt_tok[:], pm[0][:, 0:NCH * HEADS]).then_inc(pre_copied, 1)
            dve.tensor_copy(cs_tok[:], pm[0][:, NCH * HEADS:2 * NCH * HEADS]).then_inc(pre_copied, 1)
            for n in range(8):
                s, m, h = n // 4, n // 2 % 2, n % 2
                dve.wait_ge(pre_turned, n + 2)
                dve.tensor_copy(kv_tok[:, s, m, h * 512:(h + 1) * 512], pm[1 + n % 4][:]).then_inc(pre_copied, 1)
            dve.wait_ge(pre_turned, 10)
            dve.tensor_copy(bcr[0:64, :], pm[0][0:64, 0:P]).then_inc(pre_copied, 1)
            dve.wait_ge(kv_saved, 48)
            dve.wait_ge(cs_saved, 32)
            dve.wait_ge(pre_copied, 2)
            dve.memset(hT, 0.0).then_inc(h_added, 1)
            dve.memset(hb[:, 0:KA - 1], 0.0).then_inc(pads_ready, 1)
            dve.wait_ge(h_added, 1)
            dve.wait_ge(pads_ready, 2)
            dve.wait_ge(dec_in, 16 * 3)
            for e in range(2):
                part = slice(e * HD, (e + 1) * HD)
                dve.tensor_copy(dec_skip[part, :], dskip[part, e::2]).then_inc(dec_ready, 1)
            dve.tensor_tensor(dec_xdt, dec_x, dec_dd[:, :, 1, :], ALU.mult).then_inc(dec_ready, 1)
            dve.wait_ge(dec_ready, 3)
            def sample_step(c, g):
                k = c * 2 + g // 2
                flat = lambda v: v[:, bass.ds(k, 1), :].rearrange("p a b -> p (a b)")
                decay = dec_dd[:, bass.ds(k, 1), 0, :].rearrange("p a b -> p (a b)")
                if g == 0:
                    dve.wait_ge(bcd_in, (c + 1) * 16)
                dve.wait_ge(sd_in, (k + 1) * 16)
                dve.wait_ge(sd_step, k * 5 + 1)
                dve.tensor_tensor(sd2, bcd[:, 0, :, :], bcast(flat(dec_xdt), P), ALU.mult).then_inc(sd_step, 1)
                dve.tensor_tensor(sd, sd, bcast(decay, P), ALU.mult).then_inc(sd_step, 1)
                dve.wait_ge(sd_step, k * 5 + 2 + 1)
                dve.tensor_tensor(sd, sd, sd2, ALU.add).then_inc(sd_step, 1)
            def sample_output(c, g):
                k = c * 2 + g // 2
                dve.wait_ge(sd_step, k * 5 + 3 + 1)
                dve.tensor_tensor(sd2, sd, bcd[:, 1, :, :], ALU.mult).then_inc(sd_step, 1)
                dve.wait_ge(sd_step, k * 5 + 4 + 1)
                dve.tensor_reduce(dec_y[:, bass.ds(k, 1), :].rearrange("p a b -> p (a b)"), sd2, AX.X, ALU.add).then_inc(sd_step, 1)
            def dve_tile(c, m):
                t = main_tile(c, m)
                if m == 1:
                    evacuated(dve, main_tile(c, 0))
                    for p in range(NP):
                        piece_ready(dve, t, p)
                        lo, hi = p * PC, (p + 1) * PC
                        dve.wait_ge(a_conv, c * 2 * KA + 1)
                        dve.wait_ge(tails_a_kept, c + 1)
                        dve.tensor_tensor(hb[:, KA - 1 + lo:KA - 1 + hi], acc[:, p, 0:PC], cc[:, lo:hi], ALU.mult).then_inc(evac[p], 1)
                    evacuated(dve, t)
                    dve.tensor_copy(tail_a[:, bass.ds(c, 1), :].rearrange("p a b -> p (a b)"), hb[:, SEQ:]).then_inc(tails_a_kept, 1)
                    hist = hist_a[:, bass.ds(c, 1), :, :].rearrange("p a b k -> p (a b) k")
                    dve.wait_ge(a_ready, c + 1)
                    for k in range(KA):
                        now = hb[:, SEQ + KA - 1:] if k == KA - 1 else hist[:, :, k]
                        w = col(C_AW + k * KT, c)
                        if k == 0:
                            dve.tensor_scalar(av[:, 0:SEQ], hb[:, 0:SEQ], w, None, ALU.mult).then_inc(a_conv, 1)
                            dve.tensor_scalar(av[:, SEQ:], now, w, None, ALU.mult).then_inc(a_conv, 1)
                            continue
                        dve.wait_ge(a_conv, (c * KA + k) * 2 + 1)
                        dve.scalar_tensor_tensor(av[:, 0:SEQ], hb[:, k:k + SEQ], w, av[:, 0:SEQ], ALU.mult, ALU.add).then_inc(a_conv, 1)
                        dve.scalar_tensor_tensor(av[:, SEQ:], now, w, av[:, SEQ:], ALU.mult, ALU.add).then_inc(a_conv, 1)
                elif m == 3:
                    evacuated(dve, main_tile(c, 2))
                    for p in range(NP):
                        piece_ready(dve, t, p)
                        part = zc[:, p * PC:(p + 1) * PC]
                        dve.tensor_tensor(part, part, acc[:, p, 0:PC], ALU.mult).then_inc(evac[p], 1)
                    evacuated(dve, t)
                    dve.wait_ge(a_conv, (c + 1) * 2 * KA + 1)
                    dve.wait_ge(stored[0], staged(c, m) * 16 + 1)
                    dve.tensor_tensor(stage[0][:], zc, av, ALU.mult).then_inc(a_ready, 1)
            with dve.Fori(0, NCH) as c:
                for g in range(GROUPS):
                    n, b, u = c * 4 + g, g % 2, c * 2 + g // 2
                    dve.wait_ge(group_in[b], (u + 1) * 64)
                    last = csb[b][:, :, CH - 1]
                    cs = cs_tok[:, bass.ds(c * HEADS + g * HG, HG)]
                    dve.wait_ge(sm_ready, n + 1)
                    dve.tensor_tensor(sa[:, 0, :], last, cs, ALU.subtract).then_inc(args_ready, 1)
                    dve.tensor_copy(sa[:, 1, :], cs).then_inc(args_ready, 1)
                    dve.tensor_copy(sa[:, 2, :], last).then_inc(args_ready, 1)
                    dve.wait_ge(m_ready, n + 1)
                    for h in range(HG):
                        dve.tensor_scalar(seg[:, h, :], csb[b][:, h, :], cs_tok[:, bass.ds(c * HEADS + g * HG + h, 1)], 0.0,
                                          ALU.subtract, ALU.min).then_inc(seg_ready, 1)
                    dve.wait_ge(b_ready, n + 1)
                    group_before(dve, c, g)
                    dve.tensor_copy(bt, pm[1][:, 0:P]).then_inc(bt_ready, 1)
                    dve.tensor_tensor(scm, pm[1][:, P:2 * P], tri[:], ALU.mult).then_inc(sc_ready, 1)
                    dve.wait_ge(x_copied, n + 1)
                    dve.tensor_tensor(heads(xdt), heads(xt), bcast(dt_tok[:, bass.ds(c * HEADS + g * HG, HG)], HD), ALU.mult).then_inc(xdt_ready, 1)
                    dve.wait_ge(sm_ready, n + 1 + 1)
                    dve.wait_ge(xdt_ready, n + 1)
                    dve.tensor_tensor(heads(xdd), heads(xdt), bcast(sm[:, 0, :], HD), ALU.mult).then_inc(xdd_ready, 1)
                    dve.wait_ge(e_ready, n + 1)
                    dve.wait_ge(sc_ready, n + 1)
                    dve.tensor_tensor(mm_, seg, scm.unsqueeze(1).to_broadcast([P, HG, CH]), ALU.mult).then_inc(m_ready, 1)
                    dve_tile(c, SEG[g][0])
                    dve.wait_ge(gyn_ready, n + 1)
                    dve.tensor_tensor(heads(gy), heads(xt), bcast(dskip[:, g * HG:(g + 1) * HG], HD), ALU.mult).then_inc(y_step, 1)
                    dve.wait_ge(summed[b], u + 1 + 1)
                    dve.tensor_tensor(heads(yv), heads(pm[3][:]), bcast(sm[:, 1, :], HD), ALU.mult).then_inc(y_step, 1)
                    dve.tensor_tensor(heads(hT[:, g, :]), heads(hT[:, g, :]), bcast(sm[:, 2, :], HD), ALU.mult).then_inc(h_scaled, 1)
                    dve.wait_ge(y_step, n * 4 + 2)
                    dve.tensor_tensor(yv, yv, pm[4][:], ALU.add).then_inc(y_step, 1)
                    dve.wait_ge(h_scaled, n + 1)
                    dve.tensor_tensor(hT[:, g, :], hT[:, g, :], pm[0][:], ALU.add).then_inc(h_added, 1)
                    dve.wait_ge(y_step, n * 4 + 3)
                    dve.tensor_tensor(yv, yv, gy, ALU.add).then_inc(y_step, 1)
                    dve.wait_ge(y_step, n * 4 + 4)
                    dve.wait_ge(z_turned, n + 1)
                    dve.tensor_tensor(gy, yv, pm[2][:], ALU.mult).then_inc(gy_ready, 1)
                    dve.wait_ge(rt2_done, n + 1)
                    dve.wait_ge(gyn_ready, n + 1)
                    dve.tensor_scalar(var2, ss2, 1.0 / 512, EPS, ALU.mult, ALU.add).then_inc(rs2_step, 1)
                    dve.reciprocal(rs2, rt2).then_inc(rs2_step, 1)
                    dve.wait_ge(rs2_step, n * 5 + 2)
                    dve.scalar_tensor_tensor(nw2, rs2, var2, rs2, ALU.mult, ALU.mult).then_inc(rs2_step, 1)
                    dve.wait_ge(rs2_step, n * 5 + 3)
                    dve.tensor_scalar(nw2, nw2, -0.5, 1.5, ALU.mult, ALU.add).then_inc(rs2_step, 1)
                    dve.wait_ge(rs2_step, n * 5 + 4)
                    dve.tensor_tensor(rs2, rs2, nw2, ALU.mult).then_inc(rs2_step, 1)
                    if g % 2 == 0:
                        sample_step(c, g)
                    if g == 1:
                        sample_output(c, 0)
                    for m in SEG[g][1:]:
                        dve_tile(c, m)
                    if g == 2:
                        sample_output(c, 2)
            dve.wait_ge(dec_in, 16 * 4)
            dve.tensor_tensor(dec_sq, dec_x, bcast(dec_skip, NB), ALU.mult).then_inc(dec_ready, 1)
            dve.wait_ge(dec_ready, 4)
            dve.wait_ge(sd_step, 81)
            dve.tensor_tensor(dec_y, dec_y, dec_sq, ALU.add).then_inc(dec_ready, 1)
            dve.wait_ge(dec_ready, 5)
            dve.tensor_tensor(dec_y, dec_y, dec_z, ALU.mult).then_inc(dec_ready, 1)
            dve.wait_ge(dec_ready, 6)
            dve.tensor_tensor(dec_sq, dec_y, dec_y, ALU.mult).then_inc(S["dec_sq_done"], 1)
            def low_part(b, p):
                dve.wait_ge(S["act_high"], b * NP + p + 1)
                cols = slice(p * PC, (p + 1) * PC)
                dve.tensor_tensor(ulo[:, :, cols], acts_buf(b, p) if b < 4 else merged[:, :, cols],
                                  uhi[:, :, cols].bitcast(F32), ALU.subtract).then_inc(S["act_split"], 1)
            for p in range(NP):
                low_part(0, p)
            dve.wait_ge(S["dec_summed"], 1)
            dve.wait_ge(S["qx_turned"], 1)
            dve.tensor_reduce(dec_ms, pm[2][:, 0:P].rearrange("p (g t b) -> p g b t", g=GROUPS, b=NB), AX.X, ALU.add).then_inc(S["dec_step"], 1)
            dve.wait_ge(S["dec_step"], 1)
            dve.tensor_scalar(dec_ms, dec_ms, 1.0 / 512, EPS, ALU.mult, ALU.add).then_inc(S["dec_step"], 1)
            dve.wait_ge(S["dec_step"], 2)
            dve.tensor_scalar(dec_nw, dec_ms, -0.5, None, ALU.mult).then_inc(S["dec_step"], 1)
            dve.wait_ge(S["dec_root"], 1)
            dve.wait_ge(S["dec_step"], 3)
            dve.reciprocal(dec_rs, dec_rs).then_inc(S["dec_step"], 1)
            dve.wait_ge(S["dec_step"], 4)
            step(dve.tensor_tensor(dec_nw, dec_nw, dec_rs, ALU.mult))
            step(dve.tensor_tensor(dec_nw, dec_nw, dec_rs, ALU.mult))
            step(dve.tensor_scalar(dec_nw, dec_nw, 1.5, None, ALU.add))
            step(dve.tensor_tensor(dec_rs, dec_rs, dec_nw, ALU.mult))
            for g in range(GROUPS):
                step(dve.tensor_tensor(dec_y[:, 4 * g:4 * g + 4, :], dec_y[:, 4 * g:4 * g + 4, :],
                                       dec_rs[:, g:g + 1, :].to_broadcast([P, 4, NB]), ALU.mult))
            dve.tensor_tensor(dec_y, dec_y, bcast(par[:, C_SN:C_SN + ZT], NB), ALU.mult).then_inc(S["dec_step"], 1)
            for r in range(3):
                dve.wait_ge(stored[r], 16 * (16 + STAGED[r]) + 1)
            dve.tensor_copy(qrow[0:64, :], pm[2][0:64, P:2 * P]).then_inc(S["qx_copied"], 1)
            dve.wait_ge(y_stored, 16 * 32 + 1)
            def merge(b, i, r, last=False):
                t = out_tile(b, i, r)
                it = bass.ds(i * 2 + r, 1)
                dve.wait_ge(gate_in[r], (i + (b * 4 + 1)) * 16)
                for p in range(NP):
                    piece_ready(dve, t, p)
                    cols = slice(p * PC, (p + 1) * PC)
                    at = merged[:, it, cols].rearrange("p a n -> p (a n)")
                    if b == 0 and p == 0:
                        dve.wait_ge(S["h_saved"], 16)
                    dve.tensor_tensor(stage[r][:, cols] if b else at, stage[r][:, cols], acc[:, p, 0:PC], ALU.mult).then_inc(evac[p], 1)
                    if b == 3 and last:
                        dve.wait_ge(evac[p], t[2] + 1 + 1)
                        dve.tensor_tensor(at, at, stage[r][:, cols], ALU.add).then_inc(S["last_merged"], 1)
                    if last and (b, p) != (2, NP - 1):
                        low_part(b + 1, p)
                if b and not (b == 3 and last):
                    evacuated(dve, t)
                    whole = merged[:, it, :].rearrange("p a n -> p (a n)")
                    dve.tensor_tensor(whole, whole, stage[r][:], ALU.add).then_inc(merge_done[r], 1)
            def softmax(i, half):
                u = i + half * 4
                dve.wait_ge(S["qk_done"], u + 1 + 1)
                dve.wait_ge(S["att_exp"], u * 4 + 1)
                for k in range(2):
                    dve.tensor_reduce(amx[:, 2 * k:2 * k + 2], pm[k][:, :].rearrange("p (a b) -> p a b", b=NM), AX.X, ALU.max).then_inc(S["att_step"], 1)
                dve.wait_ge(S["att_step"], u * 5 + 2)
                dve.tensor_scalar(anx, amx, -1.0, None, ALU.mult).then_inc(S["att_step"], 1)
                dve.wait_ge(S["att_exp"], (u + 1) * 4 + 1)
                dve.reciprocal(arec, asum).then_inc(S["att_step"], 1)
                dve.wait_ge(S["att_step"], u * 5 + 4)
                dve.tensor_tensor(pt, pt, bcast(arec, NM), ALU.mult).then_inc(S["att_step"], 1)
            def gate_att(i, half):
                u = i + half * 4
                dve.wait_ge(S["att_in"], (u + 1) * 32)
                dve.wait_ge(S["pv_done"], u + 1 + 1)
                for d in range(2):
                    dve.tensor_tensor(amz[:, d, :], amz[:, d, :], pm[4 - d][:], ALU.mult).then_inc(S["att_ready"], 1)
            def sample_scores(k):
                dve.wait_ge(S["sam_in"], (k + 1) * 32)
                dve.wait_ge(S["sam_kept"], k + 1)
                for a in range(2):
                    for h in range(MH):
                        ks = dk[:, a, h * MD:(h + 1) * MD]
                        dve.tensor_tensor_reduce(ks, ks, dq[:, h * MD:(h + 1) * MD], 1.0, 0.0, ALU.mult, ALU.add,
                                                 sde[:, a, h:h + 1]).then_inc(S["sam_read"], 1)
                dve.wait_ge(S["sam_read"], (k + 1) * 8 + 1)
                dve.tensor_copy(sds[:, :, bass.ds(k, 1), :].rearrange("p a b h -> p a (b h)"), sde).then_inc(S["sam_kept"], 1)
            with dve.Fori(0, 3) as i:
                softmax(i, 0)
                merge(0, i, 0)
                merge(0, i, 1)
                gate_att(i, 0)
            softmax(3, 0)
            merge(0, 3, 0)
            merge(0, 3, 1, last=True)
            gate_att(3, 0)
            with dve.Fori(0, 3) as i:
                softmax(i, 1)
                merge(1, i, 0)
                sample_scores(i * 2)
                merge(1, i, 1)
                gate_att(i, 1)
                sample_scores(i * 2 + 1)
            softmax(3, 1)
            merge(1, 3, 0)
            sample_scores(6)
            merge(1, 3, 1, last=True)
            gate_att(3, 1)
            sample_scores(7)
            merge(2, 0, 0)
            dve.wait_ge(S["sds_turned"], 1)
            dve.tensor_reduce(dmx[0:32, :], pm[0][0:32, 0:NM], AX.X, ALU.max).then_inc(S["sam_step"], 1)
            dve.wait_ge(S["sam_step"], 1)
            dve.tensor_scalar(dnx[0:32, :], dmx[0:32, :], -1.0, None, ALU.mult).then_inc(S["sam_step"], 1)
            dve.wait_ge(S["sam_exp"], 1)
            dve.reciprocal(drec[0:32, :], dsum[0:32, :]).then_inc(S["sam_step"], 1)
            dve.wait_ge(S["sam_step"], 3)
            dve.tensor_scalar(dp[0:32, :, :], dp[0:32, :, :], drec[0:32, :], None, ALU.mult).then_inc(S["sam_step"], 1)
            merge(2, 0, 1)
            dve.wait_ge(S["dp_turned"], 1)
            dve.tensor_copy(dpT, pm[1][:, 0:64].rearrange("p (a b) -> p a b", a=2)).then_inc(S["dp_copied"], 1)
            dve.wait_ge(S["dp_copied"], 1)
            def values_times(i, b, k):
                dve.wait_ge(v_in[b], (i + 1) * 32)
                for a in range(2):
                    for h in range(MH):
                        part = vv[b][a][:, h * MD:(h + 1) * MD]
                        dve.tensor_scalar(part, part, dpT[:, a, bass.ds(k * 4 + h, 1)], None, ALU.mult).then_inc(S["v_scaled"], 1)
                dve.wait_ge(S["v_scaled"], k * 9 + 8)
                dve.tensor_tensor(vv[b][0], vv[b][0], vv[b][1], ALU.add).then_inc(S["v_scaled"], 1)
            with dve.Fori(1, 3) as i:
                for r in range(2):
                    values_times(i - 1, r, i * 2 + (r - 2))
                    merge(2, i, r)
            values_times(2, 0, 4)
            values_times(2, 1, 5)
            merge(2, 3, 0)
            values_times(3, 0, 6)
            values_times(3, 1, 7)
            merge(2, 3, 1, last=True)
            dve.wait_ge(S["v_used"], 9)
            dve.wait_ge(S["mzd_in"], 16)
            dve.wait_ge(S["act_split"], 9)
            dve.tensor_tensor(piece_buf[2][:, :, PC - NB:PC], mzd, pm[0][:, 0:64].rearrange("p (b t) -> p t b", t=KT), ALU.mult).then_inc(S["od_ready"], 1)
            low_part(3, 2)
            with dve.Fori(0, 3) as i:
                merge(3, i, 0)
                merge(3, i, 1)
            merge(3, 3, 0)
            merge(3, 3, 1, last=True)
            dve.wait_ge(S["act_split"], 15)
            dve.wait_ge(small_in, 96)
            def final_out(a):
                n = P if a < NCH else NB
                q = slice(a, a + 1)
                dve.wait_ge(S["row_root"], a + 1)
                dve.tensor_scalar(fvar[0:n, q], fss[0:n, q], 1.0 / D, EPS, ALU.mult, ALU.add).then_inc(S["row_step"], 1)
                dve.reciprocal(frs[0:n, q], frt[0:n, q]).then_inc(S["row_step"], 1)
                dve.wait_ge(S["row_step"], a * 5 + 2)
                dve.scalar_tensor_tensor(fnw[0:n, q], frs[0:n, q], fvar[0:n, q], frs[0:n, q], ALU.mult, ALU.mult).then_inc(S["row_step"], 1)
                dve.wait_ge(S["row_step"], a * 5 + 3)
                dve.tensor_scalar(fnw[0:n, q], fnw[0:n, q], -0.5, 1.5, ALU.mult, ALU.add).then_inc(S["row_step"], 1)
                dve.wait_ge(S["row_step"], a * 5 + 4)
                dve.tensor_tensor(frs[0:n, q], frs[0:n, q], fnw[0:n, q], ALU.mult).then_inc(S["row_step"], 1)
                dve.wait_ge(S["row_step"], a * 5 + 5)
                v = rr[a % 2][0:n, :]
                dve.scalar_tensor_tensor(v, v, frs[0:n, q], fw[0:n, :], ALU.mult, ALU.mult).then_inc(S["row_out"], 1)
            for a in range(NCH + 2):
                if a < NCH + 1:
                    n = P if a < NCH else NB
                    dve.wait_ge(rows_in[a % 2], 16 * (a // 2 + 1 + (NROW + 1 - a % 2) // 2))
                    if a >= 2:
                        dve.wait_ge(row_saved[a % 2], 16 * (a // 2))
                    for h in range(2):
                        dve.wait_ge(S["row_done"], 2 * a + h + 1)
                        half = slice(h * 512, (h + 1) * 512)
                        dve.tensor_tensor(rr[a % 2][0:n, half], xf[a % 2][0:n, half], pm[2 * (a % 2) + h][0:n, :], ALU.add).then_inc(S["row_sum"], 1)
                if a:
                    final_out(a - 1)

        @block.tensor
        def _(pe):
            pe.wait_ge(const_ready, 6)
            pe.wait_ge(par_in, 96)
            pe.transpose(pm[4][:, 0:P], par_rows[:, 0, :], ident[:])
            n1 = NPAR - P
            pe.transpose(pm[4][:, P:NPAR], par_rows[0:n1, 1, :], ident[0:n1, 0:n1])
            pe.wait_ge(hist_in, 32)
            for t in range(XT):
                pe.transpose(acc[:, t // 12, (t % 12) * 24:(t % 12) * 24 + 24], hrow_s[0:24, t * P:(t + 1) * P], ident[0:24, 0:24])
            for t in range(KT):
                tr = pe.transpose(acc[:, 2, t * 16:t * 16 + 16], hrow_a[0:16, t * P:(t + 1) * P], ident[0:16, 0:16])
            tr.then_inc(par_turned, 1)
            for a in range(NROW):
                n = row_tile(a)[0]
                pe.wait_ge(normed[a % 2], a // 2 + 1)
                for h in range(2):
                    if a >= 2:
                        pe.wait_ge(u_split, 2 * (a - 2) + h + 1)
                    for k in range(4):
                        tr = pe.transpose(pm[2 * (a % 2) + h][:, k * P:k * P + n], xn[a % 2][0:n, (4 * h + k) * P:(4 * h + k + 1) * P],
                                          ident[0:n, 0:n])
                    tr.then_inc(turned, 1)
            pe.wait_ge(u_split, 2 * NROW)
            pe.wait_ge(par_copied, 5)
            with pe.Fori(0, XT // 3) as i:
                for r in range(3):
                    dense(pe, xbc_tile(i, r))
            dense(pe, dt_tile)
            for n in range(2):
                dense(pe, z_first[n])
            with pe.Fori(0, 4) as i:
                for j in range(6):
                    t = mixed_tile(i, j)
                    if j % 3 == 0:
                        dense(pe, t)
                        continue
                    b = KV_BANK[j]
                    pe.wait_ge(w_split[t[1]], t[0] + 1 + 1)
                    pe.wait_ge(kv_evac[b], i * 2 + j // 3 + 1)
                    product(pe, t, pm[3 + b][:, 0:NM], mhi, mlo, 0, NM).then_inc(done[t[1]], 1)
            pe.wait_ge(cs_ready, 1)
            for n, v in enumerate((dtv, csv)):
                for c in range(NCH):
                    tr = pe.transpose(pm[0][:, (n * NCH + c) * HEADS:(n * NCH + c + 1) * HEADS], v[0:HEADS, c * CH:(c + 1) * CH],
                                      ident[0:HEADS, 0:HEADS])
            tr.then_inc(pre_turned, 1)
            for b in range(2):
                pe.wait_ge(kv_evac[b], KT + 1)
            for n in range(8):
                s, m, h = n // 4, n // 2 % 2, n % 2
                if n >= 4:
                    pe.wait_ge(pre_copied, n - 1)
                for k in range(4):
                    tr = pe.transpose(pm[1 + n % 4][:, k * P:(k + 1) * P], kv_t[:, s * KT + h * 4 + k, m * P:(m + 1) * P], ident[:])
                tr.then_inc(pre_turned, 1)
            pe.wait_ge(bcx_in, 16)
            pe.wait_ge(pre_copied, 2)
            pe.transpose(pm[0][0:64, 0:P], bcx.rearrange("p t b -> p (t b)"), ident[:]).then_inc(pre_turned, 1)
            with pe.Fori(0, 2) as i:
                for r in range(3):
                    dense(pe, late_z(i, r))
            pe.wait_ge(pre_copied, 2)
            pe.wait_ge(pre_copied, 11)
            with pe.Fori(0, NCH) as c:
                for g in range(GROUPS):
                    n, b, u = c * 4 + g, g % 2, c * 2 + g // 2
                    bg, cg = xg[b][:, 4, :], xg[b][:, 5, :]
                    pe.wait_ge(group_in[b], (u + 1) * 64)
                    pe.wait_ge(h_added, n + 1)
                    for k in range(4):
                        tr = pe.transpose(pm[0][:, k * P:(k + 1) * P], xg[b][:, k, :], ident[:])
                    tr.then_inc(x_turned, 1)
                    pe.transpose(pm[1][:, 0:P], bg, ident[:])
                    pe.matmul(pm[1][:, P:2 * P], bg, cg, start=True, stop=True).then_inc(b_ready, 1)
                    dense(pe, main_tile(c, SEG[g][0]))
                    pe.wait_ge(y_out, n * 4 + 1)
                    for k in range(4):
                        tr = pe.transpose(pm[2][:, k * P:(k + 1) * P], zg[b][:, k, :], ident[:])
                    tr.then_inc(z_turned, 1)
                    pe.wait_ge(m_ready, n + 1 + 1)
                    pe.wait_ge(xdd_ready, n + 1)
                    pe.wait_ge(bt_ready, n + 1)
                    pe.matmul(pm[3][:], cg, hT[:, g, :], start=True, stop=True)
                    for h in range(HG):
                        pe.matmul(pm[4][:, h * HD:(h + 1) * HD], mm_[:, h, :], xdt[:, h * HD:(h + 1) * HD], start=True, stop=True)
                    pe.matmul(pm[0][:], bt, xdd, start=True, stop=True).then_inc(summed[b], 1)
                    for m in SEG[g][1:]:
                        dense(pe, main_tile(c, m))
                    pe.wait_ge(gyn_ready, n + 1 + 1)
                    for k in range(4):
                        tr = pe.transpose(pm[2][:, k * P:(k + 1) * P], gyn[:, k * P:(k + 1) * P], ident[:])
                    tr.then_inc(y_turned, 1)
            pe.wait_ge(h_added, 33)
            pe.wait_ge(gyn_ready, 33)
            for n in range(4):
                for k in range(4):
                    tr = pe.transpose(pm[n + (n > 1)][:, k * P:(k + 1) * P], hT[:, n, k * P:(k + 1) * P], ident[:])
                tr.then_inc(S["h_final"], 1)
            pe.wait_ge(y_out, 129)
            pe.wait_ge(S["dec_sq_done"], 1)
            pe.matmul(pm[2][:, 0:P], ones[:], dec_sq.rearrange("p t b -> p (t b)"), start=True, stop=True).then_inc(S["dec_summed"], 1)
            pe.wait_ge(S["qx_in"], 16)
            pe.transpose(pm[2][0:64, P:2 * P], qx.rearrange("p t b -> p (t b)"), ident[:]).then_inc(S["qx_turned"], 1)
            pe.wait_ge(S["h_copied"], 2)
            def out_dense(b, i, r):
                dense(pe, out_tile(b, i, r), acts=(S["act_split"], b * NP))
            def scores(i, half):
                u = i + half * 4
                pe.wait_ge(S["qk_in"], (u + 1) * 32)
                pe.wait_ge(S["att_exp"], u * 4 + 1)
                for k in range(4):
                    for d in range(2):
                        mm = pe.matmul(pm[k // 2][:, (k % 2) * NM:(k % 2 + 1) * NM], aq[:, d, k * P:(k + 1) * P], ak[:, d, :],
                                       start=d == 0, stop=d == 1)
                mm.then_inc(S["qk_done"], 1)
            def turn_probs(i, half):
                u = i + half * 4
                pe.wait_ge(S["att_step"], u * 5 + 5)
                pe.wait_ge(S["att_ready"], u * 2 + 1)
                for m in range(2):
                    for k in range(4):
                        tr = pe.transpose(pm[2 + m][:, k * P:(k + 1) * P], pt[:, k, m * P:(m + 1) * P], ident[:])
                    tr.then_inc(S["p_turned"], 1)
            def values(i, half):
                u = i + half * 4
                pe.wait_ge(S["att_in"], (u + 1) * 32)
                pe.wait_ge(S["p_copied"], (u + 1) * 2 + 1)
                for d in range(2):
                    for m in range(2):
                        mm = pe.matmul(pm[4 - d][:], avv[:, m, d * P:(d + 1) * P], ptT[:, m, :], start=m == 0, stop=m == 1)
                mm.then_inc(S["pv_done"], 1)
            for half in range(2):
                with pe.Fori(0, 4) as i:
                    scores(i, half)
                    out_dense(half, i, 0)
                    turn_probs(i, half)
                    out_dense(half, i, 1)
                    values(i, half)
            def turn_tails(tails):
                for src, dst, n, q, x in tails:
                    if x >= 3:
                        pe.wait_ge(S["tail_copied"], x - 2)
                    for k in range(4):
                        tr = pe.transpose(pm[2 + x % 3][0:n, k * P:(k + 1) * P], src[:, q * 4 + k, :], ident[:])
                    tr.then_inc(S["tail_turned"], 1)
            out_dense(2, 0, 0)
            pe.wait_ge(S["att_ready"], 17)
            pe.wait_ge(S["sam_kept"], 9)
            for m in range(2):
                tr = pe.transpose(pm[0][0:32, m * P:(m + 1) * P], sds[:, m, :, :].rearrange("p b h -> p (b h)"), ident[:])
            tr.then_inc(S["sds_turned"], 1)
            turn_tails(TAILS[0:3])
            out_dense(2, 0, 1)
            pe.wait_ge(S["sam_step"], 4)
            for m in range(2):
                tr = pe.transpose(pm[1][:, m * 32:(m + 1) * 32], dp[0:32, m, :], ident[0:32, 0:32])
            tr.then_inc(S["dp_turned"], 1)
            turn_tails(TAILS[3:])
            def sample_values(k, b):
                pe.wait_ge(S["v_scaled"], (k + 1) * 9)
                for t in range(KT):
                    mm = pe.matmul(pm[0][:, bass.ds(k * KT + t, 1)], vv[b][0][:, t * P:(t + 1) * P], ones[:, 0:1], start=True, stop=True)
                mm.then_inc(S["v_used"], 1)
            with pe.Fori(1, 3) as i:
                for r in range(SLOT2):
                    out_dense(2, i, r)
                    sample_values(i * 2 + (r - 2), r)
            for r in range(SLOT2):
                out_dense(2, 3, r)
                sample_values(4 + 2 * r, 0)
                sample_values(5 + 2 * r, 1)
            with pe.Fori(0, 4) as i:
                for r in range(SLOT2):
                    out_dense(3, i, r)
            def final_sums(a, q, n=P):
                for h in range(2):
                    half = slice(h * 512, (h + 1) * 512)
                    for k in range(KT):
                        for s, (x, w) in enumerate(((uhi, wo_hi[k]), (uhi, wo_lo[k]), (ulo, wo_hi[k]))):
                            mm = pe.matmul(pm[2 * q + h][0:n, :], x[:, k, bass.ds(a * P, n)], w[:, half], start=k == 0 and s == 0,
                                           stop=k == KT - 1 and s == 2)
                    mm.then_inc(S["row_done"], 1)
            pe.wait_ge(S["wo_split"], KT)
            for a in range(NCH + 1):
                n = P if a < NCH else NB
                pe.wait_ge(S["act_split"], 13 + (a * P + n - 1) // PC)
                if a >= 2:
                    pe.wait_ge(S["row_sum"], 2 * (a - 1))
                final_sums(a, a % 2, n)



INPUTS = ["x_prompt", "x_sample", "mem_prompt", "state_conv_a", "state_conv_s", "state_ssm", "cache_mem_k",
          "cache_mem_v", "norm_w", "w_in", "conv_a_w", "w_a_out", "conv_s_w", "conv_s_b", "dt_bias", "a_log",
          "d_skip", "ssm_norm_w", "w_s_out", "mem_norm_w", "w_mem_kv", "w_m_out", "w_o", "final_norm_w"]
OUTPUTS = {"y_prompt": (1, SEQ, D), "y_sample": (NB, 1, D), "p_conv_a": (1, 1, KA - 1, D),
           "p_conv_s": (1, 1, KS - 1, XBC), "p_ssm": (1, 1, HEADS, HD, NS), "p_mem_k": (1, 1, NM, MH, MD),
           "p_mem_v": (1, 1, NM, MH, MD), "s_conv_a": (1, NB, KA - 1, D), "s_conv_s": (1, NB, KS - 1, XBC),
           "s_ssm": (1, NB, HEADS, HD, NS)}


def kernel(**inputs):
    import numpy as np
    import concourse.bacc as bacc
    from concourse.bass_utils import run_bass_kernel_spmd

    nc = bacc.Bacc("TRN2", target_bir_lowering=False, num_devices=1)
    arrays, ins, outs = {}, {}, {}
    for name in INPUTS:
        a = np.ascontiguousarray(inputs[name])
        arrays[f"in_{name}"] = a
        ins[name] = nc.dram_tensor(f"in_{name}", a.shape, F32, kind="ExternalInput").ap()
    for name, shape in OUTPUTS.items():
        outs[name] = nc.dram_tensor(f"out_{name}", shape, F32, kind="ExternalOutput").ap()
    build(nc, ins, outs)
    r = run_bass_kernel_spmd(nc, [arrays], core_ids=[0])
    return tuple(r.results[0][f"out_{name}"] for name in OUTPUTS)
```

```python
from contextlib import ExitStack

import concourse.bass as bass
from concourse import mybir

ALU = mybir.AluOpType
ACT = mybir.ActivationFunctionType
AX = mybir.AxisListType
F32 = mybir.dt.float32
F32R = mybir.dt.float32r

P = 128
D = 1024
SEQ = 1024
NB = 8
T = SEQ + NB
KT = D // P
NP = 3
PC = T // NP
INNER = 2 * D
HEADS, HD = 32, 64
GROUPS, HG = 4, 8
NS = 128
XBC = INNER + 2 * GROUPS * NS
KS, KA = 4, 3
CH = 128
NCH = SEQ // CH
NM, MH, MD = 256, 4, 256
EPS = 1e-6
ZT, XT = INNER // P, XBC // P
O_CB, O_CC, O_CH, O_CZ, O_SZ = 0, D, 2 * D, 3 * D, 4 * D
O_XBC = O_SZ + INNER
O_DT = O_XBC + XBC
O_MQ = O_DT + HEADS
O_MZ = O_MQ + D
O_G = O_MZ + D
C_SW, C_SB, C_NW = 0, KS * XT, KS * XT + XT
C_AW = C_NW + KT
C_SN = C_AW + KA * KT
C_MN = C_SN + ZT
NPAR = C_MN + KT
TAIL_S, TAIL_A = KS - 1 + NB, KA - 1 + NB
OPEN = 1
LOG1P_TERMS = 9


def build(nc, I, O):
    dram = lambda n, s: nc.dram_tensor(n, s, F32, kind="Internal").ap()
    s_xbc = dram("s_xbc", (XBC, T))
    s_z = dram("s_z", (INNER, T))
    s_q = dram("s_q", (D, T))
    s_mz = dram("s_mz", (D, T))
    s_g = dram("s_g", (3 * D, T))
    s_a = dram("s_a", (D, T))
    s_y = dram("s_y", (INNER, T))
    s_o = dram("s_o", (D, T))
    s_cs = dram("s_cs", (HEADS, SEQ))
    s_dd = dram("s_dd", (HEADS, 2, NB))
    s_bc = dram("s_bc", (NCH, 2, NB, P))
    s_kt = dram("s_kt", (D, NM))
    s_qd = dram("s_qd", (KT * NB, P))

    w_in = I["w_in"][0].rearrange("(k p) n -> p k n", p=P)
    w_kv = I["w_mem_kv"][0].rearrange("(k p) n -> p k n", p=P)

    with ExitStack() as ctx:
        def sb(name, shape, dt=F32):
            return ctx.enter_context(nc.sbuf_tensor(name, shape, dt))

        def sem(name):
            return ctx.enter_context(nc.semaphore(name))

        acc = ctx.enter_context(nc.psum_tensor("acc", [P, NP, 512], F32))
        pm = [ctx.enter_context(nc.psum_tensor(f"pm{i}", [P, 512], F32)) for i in range(5)]
        uhi = sb("uhi", [P, KT, T], F32R)
        ulo = sb("ulo", [P, KT, T], F32R)
        raw, whi, wlo = [], [], []
        for r in range(3):
            if r == 2:
                with nc.sbuf_tensor("slot2", [P, 3 * KT * P], F32) as slot2:
                    pass
                with nc.sbuf_tensor("wo_lo_b", [P, 3, D], F32R) as wo_lo_b:
                    pass
            raw.append(sb(f"raw{r}", [P, KT, P]))
            whi.append(sb(f"whi{r}", [P, KT, P], F32R))
            wlo.append(sb(f"wlo{r}", [P, KT, P], F32R))
        stage = [sb(f"stage{r}", [P, T]) for r in range(3)]
        ident = sb("ident", [P, P])
        tri = sb("tri", [P, P])
        ones = sb("ones", [P, P])
        epsc = sb("epsc", [P, 1])
        par = sb("par", [P, NPAR])
        hist_s = sb("hist_s", [P, XT, NB, KS - 1])
        hist_a = sb("hist_a", [P, KT, NB, KA - 1])
        tail_s = sb("tail_s", [P, XT, TAIL_S])
        tail_a = sb("tail_a", [P, KT, TAIL_A])
        cs_tok = sb("cs_tok", [P, NCH * HEADS])
        dt_tok = sb("dt_tok", [P, NCH * HEADS])
        dskip = sb("dskip", [P, HEADS])
        ARENA = 22096
        with nc.sbuf_tensor("mhi", [P, KT, NM], F32R) as mhi, nc.sbuf_tensor("mlo", [P, KT, NM], F32R) as mlo:
            pass
        WO_A, WO_GAP = KT * T, 2 * KT * PC - 5 * D
        with nc.sbuf_tensor("below", [P, WO_A], F32), nc.sbuf_tensor("wo_hi_a", [P, 5, D], F32R) as wo_hi_a, \
                nc.sbuf_tensor("wo_lo_a", [P, 5, D], F32R) as wo_lo_a, nc.sbuf_tensor("between", [P, WO_GAP], F32), \
                nc.sbuf_tensor("wo_hi_b", [P, 3, D], F32R) as wo_hi_b:
            pass
        arena = sb("arena", [P, ARENA])

        M0 = 2 * KT * NM
        cursor = [M0]

        def view(*shape, at=None):
            n = 1
            for s in shape:
                n *= s
            if at is None:
                at = cursor[0]
            cursor[0] = at + n
            assert cursor[0] <= ARENA, (cursor[0], shape)
            v = arena[:, at:at + n]
            if len(shape) == 2:
                v = v.rearrange("p (a b) -> p a b", b=shape[1])
            if len(shape) == 3:
                v = v.rearrange("p (a b c) -> p a b c", b=shape[1], c=shape[2])
            return v

        w_loaded = [sem(f"w_loaded{r}") for r in range(3)]
        w_high = [sem(f"w_high{r}") for r in range(3)]
        w_split = [sem(f"w_split{r}") for r in range(3)]
        ready = [sem(f"ready{p}") for p in range(NP - 1)]
        done = [sem(f"done{r}") for r in range(3)]
        evac = [sem(f"evac{p}") for p in range(NP)]
        stored = [sem(f"stored{r}") for r in range(3)]

        const_ready = sem("const_ready")

        paced = sem("paced")

        def settle(e):
            e.sem_inc(paced, 1)

        def load_w(sp, t, src):
            sp.wait_ge(w_split[t[1]], t[0] + OPEN)
            settle(sp)
            sp.dma_start(raw[t[1]][:], src).then_inc(w_loaded[t[1]], 16)

        def split_w(pool, t):
            q, r = t[0], t[1]
            pool.wait_ge(w_loaded[r], (q + 1) * 16)
            pool.wait_ge(done[r], q + OPEN)
            settle(pool)
            pool.tensor_scalar(whi[r][:], raw[r][:], 1.0, 0.0, ALU.mult, ALU.add).then_inc(w_high[r], 1)
            pool.wait_ge(w_high[r], q + 1)
            pool.tensor_tensor(wlo[r][:], raw[r][:], whi[r][:].bitcast(F32), ALU.subtract).then_inc(w_split[r], 1)

        def product(pe, t, out, hi, lo, c0, n):
            r = t[1]
            for k in range(KT):
                for s, (w, a) in enumerate(((whi, hi), (wlo, hi), (whi, lo))):
                    mm = pe.matmul(out, w[r][:, k, :], a[:, k, c0:c0 + n], start=k == 0 and s == 0, stop=k == KT - 1 and s == 2)
            return mm

        def dense(pe, t, acts=None):
            q, r, n = t
            pe.wait_ge(w_split[r], q + 1 + OPEN)
            for p in range(NP):
                pe.wait_ge(evac[p], n + OPEN)
                if acts:
                    pe.wait_ge(acts[0], acts[1] + p + 1)
                product(pe, t, acc[:, p, 0:PC], uhi, ulo, p * PC, PC).then_inc(done[r] if p == NP - 1 else ready[p], 1)

        def piece_ready(e, t, p):
            if p == NP - 1:
                e.wait_ge(done[t[1]], t[0] + 1 + OPEN)
            else:
                e.wait_ge(ready[p], t[2] + 1)

        def read_out(act, t, out, func, scale=1.0):
            for p in range(NP):
                piece_ready(act, t, p)
                act.activation(out[:, p * PC:(p + 1) * PC], acc[:, p, 0:PC], func, scale=scale).then_inc(evac[p], 1)

        def evacuated(e, t):
            for p in range(NP):
                e.wait_ge(evac[p], t[2] + 1 + OPEN)

        def to_dram(act, t, use, dst, func, scale=1.0):
            r = t[1]
            act.wait_ge(stored[r], use * 16 + OPEN)
            read_out(act, t, stage[r], func, scale)
            evacuated(act, t)
            act.dma_start(dst, stage[r][:]).then_inc(stored[r], 16)

        xbc_tile = lambda i, r: (i, r, i * 3 + r)
        Q1 = XT // 3
        dt_tile, z_first = (Q1, 0, XT), [(Q1, 1, XT + 1), (Q1, 2, XT + 2)]
        mixed_tile = lambda i, j: (i * 2 + Q1 + 1 + j // 3, j % 3, None if j % 3 else i * 2 + XT + 3 + j // 3)
        late_z = lambda i, r: (i + Q1 + 9, r, i * 3 + XT + 11 + r)
        QM, FM = Q1 + 11, XT + 1 + ZT
        main_tile = lambda c, m: (c * 3 + QM + m // 3, m % 3, c * 9 + FM + m)

        xbc_src = lambda j: w_in[:, :, bass.ds(j * P + O_XBC, P)]
        z_src = lambda j: w_in[:, :, bass.ds(j * P + O_SZ, P)]
        kv_src = lambda j: w_kv[:, :, bass.ds(j * P, P)]
        MAIN = (O_CC, O_CH, O_CZ, O_CB, O_MQ, O_MZ, O_G, O_G + D, O_G + 2 * D)
        rows = lambda d, j: d[bass.ds(j * P, P), :]

        rows_in = [sem(f"rows_in{b}") for b in range(2)]
        par_in, hist_in, small_in = sem("par_in"), sem("hist_in"), sem("small_in")
        square_done, root_done, rs_done = sem("square_done"), sem("root_done"), sem("rs_done")
        normed = [sem(f"normed{b}") for b in range(2)]
        turned, u_high, u_split = sem("turned"), sem("u_high"), sem("u_split")
        par_turned, par_copied, norm_in = sem("par_turned"), sem("par_copied"), sem("norm_in")
        PROMPT_ROWS = SEQ // P + 1
        xr = [view(D), view(D)]
        xn = [view(D), view(D)]
        nwb, mwb = view(D), view(D)
        junk = view(D)
        par_rows = view(2, P)
        hrow_s, hrow_a = view(XBC), view(D)
        ssq, root, rs = view(16), view(16), view(16)
        NROW = SEQ // P + 1 + NM // P
        def row_tile(a):
            if a < SEQ // P:
                return P, I["x_prompt"][0, a * P:(a + 1) * P, :], a * P
            if a == SEQ // P:
                return NB, I["x_sample"][:, 0, :], SEQ
            a -= SEQ // P + 1
            return P, I["mem_prompt"][0, a * P:(a + 1) * P, :], a * P
        def turned_rows(a, h):
            n, _, c0 = row_tile(a)
            hi, lo = (uhi, ulo) if a < PROMPT_ROWS else (mhi, mlo)
            src = pm[2 * (a % 2) + h][:, :].rearrange("p (k c) -> p k c", c=P)[:, :, 0:n]
            return src, hi[:, 4 * h:4 * h + 4, c0:c0 + n], lo[:, 4 * h:4 * h + 4, c0:c0 + n]
        xp = view(T + KS - 1, at=M0 + 15900)
        cv = view(T)
        dtb, alog = view(1), view(1)
        conv = [sem(f"conv{k}") for k in range(KS)]
        silu_done, tails_kept, pads_ready = sem("silu_done"), sem("tails_kept"), sem("pads_ready")

        kv_t = view(2 * KT, NM, at=M0)
        kv_tok = view(2, 2, D)
        kv_saved = sem("kv_saved")
        kv_evac = [sem(f"kv_evac{b}") for b in range(2)]
        KV_BANK = {1: 0, 2: 1, 4: 0, 5: 1}
        z_of = lambda i, j: i * 2 + 2 + j // 3
        kv_of = lambda i, j: i * 4 + (j - 1 if j < 3 else j - 2)
        pre_turned, pre_copied = sem("pre_turned"), sem("pre_copied")
        DT0 = M0 + 8192
        dtv = view(T, at=DT0)
        absv, expo, zz, csv = view(T), view(T), view(T), view(T)
        da, resets = absv, zz
        aneg, dd = view(1), view(2, NB)
        dt_step, dt_abs, dt_exp = sem("dt_step"), sem("dt_abs"), sem("dt_exp")
        dt_ready, cs_ready, dd_exp, dd_ready, cs_saved = sem("dt_ready"), sem("cs_ready"), sem("dd_exp"), sem("dd_ready"), sem("cs_saved")
        bcx, bcr = view(8, NB), view(P)
        bcx_in, bc_saved, dec_in = (sem(n) for n in ("bcx_in", "bc_saved", "dec_in"))
        SEG = ((0, 1), (2, 3), (4, 5), (6, 7, 8))
        xg = [view(6, CH, at=0 if b == 0 else None) for b in range(2)]
        zg = [view(4, CH) for b in range(2)]
        csb = [view(HG, CH) for b in range(2)]
        xt, bt, scm = view(512), view(CH), view(CH)
        xdt, xdd = view(512), view(512)
        seg, mm_ = view(HG, CH), view(HG, CH)
        yv, gy, gyn, yT = view(512), view(512), view(512), view(4, CH)
        sa, sm = view(3, HG), view(3, HG)
        ss2, rt2, rs2, nw2, var2 = view(1), view(1), view(1), view(1), view(1)
        dec_x, dec_z, dec_xdt, dec_y, dec_sq = (view(ZT, NB) for _ in range(5))
        dec_dd = view(ZT, 2, NB)
        dec_skip = view(ZT)
        dec_ms, dec_rs, dec_nw = view(GROUPS, NB), view(GROUPS, NB), view(GROUPS, NB)
        hT = view(GROUPS, 512)
        FIRST = cursor[0]
        cc, zc, av = view(T), view(T), view(T)
        hb = view(T + KA - 1)
        bcd = view(2, NB, P)
        sd, sd2 = view(NB, P), view(NB, P)
        bcd_in, sd_in, sd_step, sd_saved, dec_ready = sem("bcd_in"), sem("sd_in"), sem("sd_step"), sem("sd_saved"), sem("dec_ready")
        ssm_in = I["state_ssm"][0].rearrange("b h p n -> (h p) b n")
        ssm_out = O["s_ssm"][0].rearrange("b h p n -> (h p) b n")
        group_in = [sem(f"group_in{b}") for b in range(2)]
        summed = [sem(f"summed{b}") for b in range(2)]
        x_turned, b_ready, z_turned, x_copied = sem("x_turned"), sem("b_ready"), sem("z_turned"), sem("x_copied")
        args_ready, sm_ready, seg_ready, e_ready = sem("args_ready"), sem("sm_ready"), sem("seg_ready"), sem("e_ready")
        bt_ready, sc_ready, xdt_ready, xdd_ready, m_ready = (sem(n) for n in ("bt_ready", "sc_ready", "xdt_ready", "xdd_ready", "m_ready"))
        y_step, gy_ready, h_scaled, h_added = sem("y_step"), sem("gy_ready"), sem("h_scaled"), sem("h_added")
        sq2_done, rt2_done, rs2_step, gyn_ready = sem("sq2_done"), sem("rt2_done"), sem("rs2_step"), sem("gyn_ready")
        y_turned, y_out, y_stored = sem("y_turned"), sem("y_out"), sem("y_stored")
        tails_a_kept, a_conv, a_ready = (
            sem(n) for n in ("tails_a_kept", "a_conv", "a_ready"))
        STAGED = (Q1 + 10, Q1 + 3, Q1 + 3)
        def staged(c, m):
            return c * 2 + STAGED[m % 3] + (m >= 6)
        def bcast(v, n):
            return v.unsqueeze(2).to_broadcast([P, v.shape[1], n])
        def heads(v):
            return v.rearrange("p (h d) -> p h d", h=HG)
        def group_before(e, c, g):
            if g % 2:
                e.wait_ge(summed[0], c * 2 + g // 2 + 1 + OPEN)
            else:
                e.wait_ge(summed[1], c * 2 + g // 2 + OPEN)
        PASSES = 4
        SLOT2 = 2
        def out_tile(b, i, r):
            n = i * 2 + (b * KT + r)
            return i + (QM + 24 + b * 4), r, n + (FM + 72)
        OUT_W = [I[w][0].rearrange("(k p) n -> p k n", p=P) for w in ("w_a_out", "w_s_out", "w_m_out")]
        out_w = lambda b: (OUT_W[0], OUT_W[1][:, 0:KT], OUT_W[1][:, KT:], OUT_W[2])[b]
        GATE = (0, 1, 1, 2)
        tiles_of = lambda d: d.rearrange("(t p) n -> p t n", p=P)
        ACTS = (tiles_of(s_a), tiles_of(s_y)[:, 0:KT], tiles_of(s_y)[:, KT:], tiles_of(s_o))
        merged = view(KT, T, at=0)
        A0 = cursor[0]
        aq, ak, avv, amz = view(2, 512), view(2, NM), view(2, MD), view(2, 512)
        pt, ptT = view(4, NM), view(2, 512)
        piece_at = cursor[0]
        piece_buf = [view(KT, PC) for _ in range(2)]
        piece_buf.append(slot2[:, 0:KT * PC].rearrange("p (k n) -> p k n", n=PC))
        K0 = cursor[0]
        dk = view(2, D)
        dq = view(D)
        qx = view(KT, NB)
        first_buf = [view(KT, PC, at=FIRST + p * KT * PC) for p in range(NP)]
        acts_buf = lambda b, p: first_buf[p] if b == 0 else piece_buf[p]
        pso = view(16, P, at=6144)
        trow_s, trow_a = view(XBC, at=A0), view(D)
        vv = [(dk[:, 0, :], dk[:, 1, :]), (view(D), dq)]
        wo_raw = [view(D, at=piece_at + k * D) for k in range(5)] + [slot2[:, k * D:(k + 1) * D] for k in range(3)]
        wo_lo = [wo_lo_a[:, k, :] for k in range(5)] + [wo_lo_b[:, k, :] for k in range(3)]
        wo_hi = [wo_hi_a[:, k, :] for k in range(5)] + [wo_hi_b[:, k, :] for k in range(3)]
        assert (A0, piece_at, K0) == (WO_A, WO_A + 5 * D, WO_A + 10 * D + WO_GAP)
        xf = [view(D, at=0), view(D)]
        rr = [view(D), view(D)]
        fw, fjunk = view(D), view(D)
        small_at = [0]
        def small(*shape):
            n = 1
            for x in shape:
                n *= x
            v = stage[2][:, small_at[0]:small_at[0] + n]
            small_at[0] += n
            assert small_at[0] <= T
            return v.rearrange("p (a b) -> p a b", b=shape[-1]) if len(shape) == 2 else (
                v if len(shape) == 1 else v.rearrange("p (a b c) -> p a b c", b=shape[1], c=shape[2]))
        qrow = small(P)
        amx, anx, asum, arec = small(4), small(4), small(4), small(4)
        sde = small(2, 4)
        sds = small(2, NB, 4)
        dmx, dnx, dsum, drec = small(1), small(1), small(1), small(1)
        dp = small(2, P)
        dpT = small(2, NB * 4)
        mzd = small(KT, NB)
        fss, frt, frs, fvar, fnw = small(9), small(9), small(9), small(9), small(9)
        SEMS = """h_final h_copied h_saved dec_sq_done dec_summed dec_root dec_step dec_saved qx_in qx_turned qx_copied q_saved
            act_high act_split qk_in att_in qk_done att_step att_exp p_turned p_copied pv_done
            att_ready att_saved sam_in sam_read sam_kept sds_turned sam_step sam_exp dp_turned dp_copied
            v_scaled v_used od_ready tail_turned tail_copied tail_saved copied_dram
            last_merged wo_high wo_split row_done row_sum row_sq row_root row_step row_out""".split()
        S = {n: sem(n) for n in SEMS}
        act_in = [sem(f"act_in{p}") for p in range(NP)]
        v_in = [sem(f"v_in{b}") for b in range(2)]
        wo_in = sem("wo_in")
        gate_in = [sem(f"gate_in{r}") for r in range(2)]
        merge_done = [sem(f"merge_done{r}") for r in range(2)]
        row_saved = [sem(f"row_saved{r}") for r in range(2)]
        TAILS = [(tail_s, trow_s, TAIL_S, n, n) for n in range(6)] + [(tail_a, trow_a, TAIL_A, n, n + 6) for n in range(2)]
        def load_v(e, k, b):
            src = I["cache_mem_v"][0, bass.ds(k, 1)].rearrange("c (a m) h d -> a m (c h d)", m=P)
            for a in range(2):
                e.dma_start(vv[b][a], src[a]).then_inc(v_in[b], 16)
        def last_piece(e, b, p):
            if p < NP - 1:
                e.wait_ge(ready[p], FM + 72 + b * KT)
            elif b == 0:
                e.wait_ge(done[2], QM + 24 + OPEN)
            else:
                e.wait_ge(done[1], QM + 24 + b * 4 + OPEN)
        OPENED = (*kv_evac, *w_split, *done, *evac, *conv, tails_kept, *stored, silu_done, *summed, gy_ready, y_turned, y_stored, a_ready,
                  tails_a_kept, a_conv, sm_ready, m_ready, gyn_ready, sd_step, sd_saved, y_out, *merge_done,
                  *(S[n] for n in ("att_saved", "att_exp", "p_turned", "pv_done", "qk_done", "sam_read", "sam_kept", "v_used",
                                   "att_ready", "p_copied")))


        block = ctx.enter_context(nc.Block())

        @block.sync
        def _(sp):
            def load_rows(a):
                n, src, _ = row_tile(a)
                if a >= 2:
                    sp.wait_ge(normed[a % 2], a // 2)
                sp.dma_start(xr[a % 2][0:n, :], src).then_inc(rows_in[a % 2], 16)
            load_rows(0)
            sp.dma_start(nwb, I["norm_w"].to_broadcast([P, D])).then_inc(norm_in, 16)
            load_rows(1)
            load_w(sp, xbc_tile(0, 0), xbc_src(0))
            for a in range(2, 4):
                load_rows(a)
            for v, (r0, n) in {"conv_s_w": (C_SW, KS * XT), "conv_s_b": (C_SB, XT), "norm_w": (C_NW, KT)}.items():
                src = I[v].rearrange("a (t p) -> (a t) p", p=P) if v != "conv_s_w" else I[v][0].rearrange("k (t p) -> (k t) p", p=P)
                sp.dma_start(par_rows[r0:r0 + n, 0, :], src).then_inc(par_in, 16)
            for v, (r0, n) in {"conv_a_w": (0, KA * KT), "ssm_norm_w": (KA * KT, ZT), "mem_norm_w": (KA * KT + ZT, KT)}.items():
                src = I[v].rearrange("a (t p) -> (a t) p", p=P) if v != "conv_a_w" else I[v][0].rearrange("k (t p) -> (k t) p", p=P)
                sp.dma_start(par_rows[r0:r0 + n, 1, :], src).then_inc(par_in, 16)
            for a in range(4, 6):
                load_rows(a)
            sp.dma_start(hrow_s[0:NB * (KS - 1), :], I["state_conv_s"][0].rearrange("b k c -> (b k) c")).then_inc(hist_in, 16)
            sp.dma_start(hrow_a[0:NB * (KA - 1), :], I["state_conv_a"][0].rearrange("b k c -> (b k) c")).then_inc(hist_in, 16)
            for a in range(6, PROMPT_ROWS):
                load_rows(a)
            for r in range(1, 3):
                load_w(sp, xbc_tile(0, r), xbc_src(r))
            with sp.Fori(1, XT // 3) as i:
                for r in range(3):
                    load_w(sp, xbc_tile(i, r), xbc_src(i * 3 + r))
            sp.dma_start(mwb, I["mem_norm_w"].to_broadcast([P, D])).then_inc(small_in, 16)
            sp.dma_start(dskip[:], I["d_skip"].to_broadcast([P, HEADS])).then_inc(small_in, 16)
            sp.dma_start(dtb[0:HEADS, :], I["dt_bias"].rearrange("a h -> h a")).then_inc(small_in, 16)
            sp.dma_start(alog[0:HEADS, :], I["a_log"].rearrange("a h -> h a")).then_inc(small_in, 16)
            for a in range(PROMPT_ROWS, NROW):
                load_rows(a)
            load_w(sp, dt_tile, w_in[:, :, O_DT:O_DT + P])
            for n in range(2):
                load_w(sp, z_first[n], w_in[:, :, O_SZ + n * P:O_SZ + (n + 1) * P])
            with sp.Fori(0, 4) as i:
                for j in range(6):
                    load_w(sp, mixed_tile(i, j), kv_src(kv_of(i, j)) if j % 3 else z_src(z_of(i, j)))
            with sp.Fori(0, 2) as i:
                for r in range(3):
                    load_w(sp, late_z(i, r), z_src(i * 3 + 10 + r))
            sp.wait_ge(cs_ready, 1)
            sp.dma_start(s_cs, csv[0:HEADS, 0:SEQ]).then_inc(cs_saved, 16)
            sp.wait_ge(dd_ready, 2)
            sp.dma_start(s_dd, dd[0:HEADS, :, :]).then_inc(cs_saved, 16)
            for b in range(2):
                sp.wait_ge(kv_evac[b], KT + OPEN)
            sp.dma_start(s_kt.rearrange("(t p) m -> p t m", p=P), kv_t[:, 0:KT, :]).then_inc(kv_saved, 16)
            sp.wait_ge(pre_copied, 10)
            for s, dst in enumerate(("p_mem_k", "p_mem_v")):
                sp.dma_start(O[dst][0, 0].rearrange("(a m) h d -> m a (h d)", m=P), kv_tok[:, s, :, :]).then_inc(kv_saved, 16)
            sp.wait_ge(pre_copied, 11)
            for c in range(NCH):
                for s in range(2):
                    r0 = (s * GROUPS + c // 2) * NB
                    sp.dma_start(s_bc[c, s], bcr[r0:r0 + NB, :]).then_inc(bc_saved, 16)
            xbc_t = s_xbc.rearrange("(t p) n -> p t n", p=P)
            z_t = s_z.rearrange("(t p) n -> p t n", p=P)
            def sample_inputs():
                sp.dma_start(dec_x, s_xbc[0:INNER, SEQ:].rearrange("(t p) b -> p t b", p=P)).then_inc(dec_in, 16)
                for e in range(2):
                    part = slice(e * HD, (e + 1) * HD)
                    sp.dma_start(dec_dd[part, :, :, :], s_dd[e::2].unsqueeze(0).to_broadcast([HD, ZT, 2, NB])).then_inc(dec_in, 16)
            sp.wait_ge(kv_saved, 48)
            sp.wait_ge(cs_saved, 32)
            sample_inputs()
            sp.wait_ge(bc_saved, 16 * 16)
            for r, n in enumerate((Q1 + 8, Q1 + 1, Q1 + 1)):
                sp.wait_ge(stored[r], 16 * n + OPEN)
            with sp.Fori(0, NCH) as c:
                for g in range(GROUPS):
                    b, u = g % 2, c * 2 + g // 2
                    sp.wait_ge(summed[b], u + OPEN)
                    settle(sp)
                    if g == 2:
                        for r in range(3):
                            sp.wait_ge(stored[r], 16 * STAGED[r] + OPEN)
                    tok = bass.ds(c * CH, CH)
                    sp.dma_start(xg[b][:, 0:4, :], xbc_t[:, 4 * g:4 * g + 4, tok]).then_inc(group_in[b], 16)
                    sp.dma_start(xg[b][:, 4:6, :], xbc_t[:, ZT + g::GROUPS, tok]).then_inc(group_in[b], 16)
                    sp.dma_start(zg[b], z_t[:, 4 * g:4 * g + 4, tok]).then_inc(group_in[b], 16)
                    sp.dma_start(csb[b], s_cs[g * HG:(g + 1) * HG, tok].unsqueeze(0).to_broadcast([P, HG, CH])).then_inc(group_in[b], 16)
                    for m in SEG[g]:
                        load_w(sp, main_tile(c, m), w_in[:, :, bass.ds(c * P + MAIN[m], P)])
                    if g % 2 == 0:
                        if g == 0:
                            sp.wait_ge(sd_step, c * 10 + OPEN)
                            settle(sp)
                            sp.dma_start(bcd, s_bc[bass.ds(c, 1)].rearrange("a s b n -> a (s b) n").to_broadcast([P, 2 * NB, P])
                                         .rearrange("p (s b) n -> p s b n", s=2)).then_inc(bcd_in, 16)
                        sp.wait_ge(sd_saved, (c * 2 + g // 2) * 16 + OPEN)
                        settle(sp)
                        sp.wait_ge(sd_step, (c * 2 + g // 2) * 5 + OPEN)
                        settle(sp)
                        sp.dma_start(sd, ssm_in[bass.ds((c * 2 + g // 2) * P, P)]).then_inc(sd_in, 16)
            sp.dma_start(O["s_conv_s"][0, :, 0:KS - 2, :], I["state_conv_s"][0, :, 1:KS - 1, :]).then_inc(S["copied_dram"], 16)
            sp.dma_start(O["s_conv_a"][0, :, 0:KA - 2, :], I["state_conv_a"][0, :, 1:KA - 1, :]).then_inc(S["copied_dram"], 16)
            sp.dma_start(dec_z, s_z[:, SEQ:].rearrange("(t p) b -> p t b", p=P)).then_inc(dec_in, 16)
            def first_acts(p):
                sp.dma_start(first_buf[p], ACTS[0][:, :, p * PC:(p + 1) * PC]).then_inc(act_in[p], 16)
            sp.wait_ge(a_ready, NCH + OPEN)
            sp.wait_ge(stored[0], 16 * (15 + STAGED[0]) + OPEN)
            first_acts(0)
            sp.wait_ge(sd_step, 80 + OPEN)
            first_acts(1)
            sp.wait_ge(sd_saved, 16 * 16 + OPEN)
            first_acts(2)
            def load_gate(b, i, r):
                n = i * 2 + (b * KT + r)
                for p in range(NP):
                    sp.wait_ge(evac[p], n + (FM + 71) + OPEN)
                    settle(sp)
                if b:
                    sp.wait_ge(merge_done[r], i + (b - 1) * 4 + OPEN)
                    settle(sp)
                sp.dma_start(stage[r][:], s_g[bass.ds((i * 2 + r) * P + GATE[b] * D, P), :]).then_inc(gate_in[r], 16)
            def sp_tile(b, i, r):
                load_w(sp, out_tile(b, i, r), out_w(b)[:, :, bass.ds((i * 2 + r) * P, P)])
                load_gate(b, i, r)
            head = lambda d, i: d[bass.ds(i * MD, MD), :].rearrange("(t p) n -> p t n", p=P)
            def load_qk(i, half):
                u = i + half * 4
                sp.wait_ge(S["qk_done"], u + OPEN)
                settle(sp)
                sp.dma_start(aq, head(s_q, i)[:, :, half * 512:half * 512 + 512]).then_inc(S["qk_in"], 16)
                sp.dma_start(ak, head(s_kt, i)).then_inc(S["qk_in"], 16)
            def load_att(i, half):
                u = i + half * 4
                sp.wait_ge(S["pv_done"], u + OPEN)
                settle(sp)
                sp.dma_start(avv, O["p_mem_v"][0, 0].rearrange("(a m) h d -> m a (h d)", m=P)[:, :, bass.ds(i * MD, MD)]).then_inc(S["att_in"], 16)
                sp.wait_ge(S["att_saved"], u * 16 + OPEN)
                settle(sp)
                sp.dma_start(amz, head(s_mz, i)[:, :, half * 512:half * 512 + 512]).then_inc(S["att_in"], 16)
            for r in range(2):
                load_w(sp, out_tile(0, 0, r), out_w(0)[:, :, r * P:(r + 1) * P])
            sp.wait_ge(stored[1], 16 * (15 + STAGED[1]) + OPEN)
            sp.dma_start(qx, s_q[:, SEQ:].rearrange("(t p) b -> p t b", p=P)).then_inc(S["qx_in"], 16)
            sp.wait_ge(y_turned, 32 + OPEN)
            load_qk(0, 0)
            for r in range(3):
                sp.wait_ge(stored[r], 16 * (16 + STAGED[r]) + OPEN)
            for r in range(2):
                load_gate(0, 0, r)
            sp.wait_ge(S["h_copied"], 4)
            sp.dma_start(O["p_ssm"][0, 0].rearrange("h p n -> (h p) n").rearrange("(t q) n -> q t n", q=P), pso).then_inc(S["h_saved"], 16)
            sp.wait_ge(S["dec_step"], 5)
            sp.dma_start(s_y[:, SEQ:].rearrange("(t p) b -> p t b", p=P), dec_y).then_inc(S["dec_saved"], 16)
            sp.wait_ge(y_stored, 16 * 32 + OPEN)
            sp.wait_ge(S["dec_saved"], 16)
            load_att(0, 0)
            sp.wait_ge(S["act_split"], 3)
            sp.dma_start(piece_buf[2], ACTS[1][:, :, 2 * PC:]).then_inc(act_in[2], 16)
            sp.wait_ge(S["qx_copied"], 1)
            sp.dma_start(s_qd, qrow[0:64, :]).then_inc(S["q_saved"], 16)
            sp.wait_ge(S["h_saved"], 16)
            sp.dma_start(mzd, s_mz[:, SEQ:].rearrange("(t p) b -> p t b", p=P)).then_inc(S["qx_in"], 16)
            for half in range(2):
                with sp.Fori(1 - half, 4) as i:
                    sp_tile(half, i, 0)
                    load_qk(i, half)
                    sp_tile(half, i, 1)
                    load_att(i, half)
            for n in range(3):
                sp_tile(2, n // 2, n % 2)
            sp.wait_ge(S["sam_read"], 64 + OPEN)
            load_v(sp, 0, 0)
            sp.wait_ge(S["att_saved"], 16 * 8 + OPEN)
            load_v(sp, 1, 1)
            sp_tile(2, 1, 1)
            with sp.Fori(2, 4) as i:
                for r in range(SLOT2):
                    sp_tile(2, i, r)
            for n in range(4):
                sp_tile(3, n // 2, n % 2)
            sp.wait_ge(S["act_split"], 12)
            for k in range(KT):
                sp.dma_start(wo_raw[k], I["w_o"][0, k * P:(k + 1) * P, :]).then_inc(wo_in, 16)
            for n in range(4, KT):
                sp_tile(3, n // 2, n % 2)
            sp.wait_ge(S["act_split"], 15)
            sp.dma_start(fw, I["final_norm_w"].rearrange("(a n) -> a n", a=1).to_broadcast([P, D])).then_inc(small_in, 16)
            def final_rows(a):
                if a < NCH:
                    return P, I["x_prompt"][0, a * P:(a + 1) * P, :], O["y_prompt"][0, a * P:(a + 1) * P, :]
                return NB, I["x_sample"][:, 0, :], O["y_sample"][:, 0, :]
            for a in range(NCH + 1 + 2):
                if a < NCH + 1:
                    if a >= 2:
                        sp.wait_ge(S["row_sum"], 2 * (a - 1))
                    sp.dma_start(xf[a % 2][0:final_rows(a)[0], :], final_rows(a)[1]).then_inc(rows_in[a % 2], 16)
                if a >= 2:
                    n, _, dst = final_rows(a - 2)
                    sp.wait_ge(S["row_out"], a - 1)
                    sp.dma_start(dst, rr[a % 2][0:n, :]).then_inc(row_saved[a % 2], 16)
            sp.wait_ge(row_saved[0], 16 * 5)
            sp.wait_ge(row_saved[1], 16 * 4)
            sp.wait_ge(S["copied_dram"], 32)
            sp.wait_ge(S["tail_saved"], 64)

        @block.gpsimd
        def _(pool):
            for s in OPENED:
                pool.sem_inc(s, OPEN)
            pool.memset(ident[:], 0.0).then_inc(const_ready, 1)
            pool.memset(tri[:], 1.0).then_inc(const_ready, 1)
            pool.memset(ones[:], 1.0).then_inc(const_ready, 1)
            pool.memset(epsc[:], EPS).then_inc(const_ready, 1)
            pool.memset(xp[:, 0:KS - 1], 0.0).then_inc(pads_ready, 1)
            pool.wait_ge(const_ready, 4)
            pool.affine_select(out=ident[:], in_=ident[:], compare_op=ALU.not_equal, fill=1.0, base=0,
                               pattern=[[-1, P]], channel_multiplier=1).then_inc(const_ready, 1)
            pool.affine_select(out=tri[:], in_=tri[:], compare_op=ALU.is_ge, fill=0.0, base=0,
                               pattern=[[1, P]], channel_multiplier=-1).then_inc(const_ready, 1)
            with pool.Fori(0, XT // 3) as i:
                for r in range(3):
                    split_w(pool, xbc_tile(i, r))
            for t in (dt_tile, *z_first):
                split_w(pool, t)
            with pool.Fori(0, 4) as i:
                for j in range(6):
                    split_w(pool, mixed_tile(i, j))
            with pool.Fori(0, 2) as i:
                for r in range(3):
                    split_w(pool, late_z(i, r))
            with pool.Fori(0, NCH) as c:
                for m in range(9):
                    split_w(pool, main_tile(c, m))
            for b in range(PASSES - 1):
                with pool.Fori(0, 4) as i:
                    for r in range(SLOT2):
                        split_w(pool, out_tile(b, i, r))
            def split_wo(k):
                pool.wait_ge(wo_in, 16 * KT)
                if k == 0:
                    pool.wait_ge(S["tail_saved"], 64)
                    pool.wait_ge(S["v_used"], 8 + OPEN)
                pool.tensor_scalar(wo_hi[k], wo_raw[k], 1.0, 0.0, ALU.mult, ALU.add).then_inc(S["wo_high"], 1)
                pool.wait_ge(S["wo_high"], k + 1)
                pool.tensor_tensor(wo_lo[k], wo_raw[k], wo_hi[k].bitcast(F32), ALU.subtract).then_inc(S["wo_split"], 1)
            for n in range(KT):
                split_w(pool, out_tile(3, n // 2, n % 2))
                if n >= 4:
                    split_wo(2 * n - 8)
                    split_wo(2 * n - 7)

        @block.scalar
        def _(act):
            act.wait_ge(const_ready, 4)
            act.activation(root[:, NROW:NROW + 1], epsc[:], ACT.Sqrt).then_inc(paced, 1)
            def root_rows(a):
                n = row_tile(a)[0]
                act.wait_ge(rows_in[a % 2], 16 * (a // 2 + 1))
                if a:
                    act.wait_ge(square_done, a)
                act.activation(junk[0:n, :], xr[a % 2][0:n, :], ACT.Square, accum_out=ssq[0:n, a:a + 1]).then_inc(square_done, 1)
                act.wait_ge(square_done, a + 1)
                act.activation(root[0:n, a:a + 1], ssq[0:n, a:a + 1], ACT.Sqrt, scale=1.0 / D, bias=epsc[0:n, :]).then_inc(root_done, 1)
            def high_rows(a):
                for h in range(2):
                    src, hi, _ = turned_rows(a, h)
                    act.wait_ge(turned, 2 * a + h + 1)
                    act.activation(hi, src, ACT.Copy).then_inc(u_high, 1)
            for a in range(PROMPT_ROWS + 1):
                if a < PROMPT_ROWS:
                    root_rows(a)
                if a:
                    high_rows(a - 1)
            act.wait_ge(pads_ready, 1)
            with act.Fori(0, XT // 3) as i:
                for r in range(3):
                    t = xbc_tile(i, r)
                    j = i * 3 + r
                    act.wait_ge(conv[KS - 1], j * 2 + OPEN)
                    act.wait_ge(tails_kept, j + OPEN)
                    read_out(act, t, xp[:, KS - 1:], ACT.Copy)
                    act.wait_ge(conv[KS - 1], (j + 1) * 2 + OPEN)
                    act.wait_ge(stored[r], i * 16 + OPEN)
                    act.activation(stage[r][:], cv[:, :], ACT.Silu).then_inc(silu_done, 1)
                    act.wait_ge(silu_done, j + 1 + OPEN)
                    act.dma_start(rows(s_xbc, j), stage[r][:]).then_inc(stored[r], 16)
            for a in range(PROMPT_ROWS, NROW):
                root_rows(a)
            act.wait_ge(par_turned, 1)
            evacuated(act, dt_tile)
            act.activation(absv[0:HEADS, :], dtv[0:HEADS, :], ACT.Abs).then_inc(dt_abs, 1)
            act.wait_ge(dt_abs, 1)
            act.activation(expo[0:HEADS, :], absv[0:HEADS, :], ACT.Exp, scale=-1.0).then_inc(dt_exp, 1)
            act.activation(aneg[0:HEADS, :], alog[0:HEADS, :], ACT.Exp).then_inc(dt_exp, 1)
            to_dram(act, z_first[0], Q1, s_z[0:P, :], ACT.Silu)
            for a in range(PROMPT_ROWS, NROW):
                high_rows(a)
            to_dram(act, z_first[1], Q1, s_z[P:2 * P, :], ACT.Silu)
            for r in range(3):
                act.wait_ge(stored[r], 16 * Q1 + OPEN)
            act.dma_start(bcx, s_xbc[INNER:, SEQ:].rearrange("(t p) b -> p t b", p=P)).then_inc(bcx_in, 16)
            act.wait_ge(u_split, 2 * NROW)
            with act.Fori(0, 4) as i:
                for j in range(6):
                    t = mixed_tile(i, j)
                    if j % 3 == 0:
                        to_dram(act, t, i * 2 + Q1 + j // 3, rows(s_z, z_of(i, j)), ACT.Silu)
                    else:
                        b = KV_BANK[j]
                        act.wait_ge(done[t[1]], t[0] + 1 + OPEN)
                        act.activation(kv_t[:, bass.ds(kv_of(i, j), 1), :].rearrange("p a m -> p (a m)"), pm[3 + b][:, 0:NM],
                                       ACT.Copy).then_inc(kv_evac[b], 1)
            act.wait_ge(dt_ready, 1)
            act.activation(dd[0:HEADS, 0, :], da[0:HEADS, SEQ:], ACT.Exp).then_inc(dd_ready, 1)
            with act.Fori(0, 2) as i:
                for r in range(3):
                    to_dram(act, late_z(i, r), i + (Q1 + 8 if r == 0 else Q1 + 1), rows(s_z, i * 3 + 10 + r), ACT.Silu)
            act.wait_ge(kv_saved, 48)
            act.wait_ge(cs_saved, 32)
            act.wait_ge(pre_turned, 1)
            def act_tile(c, m):
                t = main_tile(c, m)
                if m == 0:
                    act.wait_ge(tails_a_kept, c + OPEN)
                    read_out(act, t, cc, ACT.Copy)
                elif m == 2:
                    act.wait_ge(a_ready, c + OPEN)
                    read_out(act, t, zc, ACT.Silu)
                elif m == 3:
                    act.wait_ge(a_ready, c + 1 + OPEN)
                    act.dma_start(rows(s_a, c), stage[0][:]).then_inc(stored[0], 16)
                elif m == 4:
                    to_dram(act, t, staged(c, m), rows(s_q, c), ACT.Copy, MD ** -0.5)
                elif m == 5:
                    to_dram(act, t, staged(c, m), rows(s_mz, c), ACT.Silu)
                elif m >= 6:
                    to_dram(act, t, staged(c, m), s_g[bass.ds(c * P + (m - 6) * D, P), :], ACT.Sigmoid)
            with act.Fori(0, NCH) as c:
                for g in range(GROUPS):
                    n = c * 4 + g
                    act.wait_ge(x_turned, n + 1)
                    act.wait_ge(gy_ready, n + OPEN)
                    act.activation(xt, pm[0][:], ACT.Copy).then_inc(x_copied, 1)
                    act.wait_ge(args_ready, (n + 1) * 3)
                    act.activation(sm, sa, ACT.Exp).then_inc(sm_ready, 1)
                    act.wait_ge(seg_ready, (n + 1) * HG)
                    act.activation(seg, seg, ACT.Exp).then_inc(e_ready, 1)
                    act_tile(c, SEG[g][0])
                    if g % 2:
                        k = c * 2 + g // 2
                        act.wait_ge(sd_step, k * 5 + 3 + OPEN)
                        act.dma_start(ssm_out[bass.ds(k * P, P)], sd).then_inc(sd_saved, 16)
                    act.wait_ge(gy_ready, n + 1 + OPEN)
                    act.wait_ge(y_turned, n + OPEN)
                    act.activation(gyn, gy, ACT.Square, accum_out=ss2).then_inc(sq2_done, 1)
                    act.wait_ge(sq2_done, n + 1)
                    act.activation(rt2, ss2, ACT.Sqrt, scale=1.0 / 512, bias=epsc[:]).then_inc(rt2_done, 1)
                    act.wait_ge(rs2_step, (n + 1) * 5)
                    act.activation(gyn, gy, ACT.Copy, scale=rs2).then_inc(gyn_ready, 1)
                    for m in SEG[g][1:]:
                        act_tile(c, m)
                    act.wait_ge(y_turned, n + 1 + OPEN)
                    act.wait_ge(y_stored, n * 16 + OPEN)
                    for k in range(4):
                        act.activation(yT[:, k, :], pm[2][:, k * P:(k + 1) * P], ACT.Copy,
                                       scale=par[:, C_SN + 4 * g + k:C_SN + 4 * g + k + 1]).then_inc(y_out, 1)
                    act.wait_ge(y_out, (n + 1) * 4 + OPEN)
                    act.dma_start(s_y.rearrange("(t p) n -> p t n", p=P)[:, 4 * g:4 * g + 4, bass.ds(c * CH, CH)], yT).then_inc(y_stored, 16)
            def high_part(b, p):
                if b < 4:
                    act.wait_ge(act_in[p], 16 * (b + 1))
                else:
                    act.wait_ge(merge_done[0], 3 * 4 + OPEN)
                    act.wait_ge(merge_done[1], 3 * 4 - 1 + OPEN)
                    act.wait_ge(S["last_merged"], p + 1)
                if (b, p) == (3, 2):
                    act.wait_ge(S["od_ready"], 1)
                last_piece(act, b, p)
                cols = slice(p * PC, (p + 1) * PC)
                act.activation(uhi[:, :, cols], acts_buf(b, p) if b < 4 else merged[:, :, cols], ACT.Copy).then_inc(S["act_high"], 1)
            def load_acts(b):
                act.wait_ge(S["act_split"], 3 * b)
                for p in range(NP - (b == 1)):
                    c1 = SEQ if (b, p) == (3, 2) else (p + 1) * PC
                    act.dma_start(acts_buf(b, p)[:, :, 0:c1 - p * PC], ACTS[b][:, :, p * PC:c1]).then_inc(act_in[p], 16)
            act.wait_ge(gy_ready, 32 + OPEN)
            for n in range(4):
                act.wait_ge(S["h_final"], n + 1)
                act.activation(pso[:, 4 * n:4 * n + 4, :], pm[n + (n > 1)][:, :].rearrange("p (a b) -> p a b", b=P), ACT.Copy).then_inc(S["h_copied"], 1)
            act.wait_ge(S["dec_step"], 3)
            act.activation(dec_rs, dec_ms, ACT.Sqrt).then_inc(S["dec_root"], 1)
            act.wait_ge(y_stored, 16 * 32 + OPEN)
            load_acts(1)
            def exp_scores(i, half):
                u = i + half * 4
                act.wait_ge(S["att_step"], u * 5 + 3)
                act.wait_ge(S["p_turned"], u * 2 + OPEN)
                for k in range(4):
                    act.activation(pt[:, k, :], pm[k // 2][:, (k % 2) * NM:(k % 2 + 1) * NM], ACT.Exp, bias=anx[:, k:k + 1],
                                   accum_out=asum[:, k:k + 1]).then_inc(S["att_exp"], 1)
            def copy_probs(i, half):
                u = i + half * 4
                for m in range(2):
                    act.wait_ge(S["p_turned"], u * 2 + m + 1 + OPEN)
                    act.wait_ge(S["pv_done"], u + OPEN)
                    act.activation(ptT[:, m, :], pm[2 + m][:], ACT.Copy).then_inc(S["p_copied"], 1)
            def save_att(i, half):
                u = i + half * 4
                act.wait_ge(S["att_ready"], (u + 1) * 2 + OPEN)
                act.dma_start(s_o[bass.ds(i * MD, MD), half * 512:half * 512 + 512].rearrange("(t p) n -> p t n", p=P), amz).then_inc(S["att_saved"], 16)
            def load_sample(k):
                act.wait_ge(S["sam_read"], k * 8 + OPEN)
                settle(act)
                act.dma_start(dk, I["cache_mem_k"][0, bass.ds(k, 1)].rearrange("c (a m) h d -> m (c a) (h d)", m=P)).then_inc(S["sam_in"], 16)
                act.dma_start(dq.rearrange("p (t n) -> p t n", n=P),
                              s_qd.rearrange("(t b) n -> b t n", b=NB)[bass.ds(k, 1)].to_broadcast([P, KT, P])).then_inc(S["sam_in"], 16)
            with act.Fori(0, 3) as i:
                exp_scores(i, 0)
                copy_probs(i, 0)
                save_att(i, 0)
            exp_scores(3, 0)
            copy_probs(3, 0)
            for p in range(NP):
                high_part(1, p)
            save_att(3, 0)
            act.wait_ge(S["q_saved"], 16)
            load_acts(2)
            with act.Fori(0, 3) as i:
                load_sample(i * 2)
                exp_scores(i, 1)
                copy_probs(i, 1)
                load_sample(i * 2 + 1)
                save_att(i, 1)
            load_sample(6)
            exp_scores(3, 1)
            copy_probs(3, 1)
            load_sample(7)
            for p in range(NP):
                high_part(2, p)
            save_att(3, 1)
            act.wait_ge(S["att_saved"], 16 * 8 + OPEN)
            load_acts(3)
            act.wait_ge(S["sam_step"], 2)
            act.activation(dp[0:32, :, :], pm[0][0:32, 0:NM].rearrange("p (a b) -> p a b", b=P), ACT.Exp, bias=dnx[0:32, :],
                           accum_out=dsum[0:32, :]).then_inc(S["sam_exp"], 1)
            for src, dst, n, q, x in TAILS:
                act.wait_ge(S["tail_turned"], x + 1)
                act.activation(dst[0:n, q * 512:(q + 1) * 512], pm[2 + x % 3][0:n, :], ACT.Copy).then_inc(S["tail_copied"], 1)
            act.wait_ge(S["tail_copied"], 8)
            for src, dst in ((trow_s[0:KS - 1, :], O["p_conv_s"][0, 0]), (trow_s[KS - 1:TAIL_S, :], O["s_conv_s"][0, :, KS - 2, :]),
                             (trow_a[0:KA - 1, :], O["p_conv_a"][0, 0]), (trow_a[KA - 1:TAIL_A, :], O["s_conv_a"][0, :, KA - 2, :])):
                act.dma_start(dst, src).then_inc(S["tail_saved"], 16)
            with act.Fori(1, 4) as i:
                for r in range(2):
                    act.wait_ge(S["v_used"], i * 2 + (r - 1) + OPEN)
                    settle(act)
                    load_v(act, i * 2 + r, r)
            for b in (3, 4):
                for p in range(NP):
                    high_part(b, p)
            act.wait_ge(S["act_split"], 15)
            for a in range(NCH + 1):
                n = P if a < NCH else NB
                act.wait_ge(S["row_sum"], 2 * (a + 1))
                if a:
                    act.wait_ge(S["row_sq"], a)
                act.activation(fjunk[0:n, :], rr[a % 2][0:n, :], ACT.Square, accum_out=fss[0:n, a:a + 1]).then_inc(S["row_sq"], 1)
                act.wait_ge(S["row_sq"], a + 1)
                act.activation(frt[0:n, a:a + 1], fss[0:n, a:a + 1], ACT.Sqrt, scale=1.0 / D, bias=epsc[0:n, :]).then_inc(S["row_root"], 1)

        @block.vector
        def _(dve):
            dve.wait_ge(norm_in, 16)
            def norm_rows(a):
                n = row_tile(a)[0]
                b = a % 2
                dve.wait_ge(root_done, a + 1)
                dve.reciprocal(rs[0:n, a:a + 1], root[0:n, a:a + 1]).then_inc(rs_done, 1)
                dve.wait_ge(rs_done, a + 1)
                if a >= 2:
                    dve.wait_ge(turned, 2 * (a - 1))
                w = nwb if a < PROMPT_ROWS else mwb
                dve.scalar_tensor_tensor(xn[b][0:n, :], xr[b][0:n, :], rs[0:n, a:a + 1], w[0:n, :],
                                         ALU.mult, ALU.mult).then_inc(normed[b], 1)
            def low_rows(a):
                for h in range(2):
                    src, hi, lo = turned_rows(a, h)
                    dve.wait_ge(u_high, 2 * a + h + 1)
                    dve.tensor_tensor(lo, src, hi.bitcast(F32), ALU.subtract).then_inc(u_split, 1)
            for a in range(PROMPT_ROWS + 1):
                if a < PROMPT_ROWS:
                    norm_rows(a)
                if a:
                    low_rows(a - 1)
            dve.wait_ge(par_turned, 1)
            dve.tensor_copy(par[:, 0:P], pm[4][:, 0:P]).then_inc(par_copied, 1)
            dve.tensor_copy(par[:, P:NPAR], pm[4][:, P:NPAR]).then_inc(par_copied, 1)
            for h in range(2):
                dve.tensor_copy(hist_s[:, 12 * h:12 * h + 12, :, :],
                                pm[h][:, 0:288].rearrange("p (t b k) -> p t b k", b=NB, k=KS - 1)).then_inc(par_copied, 1)
            dve.tensor_copy(hist_a[:, :, :, :],
                            pm[2][:, 0:128].rearrange("p (t b k) -> p t b k", b=NB, k=KA - 1)).then_inc(par_copied, 1)
            dve.wait_ge(par_copied, 5)
            def col(c, j=None):
                return par[:, c:c + 1] if j is None else par[:, bass.ds(j + c, 1)]
            with dve.Fori(0, XT // 3) as i:
                for r in range(3):
                    t = xbc_tile(i, r)
                    j = i * 3 + r
                    evacuated(dve, t)
                    hist = hist_s[:, bass.ds(j, 1), :, :].rearrange("p a b k -> p (a b) k")
                    for k in range(KS):
                        now = xp[:, SEQ + KS - 1:] if k == KS - 1 else hist[:, :, k]
                        if k == 0:
                            dve.wait_ge(silu_done, j + OPEN)
                            dve.tensor_scalar(cv[:, 0:SEQ], xp[:, 0:SEQ], col(C_SW, j), col(C_SB, j), ALU.mult, ALU.add).then_inc(conv[0], 1)
                            dve.tensor_scalar(cv[:, SEQ:], now, col(C_SW, j), col(C_SB, j), ALU.mult, ALU.add).then_inc(conv[0], 1)
                            continue
                        w = col(C_SW + k * XT, j)
                        dve.wait_ge(conv[k - 1], (j + 1) * 2 + OPEN)
                        dve.scalar_tensor_tensor(cv[:, 0:SEQ], xp[:, k:k + SEQ], w, cv[:, 0:SEQ], ALU.mult, ALU.add).then_inc(conv[k], 1)
                        dve.scalar_tensor_tensor(cv[:, SEQ:], now, w, cv[:, SEQ:], ALU.mult, ALU.add).then_inc(conv[k], 1)
                    dve.tensor_copy(tail_s[:, bass.ds(j, 1), :].rearrange("p a b -> p (a b)"), xp[:, SEQ:]).then_inc(tails_kept, 1)
            dve.wait_ge(small_in, 64)
            dve.wait_ge(par_turned, 1)
            H = slice(0, HEADS)
            for p in range(NP):
                piece_ready(dve, dt_tile, p)
                dve.tensor_scalar(dtv[H, p * PC:(p + 1) * PC], acc[H, p, 0:PC], dtb[H, :], None, ALU.add).then_inc(evac[p], 1)
            for a in range(PROMPT_ROWS, NROW):
                norm_rows(a)
            for a in range(PROMPT_ROWS, NROW):
                low_rows(a)
            dve.wait_ge(u_split, 2 * NROW)
            evacuated(dve, dt_tile)
            steps = [0]
            def step(ins):
                steps[0] += 1
                ins.then_inc(dt_step, 1)
                dve.wait_ge(dt_step, steps[0])
            dve.wait_ge(dt_exp, 1)
            step(dve.tensor_scalar(zz[H, :], expo[H, :], 2.0, None, ALU.add))
            step(dve.reciprocal(zz[H, :], zz[H, :]))
            step(dve.tensor_tensor(zz[H, :], zz[H, :], expo[H, :], ALU.mult))
            step(dve.tensor_tensor(expo[H, :], zz[H, :], zz[H, :], ALU.mult))
            step(dve.tensor_scalar(csv[H, :], expo[H, :], 1.0 / (2 * LOG1P_TERMS + 1), None, ALU.mult))
            for n in range(LOG1P_TERMS - 1, 0, -1):
                step(dve.scalar_tensor_tensor(csv[H, :], csv[H, :], 1.0 / (2 * n + 1), expo[H, :], ALU.add, ALU.mult))
            step(dve.scalar_tensor_tensor(csv[H, :], csv[H, :], 1.0, zz[H, :], ALU.add, ALU.mult))
            step(dve.tensor_scalar(dtv[H, :], dtv[H, :], 0.0, None, ALU.max))
            step(dve.scalar_tensor_tensor(dtv[H, :], csv[H, :], 2.0, dtv[H, :], ALU.mult, ALU.add))
            dve.wait_ge(dt_exp, 2)
            step(dve.tensor_scalar(aneg[H, :], aneg[H, :], -1.0, None, ALU.mult))
            dve.tensor_scalar(da[H, :], dtv[H, :], aneg[H, :], None, ALU.mult).then_inc(dt_ready, 1)
            step(dve.memset(resets[H, :], 1.0))
            step(dve.memset(resets[H, 0:SEQ:CH], 0.0))
            dve.wait_ge(dt_ready, 1)
            dve.tensor_tensor_scan(csv[H, 0:SEQ], resets[H, 0:SEQ], da[H, 0:SEQ], 0.0, ALU.mult, ALU.add).then_inc(cs_ready, 1)
            dve.tensor_copy(dd[H, 1, :], dtv[H, SEQ:]).then_inc(dd_ready, 1)
            dve.wait_ge(pre_turned, 1)
            dve.tensor_copy(dt_tok[:], pm[0][:, 0:NCH * HEADS]).then_inc(pre_copied, 1)
            dve.tensor_copy(cs_tok[:], pm[0][:, NCH * HEADS:2 * NCH * HEADS]).then_inc(pre_copied, 1)
            for n in range(8):
                s, m, h = n // 4, n // 2 % 2, n % 2
                dve.wait_ge(pre_turned, n + 2)
                dve.tensor_copy(kv_tok[:, s, m, h * 512:(h + 1) * 512], pm[1 + n % 4][:]).then_inc(pre_copied, 1)
            dve.wait_ge(pre_turned, 10)
            dve.tensor_copy(bcr[0:64, :], pm[0][0:64, 0:P]).then_inc(pre_copied, 1)
            dve.wait_ge(kv_saved, 48)
            dve.wait_ge(cs_saved, 32)
            dve.wait_ge(pre_copied, 2)
            dve.memset(hT, 0.0).then_inc(h_added, 1)
            dve.memset(hb[:, 0:KA - 1], 0.0).then_inc(pads_ready, 1)
            dve.wait_ge(h_added, 1)
            dve.wait_ge(pads_ready, 2)
            dve.wait_ge(dec_in, 16 * 3)
            for e in range(2):
                part = slice(e * HD, (e + 1) * HD)
                dve.tensor_copy(dec_skip[part, :], dskip[part, e::2]).then_inc(dec_ready, 1)
            dve.tensor_tensor(dec_xdt, dec_x, dec_dd[:, :, 1, :], ALU.mult).then_inc(dec_ready, 1)
            dve.wait_ge(dec_ready, 3)
            def sample_step(c, g):
                k = c * 2 + g // 2
                flat = lambda v: v[:, bass.ds(k, 1), :].rearrange("p a b -> p (a b)")
                decay = dec_dd[:, bass.ds(k, 1), 0, :].rearrange("p a b -> p (a b)")
                if g == 0:
                    dve.wait_ge(bcd_in, (c + 1) * 16)
                dve.wait_ge(sd_in, (k + 1) * 16)
                dve.wait_ge(sd_step, k * 5 + OPEN)
                dve.tensor_tensor(sd2, bcd[:, 0, :, :], bcast(flat(dec_xdt), P), ALU.mult).then_inc(sd_step, 1)
                dve.tensor_tensor(sd, sd, bcast(decay, P), ALU.mult).then_inc(sd_step, 1)
                dve.wait_ge(sd_step, k * 5 + 2 + OPEN)
                dve.tensor_tensor(sd, sd, sd2, ALU.add).then_inc(sd_step, 1)
            def sample_output(c, g):
                k = c * 2 + g // 2
                dve.wait_ge(sd_step, k * 5 + 3 + OPEN)
                dve.tensor_tensor(sd2, sd, bcd[:, 1, :, :], ALU.mult).then_inc(sd_step, 1)
                dve.wait_ge(sd_step, k * 5 + 4 + OPEN)
                dve.tensor_reduce(dec_y[:, bass.ds(k, 1), :].rearrange("p a b -> p (a b)"), sd2, AX.X, ALU.add).then_inc(sd_step, 1)
            def dve_tile(c, m):
                t = main_tile(c, m)
                if m == 1:
                    evacuated(dve, main_tile(c, 0))
                    for p in range(NP):
                        piece_ready(dve, t, p)
                        lo, hi = p * PC, (p + 1) * PC
                        dve.wait_ge(a_conv, c * 2 * KA + OPEN)
                        dve.wait_ge(tails_a_kept, c + OPEN)
                        dve.tensor_tensor(hb[:, KA - 1 + lo:KA - 1 + hi], acc[:, p, 0:PC], cc[:, lo:hi], ALU.mult).then_inc(evac[p], 1)
                    evacuated(dve, t)
                    dve.tensor_copy(tail_a[:, bass.ds(c, 1), :].rearrange("p a b -> p (a b)"), hb[:, SEQ:]).then_inc(tails_a_kept, 1)
                    hist = hist_a[:, bass.ds(c, 1), :, :].rearrange("p a b k -> p (a b) k")
                    dve.wait_ge(a_ready, c + OPEN)
                    for k in range(KA):
                        now = hb[:, SEQ + KA - 1:] if k == KA - 1 else hist[:, :, k]
                        w = col(C_AW + k * KT, c)
                        if k == 0:
                            dve.tensor_scalar(av[:, 0:SEQ], hb[:, 0:SEQ], w, None, ALU.mult).then_inc(a_conv, 1)
                            dve.tensor_scalar(av[:, SEQ:], now, w, None, ALU.mult).then_inc(a_conv, 1)
                            continue
                        dve.wait_ge(a_conv, (c * KA + k) * 2 + OPEN)
                        dve.scalar_tensor_tensor(av[:, 0:SEQ], hb[:, k:k + SEQ], w, av[:, 0:SEQ], ALU.mult, ALU.add).then_inc(a_conv, 1)
                        dve.scalar_tensor_tensor(av[:, SEQ:], now, w, av[:, SEQ:], ALU.mult, ALU.add).then_inc(a_conv, 1)
                elif m == 3:
                    evacuated(dve, main_tile(c, 2))
                    for p in range(NP):
                        piece_ready(dve, t, p)
                        part = zc[:, p * PC:(p + 1) * PC]
                        dve.tensor_tensor(part, part, acc[:, p, 0:PC], ALU.mult).then_inc(evac[p], 1)
                    evacuated(dve, t)
                    dve.wait_ge(a_conv, (c + 1) * 2 * KA + OPEN)
                    dve.wait_ge(stored[0], staged(c, m) * 16 + OPEN)
                    dve.tensor_tensor(stage[0][:], zc, av, ALU.mult).then_inc(a_ready, 1)
            with dve.Fori(0, NCH) as c:
                for g in range(GROUPS):
                    n, b, u = c * 4 + g, g % 2, c * 2 + g // 2
                    dve.wait_ge(group_in[b], (u + 1) * 64)
                    last = csb[b][:, :, CH - 1]
                    cs = cs_tok[:, bass.ds(c * HEADS + g * HG, HG)]
                    dve.wait_ge(sm_ready, n + OPEN)
                    dve.tensor_tensor(sa[:, 0, :], last, cs, ALU.subtract).then_inc(args_ready, 1)
                    dve.tensor_copy(sa[:, 1, :], cs).then_inc(args_ready, 1)
                    dve.tensor_copy(sa[:, 2, :], last).then_inc(args_ready, 1)
                    dve.wait_ge(m_ready, n + OPEN)
                    for h in range(HG):
                        dve.tensor_scalar(seg[:, h, :], csb[b][:, h, :], cs_tok[:, bass.ds(c * HEADS + g * HG + h, 1)], 0.0,
                                          ALU.subtract, ALU.min).then_inc(seg_ready, 1)
                    dve.wait_ge(b_ready, n + 1)
                    group_before(dve, c, g)
                    dve.tensor_copy(bt, pm[1][:, 0:P]).then_inc(bt_ready, 1)
                    dve.tensor_tensor(scm, pm[1][:, P:2 * P], tri[:], ALU.mult).then_inc(sc_ready, 1)
                    dve.wait_ge(x_copied, n + 1)
                    dve.tensor_tensor(heads(xdt), heads(xt), bcast(dt_tok[:, bass.ds(c * HEADS + g * HG, HG)], HD), ALU.mult).then_inc(xdt_ready, 1)
                    dve.wait_ge(sm_ready, n + 1 + OPEN)
                    dve.wait_ge(xdt_ready, n + 1)
                    dve.tensor_tensor(heads(xdd), heads(xdt), bcast(sm[:, 0, :], HD), ALU.mult).then_inc(xdd_ready, 1)
                    dve.wait_ge(e_ready, n + 1)
                    dve.wait_ge(sc_ready, n + 1)
                    dve.tensor_tensor(mm_, seg, scm.unsqueeze(1).to_broadcast([P, HG, CH]), ALU.mult).then_inc(m_ready, 1)
                    dve_tile(c, SEG[g][0])
                    dve.wait_ge(gyn_ready, n + OPEN)
                    dve.tensor_tensor(heads(gy), heads(xt), bcast(dskip[:, g * HG:(g + 1) * HG], HD), ALU.mult).then_inc(y_step, 1)
                    dve.wait_ge(summed[b], u + 1 + OPEN)
                    dve.tensor_tensor(heads(yv), heads(pm[3][:]), bcast(sm[:, 1, :], HD), ALU.mult).then_inc(y_step, 1)
                    dve.tensor_tensor(heads(hT[:, g, :]), heads(hT[:, g, :]), bcast(sm[:, 2, :], HD), ALU.mult).then_inc(h_scaled, 1)
                    dve.wait_ge(y_step, n * 4 + 2)
                    dve.tensor_tensor(yv, yv, pm[4][:], ALU.add).then_inc(y_step, 1)
                    dve.wait_ge(h_scaled, n + 1)
                    dve.tensor_tensor(hT[:, g, :], hT[:, g, :], pm[0][:], ALU.add).then_inc(h_added, 1)
                    dve.wait_ge(y_step, n * 4 + 3)
                    dve.tensor_tensor(yv, yv, gy, ALU.add).then_inc(y_step, 1)
                    dve.wait_ge(y_step, n * 4 + 4)
                    dve.wait_ge(z_turned, n + 1)
                    dve.tensor_tensor(gy, yv, pm[2][:], ALU.mult).then_inc(gy_ready, 1)
                    dve.wait_ge(rt2_done, n + 1)
                    dve.wait_ge(gyn_ready, n + OPEN)
                    dve.tensor_scalar(var2, ss2, 1.0 / 512, EPS, ALU.mult, ALU.add).then_inc(rs2_step, 1)
                    dve.reciprocal(rs2, rt2).then_inc(rs2_step, 1)
                    dve.wait_ge(rs2_step, n * 5 + 2)
                    dve.scalar_tensor_tensor(nw2, rs2, var2, rs2, ALU.mult, ALU.mult).then_inc(rs2_step, 1)
                    dve.wait_ge(rs2_step, n * 5 + 3)
                    dve.tensor_scalar(nw2, nw2, -0.5, 1.5, ALU.mult, ALU.add).then_inc(rs2_step, 1)
                    dve.wait_ge(rs2_step, n * 5 + 4)
                    dve.tensor_tensor(rs2, rs2, nw2, ALU.mult).then_inc(rs2_step, 1)
                    if g % 2 == 0:
                        sample_step(c, g)
                    if g == 1:
                        sample_output(c, 0)
                    for m in SEG[g][1:]:
                        dve_tile(c, m)
                    if g == 2:
                        sample_output(c, 2)
            dve.wait_ge(dec_in, 16 * 4)
            dve.tensor_tensor(dec_sq, dec_x, bcast(dec_skip, NB), ALU.mult).then_inc(dec_ready, 1)
            dve.wait_ge(dec_ready, 4)
            dve.wait_ge(sd_step, 80 + OPEN)
            dve.tensor_tensor(dec_y, dec_y, dec_sq, ALU.add).then_inc(dec_ready, 1)
            dve.wait_ge(dec_ready, 5)
            dve.tensor_tensor(dec_y, dec_y, dec_z, ALU.mult).then_inc(dec_ready, 1)
            dve.wait_ge(dec_ready, 6)
            dve.tensor_tensor(dec_sq, dec_y, dec_y, ALU.mult).then_inc(S["dec_sq_done"], 1)
            def low_part(b, p):
                dve.wait_ge(S["act_high"], b * NP + p + 1)
                cols = slice(p * PC, (p + 1) * PC)
                dve.tensor_tensor(ulo[:, :, cols], acts_buf(b, p) if b < 4 else merged[:, :, cols],
                                  uhi[:, :, cols].bitcast(F32), ALU.subtract).then_inc(S["act_split"], 1)
            for p in range(NP):
                dve.wait_ge(act_in[p], 16)
                last_piece(dve, 0, p)
                cols = slice(p * PC, (p + 1) * PC)
                dve.tensor_copy(uhi[:, :, cols], first_buf[p]).then_inc(S["act_high"], 1)
                low_part(0, p)
            dve.wait_ge(S["dec_summed"], 1)
            dve.wait_ge(S["qx_turned"], 1)
            dve.tensor_reduce(dec_ms, pm[2][:, 0:P].rearrange("p (g t b) -> p g b t", g=GROUPS, b=NB), AX.X, ALU.add).then_inc(S["dec_step"], 1)
            dve.wait_ge(S["dec_step"], 1)
            dve.tensor_scalar(dec_ms, dec_ms, 1.0 / 512, EPS, ALU.mult, ALU.add).then_inc(S["dec_step"], 1)
            dve.wait_ge(S["dec_step"], 2)
            dve.tensor_scalar(dec_nw, dec_ms, -0.5, None, ALU.mult).then_inc(S["dec_step"], 1)
            dve.wait_ge(S["dec_root"], 1)
            dve.wait_ge(S["dec_step"], 3)
            dve.reciprocal(dec_rs, dec_rs).then_inc(S["dec_step"], 1)
            dve.wait_ge(S["dec_step"], 4)
            step(dve.tensor_tensor(dec_nw, dec_nw, dec_rs, ALU.mult))
            step(dve.tensor_tensor(dec_nw, dec_nw, dec_rs, ALU.mult))
            step(dve.tensor_scalar(dec_nw, dec_nw, 1.5, None, ALU.add))
            step(dve.tensor_tensor(dec_rs, dec_rs, dec_nw, ALU.mult))
            for g in range(GROUPS):
                step(dve.tensor_tensor(dec_y[:, 4 * g:4 * g + 4, :], dec_y[:, 4 * g:4 * g + 4, :],
                                       dec_rs[:, g:g + 1, :].to_broadcast([P, 4, NB]), ALU.mult))
            dve.tensor_tensor(dec_y, dec_y, bcast(par[:, C_SN:C_SN + ZT], NB), ALU.mult).then_inc(S["dec_step"], 1)
            for r in range(3):
                dve.wait_ge(stored[r], 16 * (16 + STAGED[r]) + OPEN)
            dve.tensor_copy(qrow[0:64, :], pm[2][0:64, P:2 * P]).then_inc(S["qx_copied"], 1)
            dve.wait_ge(y_stored, 16 * 32 + OPEN)
            def merge(b, i, r, last=False):
                t = out_tile(b, i, r)
                it = bass.ds(i * 2 + r, 1)
                dve.wait_ge(gate_in[r], (i + (b * 4 + 1)) * 16)
                for p in range(NP):
                    piece_ready(dve, t, p)
                    cols = slice(p * PC, (p + 1) * PC)
                    at = merged[:, it, cols].rearrange("p a n -> p (a n)")
                    if b == 0 and p == 0:
                        dve.wait_ge(S["h_saved"], 16)
                    dve.tensor_tensor(stage[r][:, cols] if b else at, stage[r][:, cols], acc[:, p, 0:PC], ALU.mult).then_inc(evac[p], 1)
                    if b == 3 and last:
                        dve.wait_ge(evac[p], t[2] + 1 + OPEN)
                        dve.tensor_tensor(at, at, stage[r][:, cols], ALU.add).then_inc(S["last_merged"], 1)
                    if last and (b, p) != (2, NP - 1):
                        low_part(b + 1, p)
                if b and not (b == 3 and last):
                    evacuated(dve, t)
                    whole = merged[:, it, :].rearrange("p a n -> p (a n)")
                    dve.tensor_tensor(whole, whole, stage[r][:], ALU.add).then_inc(merge_done[r], 1)
            def softmax(i, half):
                u = i + half * 4
                dve.wait_ge(S["qk_done"], u + 1 + OPEN)
                dve.wait_ge(S["att_exp"], u * 4 + OPEN)
                for k in range(2):
                    dve.tensor_reduce(amx[:, 2 * k:2 * k + 2], pm[k][:, :].rearrange("p (a b) -> p a b", b=NM), AX.X, ALU.max).then_inc(S["att_step"], 1)
                dve.wait_ge(S["att_step"], u * 5 + 2)
                dve.tensor_scalar(anx, amx, -1.0, None, ALU.mult).then_inc(S["att_step"], 1)
                dve.wait_ge(S["att_exp"], (u + 1) * 4 + OPEN)
                dve.reciprocal(arec, asum).then_inc(S["att_step"], 1)
                dve.wait_ge(S["att_step"], u * 5 + 4)
                dve.tensor_tensor(pt, pt, bcast(arec, NM), ALU.mult).then_inc(S["att_step"], 1)
            def gate_att(i, half):
                u = i + half * 4
                dve.wait_ge(S["att_in"], (u + 1) * 32)
                dve.wait_ge(S["pv_done"], u + 1 + OPEN)
                for d in range(2):
                    dve.tensor_tensor(amz[:, d, :], amz[:, d, :], pm[4 - d][:], ALU.mult).then_inc(S["att_ready"], 1)
            def sample_scores(k):
                dve.wait_ge(S["sam_in"], (k + 1) * 32)
                dve.wait_ge(S["sam_kept"], k + OPEN)
                for a in range(2):
                    for h in range(MH):
                        ks = dk[:, a, h * MD:(h + 1) * MD]
                        dve.tensor_tensor_reduce(ks, ks, dq[:, h * MD:(h + 1) * MD], 1.0, 0.0, ALU.mult, ALU.add,
                                                 sde[:, a, h:h + 1]).then_inc(S["sam_read"], 1)
                dve.wait_ge(S["sam_read"], (k + 1) * 8 + OPEN)
                dve.tensor_copy(sds[:, :, bass.ds(k, 1), :].rearrange("p a b h -> p a (b h)"), sde).then_inc(S["sam_kept"], 1)
            with dve.Fori(0, 3) as i:
                softmax(i, 0)
                merge(0, i, 0)
                merge(0, i, 1)
                gate_att(i, 0)
            softmax(3, 0)
            merge(0, 3, 0)
            merge(0, 3, 1, last=True)
            gate_att(3, 0)
            with dve.Fori(0, 3) as i:
                softmax(i, 1)
                merge(1, i, 0)
                sample_scores(i * 2)
                merge(1, i, 1)
                gate_att(i, 1)
                sample_scores(i * 2 + 1)
            softmax(3, 1)
            merge(1, 3, 0)
            sample_scores(6)
            merge(1, 3, 1, last=True)
            gate_att(3, 1)
            sample_scores(7)
            merge(2, 0, 0)
            dve.wait_ge(S["sds_turned"], 1)
            dve.tensor_reduce(dmx[0:32, :], pm[0][0:32, 0:NM], AX.X, ALU.max).then_inc(S["sam_step"], 1)
            dve.wait_ge(S["sam_step"], 1)
            dve.tensor_scalar(dnx[0:32, :], dmx[0:32, :], -1.0, None, ALU.mult).then_inc(S["sam_step"], 1)
            dve.wait_ge(S["sam_exp"], 1)
            dve.reciprocal(drec[0:32, :], dsum[0:32, :]).then_inc(S["sam_step"], 1)
            dve.wait_ge(S["sam_step"], 3)
            dve.tensor_scalar(dp[0:32, :, :], dp[0:32, :, :], drec[0:32, :], None, ALU.mult).then_inc(S["sam_step"], 1)
            merge(2, 0, 1)
            dve.wait_ge(S["dp_turned"], 1)
            dve.tensor_copy(dpT, pm[1][:, 0:64].rearrange("p (a b) -> p a b", a=2)).then_inc(S["dp_copied"], 1)
            dve.wait_ge(S["dp_copied"], 1)
            def values_times(i, b, k):
                dve.wait_ge(v_in[b], (i + 1) * 32)
                for a in range(2):
                    for h in range(MH):
                        part = vv[b][a][:, h * MD:(h + 1) * MD]
                        dve.tensor_scalar(part, part, dpT[:, a, bass.ds(k * 4 + h, 1)], None, ALU.mult).then_inc(S["v_scaled"], 1)
                dve.wait_ge(S["v_scaled"], k * 9 + 8)
                dve.tensor_tensor(vv[b][0], vv[b][0], vv[b][1], ALU.add).then_inc(S["v_scaled"], 1)
            with dve.Fori(1, 3) as i:
                for r in range(2):
                    values_times(i - 1, r, i * 2 + (r - 2))
                    merge(2, i, r)
            values_times(2, 0, 4)
            values_times(2, 1, 5)
            merge(2, 3, 0)
            values_times(3, 0, 6)
            values_times(3, 1, 7)
            merge(2, 3, 1, last=True)
            dve.wait_ge(S["v_used"], 8 + OPEN)
            dve.wait_ge(S["qx_in"], 32)
            dve.wait_ge(S["act_split"], 9)
            dve.tensor_tensor(piece_buf[2][:, :, PC - NB:PC], mzd, pm[0][:, 0:64].rearrange("p (b t) -> p t b", t=KT), ALU.mult).then_inc(S["od_ready"], 1)
            low_part(3, 2)
            with dve.Fori(0, 3) as i:
                merge(3, i, 0)
                merge(3, i, 1)
            merge(3, 3, 0)
            merge(3, 3, 1, last=True)
            dve.wait_ge(S["act_split"], 15)
            dve.wait_ge(small_in, 80)
            def final_out(a):
                n = P if a < NCH else NB
                q = slice(a, a + 1)
                dve.wait_ge(S["row_root"], a + 1)
                dve.tensor_scalar(fvar[0:n, q], fss[0:n, q], 1.0 / D, EPS, ALU.mult, ALU.add).then_inc(S["row_step"], 1)
                dve.reciprocal(frs[0:n, q], frt[0:n, q]).then_inc(S["row_step"], 1)
                dve.wait_ge(S["row_step"], a * 5 + 2)
                dve.scalar_tensor_tensor(fnw[0:n, q], frs[0:n, q], fvar[0:n, q], frs[0:n, q], ALU.mult, ALU.mult).then_inc(S["row_step"], 1)
                dve.wait_ge(S["row_step"], a * 5 + 3)
                dve.tensor_scalar(fnw[0:n, q], fnw[0:n, q], -0.5, 1.5, ALU.mult, ALU.add).then_inc(S["row_step"], 1)
                dve.wait_ge(S["row_step"], a * 5 + 4)
                dve.tensor_tensor(frs[0:n, q], frs[0:n, q], fnw[0:n, q], ALU.mult).then_inc(S["row_step"], 1)
                dve.wait_ge(S["row_step"], a * 5 + 5)
                v = rr[a % 2][0:n, :]
                dve.scalar_tensor_tensor(v, v, frs[0:n, q], fw[0:n, :], ALU.mult, ALU.mult).then_inc(S["row_out"], 1)
            for a in range(NCH + 2):
                if a < NCH + 1:
                    n = P if a < NCH else NB
                    dve.wait_ge(rows_in[a % 2], 16 * (a // 2 + 1 + (NROW + 1 - a % 2) // 2))
                    if a >= 2:
                        dve.wait_ge(row_saved[a % 2], 16 * (a // 2))
                    for h in range(2):
                        dve.wait_ge(S["row_done"], 2 * a + h + 1)
                        half = slice(h * 512, (h + 1) * 512)
                        dve.tensor_tensor(rr[a % 2][0:n, half], xf[a % 2][0:n, half], pm[2 * (a % 2) + h][0:n, :], ALU.add).then_inc(S["row_sum"], 1)
                if a:
                    final_out(a - 1)

        @block.tensor
        def _(pe):
            pe.wait_ge(const_ready, 6)
            def turn_rows(a):
                n = row_tile(a)[0]
                pe.wait_ge(normed[a % 2], a // 2 + 1)
                for h in range(2):
                    if a >= 2:
                        pe.wait_ge(u_split, 2 * (a - 2) + h + 1)
                    for k in range(4):
                        tr = pe.transpose(pm[2 * (a % 2) + h][:, k * P:k * P + n], xn[a % 2][0:n, (4 * h + k) * P:(4 * h + k + 1) * P],
                                          ident[0:n, 0:n])
                    tr.then_inc(turned, 1)
            for a in range(PROMPT_ROWS):
                turn_rows(a)
                piece_after = {3: 0, 6: 1, PROMPT_ROWS - 1: 2}
                if a in piece_after:
                    p = piece_after[a]
                    pe.wait_ge(w_split[0], 1 + OPEN)
                    pe.wait_ge(u_split, 6 * (p + 1))
                    product(pe, xbc_tile(0, 0), acc[:, p, 0:PC], uhi, ulo, p * PC, PC).then_inc(done[0] if p == NP - 1 else ready[p], 1)
            pe.wait_ge(par_in, 96)
            pe.transpose(pm[4][:, 0:P], par_rows[:, 0, :], ident[:])
            n1 = NPAR - P
            pe.transpose(pm[4][:, P:NPAR], par_rows[0:n1, 1, :], ident[0:n1, 0:n1])
            pe.wait_ge(hist_in, 32)
            for t in range(XT):
                pe.transpose(pm[t // 12][:, (t % 12) * 24:(t % 12) * 24 + 24], hrow_s[0:24, t * P:(t + 1) * P], ident[0:24, 0:24])
            for t in range(KT):
                tr = pe.transpose(pm[2][:, t * 16:t * 16 + 16], hrow_a[0:16, t * P:(t + 1) * P], ident[0:16, 0:16])
            tr.then_inc(par_turned, 1)
            for r in range(1, 3):
                dense(pe, xbc_tile(0, r))
            with pe.Fori(1, XT // 3) as i:
                for r in range(3):
                    dense(pe, xbc_tile(i, r))
            dense(pe, dt_tile)
            dense(pe, z_first[0])
            pe.wait_ge(par_copied, 5)
            for a in range(PROMPT_ROWS, NROW):
                turn_rows(a)
            dense(pe, z_first[1])
            pe.wait_ge(u_split, 2 * NROW)
            with pe.Fori(0, 4) as i:
                for j in range(6):
                    t = mixed_tile(i, j)
                    if j % 3 == 0:
                        dense(pe, t)
                        continue
                    b = KV_BANK[j]
                    pe.wait_ge(w_split[t[1]], t[0] + 1 + OPEN)
                    pe.wait_ge(kv_evac[b], i * 2 + j // 3 + OPEN)
                    product(pe, t, pm[3 + b][:, 0:NM], mhi, mlo, 0, NM).then_inc(done[t[1]], 1)
            pe.wait_ge(cs_ready, 1)
            for n, v in enumerate((dtv, csv)):
                for c in range(NCH):
                    tr = pe.transpose(pm[0][:, (n * NCH + c) * HEADS:(n * NCH + c + 1) * HEADS], v[0:HEADS, c * CH:(c + 1) * CH],
                                      ident[0:HEADS, 0:HEADS])
            tr.then_inc(pre_turned, 1)
            for b in range(2):
                pe.wait_ge(kv_evac[b], KT + OPEN)
            for n in range(8):
                s, m, h = n // 4, n // 2 % 2, n % 2
                if n >= 4:
                    pe.wait_ge(pre_copied, n - 1)
                for k in range(4):
                    tr = pe.transpose(pm[1 + n % 4][:, k * P:(k + 1) * P], kv_t[:, s * KT + h * 4 + k, m * P:(m + 1) * P], ident[:])
                tr.then_inc(pre_turned, 1)
            pe.wait_ge(bcx_in, 16)
            pe.wait_ge(pre_copied, 2)
            pe.transpose(pm[0][0:64, 0:P], bcx.rearrange("p t b -> p (t b)"), ident[:]).then_inc(pre_turned, 1)
            with pe.Fori(0, 2) as i:
                for r in range(3):
                    dense(pe, late_z(i, r))
            pe.wait_ge(pre_copied, 2)
            pe.wait_ge(pre_copied, 11)
            with pe.Fori(0, NCH) as c:
                for g in range(GROUPS):
                    n, b, u = c * 4 + g, g % 2, c * 2 + g // 2
                    bg, cg = xg[b][:, 4, :], xg[b][:, 5, :]
                    pe.wait_ge(group_in[b], (u + 1) * 64)
                    pe.wait_ge(h_added, n + 1)
                    for k in range(4):
                        tr = pe.transpose(pm[0][:, k * P:(k + 1) * P], xg[b][:, k, :], ident[:])
                    tr.then_inc(x_turned, 1)
                    pe.transpose(pm[1][:, 0:P], bg, ident[:])
                    pe.matmul(pm[1][:, P:2 * P], bg, cg, start=True, stop=True).then_inc(b_ready, 1)
                    dense(pe, main_tile(c, SEG[g][0]))
                    pe.wait_ge(y_out, n * 4 + OPEN)
                    for k in range(4):
                        tr = pe.transpose(pm[2][:, k * P:(k + 1) * P], zg[b][:, k, :], ident[:])
                    tr.then_inc(z_turned, 1)
                    pe.wait_ge(m_ready, n + 1 + OPEN)
                    pe.wait_ge(xdd_ready, n + 1)
                    pe.wait_ge(bt_ready, n + 1)
                    pe.matmul(pm[3][:], cg, hT[:, g, :], start=True, stop=True)
                    for h in range(HG):
                        pe.matmul(pm[4][:, h * HD:(h + 1) * HD], mm_[:, h, :], xdt[:, h * HD:(h + 1) * HD], start=True, stop=True)
                    pe.matmul(pm[0][:], bt, xdd, start=True, stop=True).then_inc(summed[b], 1)
                    for m in SEG[g][1:]:
                        dense(pe, main_tile(c, m))
                    pe.wait_ge(gyn_ready, n + 1 + OPEN)
                    for k in range(4):
                        tr = pe.transpose(pm[2][:, k * P:(k + 1) * P], gyn[:, k * P:(k + 1) * P], ident[:])
                    tr.then_inc(y_turned, 1)
            pe.wait_ge(h_added, 33)
            pe.wait_ge(gyn_ready, 32 + OPEN)
            for n in range(4):
                for k in range(4):
                    tr = pe.transpose(pm[n + (n > 1)][:, k * P:(k + 1) * P], hT[:, n, k * P:(k + 1) * P], ident[:])
                tr.then_inc(S["h_final"], 1)
            pe.wait_ge(y_out, 128 + OPEN)
            pe.wait_ge(S["dec_sq_done"], 1)
            pe.matmul(pm[2][:, 0:P], ones[:], dec_sq.rearrange("p t b -> p (t b)"), start=True, stop=True).then_inc(S["dec_summed"], 1)
            pe.wait_ge(S["qx_in"], 16)
            pe.transpose(pm[2][0:64, P:2 * P], qx.rearrange("p t b -> p (t b)"), ident[:]).then_inc(S["qx_turned"], 1)
            pe.wait_ge(S["h_copied"], 2)
            def out_dense(b, i, r):
                dense(pe, out_tile(b, i, r), acts=(S["act_split"], b * NP))
            def scores(i, half):
                u = i + half * 4
                pe.wait_ge(S["qk_in"], (u + 1) * 32)
                pe.wait_ge(S["att_exp"], u * 4 + OPEN)
                for k in range(4):
                    for d in range(2):
                        mm = pe.matmul(pm[k // 2][:, (k % 2) * NM:(k % 2 + 1) * NM], aq[:, d, k * P:(k + 1) * P], ak[:, d, :],
                                       start=d == 0, stop=d == 1)
                mm.then_inc(S["qk_done"], 1)
            def turn_probs(i, half):
                u = i + half * 4
                pe.wait_ge(S["att_step"], u * 5 + 5)
                pe.wait_ge(S["att_ready"], u * 2 + OPEN)
                for m in range(2):
                    for k in range(4):
                        tr = pe.transpose(pm[2 + m][:, k * P:(k + 1) * P], pt[:, k, m * P:(m + 1) * P], ident[:])
                    tr.then_inc(S["p_turned"], 1)
            def values(i, half):
                u = i + half * 4
                pe.wait_ge(S["att_in"], (u + 1) * 32)
                pe.wait_ge(S["p_copied"], (u + 1) * 2 + OPEN)
                for d in range(2):
                    for m in range(2):
                        mm = pe.matmul(pm[4 - d][:], avv[:, m, d * P:(d + 1) * P], ptT[:, m, :], start=m == 0, stop=m == 1)
                mm.then_inc(S["pv_done"], 1)
            for half in range(2):
                with pe.Fori(0, 4) as i:
                    scores(i, half)
                    out_dense(half, i, 0)
                    turn_probs(i, half)
                    out_dense(half, i, 1)
                    values(i, half)
            def turn_tails(tails):
                for src, dst, n, q, x in tails:
                    if x >= 3:
                        pe.wait_ge(S["tail_copied"], x - 2)
                    for k in range(4):
                        tr = pe.transpose(pm[2 + x % 3][0:n, k * P:(k + 1) * P], src[:, q * 4 + k, :], ident[:])
                    tr.then_inc(S["tail_turned"], 1)
            out_dense(2, 0, 0)
            pe.wait_ge(S["att_ready"], 16 + OPEN)
            pe.wait_ge(S["sam_kept"], 8 + OPEN)
            for m in range(2):
                tr = pe.transpose(pm[0][0:32, m * P:(m + 1) * P], sds[:, m, :, :].rearrange("p b h -> p (b h)"), ident[:])
            tr.then_inc(S["sds_turned"], 1)
            turn_tails(TAILS[0:3])
            out_dense(2, 0, 1)
            pe.wait_ge(S["sam_step"], 4)
            for m in range(2):
                tr = pe.transpose(pm[1][:, m * 32:(m + 1) * 32], dp[0:32, m, :], ident[0:32, 0:32])
            tr.then_inc(S["dp_turned"], 1)
            turn_tails(TAILS[3:])
            def sample_values(k, b):
                pe.wait_ge(S["v_scaled"], (k + 1) * 9)
                for t in range(KT):
                    mm = pe.matmul(pm[0][:, bass.ds(k * KT + t, 1)], vv[b][0][:, t * P:(t + 1) * P], ones[:, 0:1], start=True, stop=True)
                mm.then_inc(S["v_used"], 1)
            with pe.Fori(1, 3) as i:
                for r in range(SLOT2):
                    out_dense(2, i, r)
                    sample_values(i * 2 + (r - 2), r)
            for r in range(SLOT2):
                out_dense(2, 3, r)
                sample_values(4 + 2 * r, 0)
                sample_values(5 + 2 * r, 1)
            with pe.Fori(0, 4) as i:
                for r in range(SLOT2):
                    out_dense(3, i, r)
            def final_sums(a, q, n=P):
                for h in range(2):
                    half = slice(h * 512, (h + 1) * 512)
                    for k in range(KT):
                        for s, (x, w) in enumerate(((uhi, wo_hi[k]), (uhi, wo_lo[k]), (ulo, wo_hi[k]))):
                            mm = pe.matmul(pm[2 * q + h][0:n, :], x[:, k, bass.ds(a * P, n)], w[:, half], start=k == 0 and s == 0,
                                           stop=k == KT - 1 and s == 2)
                    mm.then_inc(S["row_done"], 1)
            pe.wait_ge(S["wo_split"], KT)
            for a in range(NCH + 1):
                n = P if a < NCH else NB
                pe.wait_ge(S["act_split"], 13 + (a * P + n - 1) // PC)
                if a >= 2:
                    pe.wait_ge(S["row_sum"], 2 * (a - 1))
                final_sums(a, a % 2, n)



INPUTS = ["x_prompt", "x_sample", "mem_prompt", "state_conv_a", "state_conv_s", "state_ssm", "cache_mem_k",
          "cache_mem_v", "norm_w", "w_in", "conv_a_w", "w_a_out", "conv_s_w", "conv_s_b", "dt_bias", "a_log",
          "d_skip", "ssm_norm_w", "w_s_out", "mem_norm_w", "w_mem_kv", "w_m_out", "w_o", "final_norm_w"]
OUTPUTS = {"y_prompt": (1, SEQ, D), "y_sample": (NB, 1, D), "p_conv_a": (1, 1, KA - 1, D),
           "p_conv_s": (1, 1, KS - 1, XBC), "p_ssm": (1, 1, HEADS, HD, NS), "p_mem_k": (1, 1, NM, MH, MD),
           "p_mem_v": (1, 1, NM, MH, MD), "s_conv_a": (1, NB, KA - 1, D), "s_conv_s": (1, NB, KS - 1, XBC),
           "s_ssm": (1, NB, HEADS, HD, NS)}


def kernel(**inputs):
    import numpy as np
    import concourse.bacc as bacc
    from concourse.bass_utils import run_bass_kernel_spmd

    nc = bacc.Bacc("TRN2", target_bir_lowering=False, num_devices=1)
    arrays, ins, outs = {}, {}, {}
    for name in INPUTS:
        a = np.ascontiguousarray(inputs[name])
        arrays[f"in_{name}"] = a
        ins[name] = nc.dram_tensor(f"in_{name}", a.shape, F32, kind="ExternalInput").ap()
    for name, shape in OUTPUTS.items():
        outs[name] = nc.dram_tensor(f"out_{name}", shape, F32, kind="ExternalOutput").ap()
    build(nc, ins, outs)
    r = run_bass_kernel_spmd(nc, [arrays], core_ids=[0])
    return tuple(r.results[0][f"out_{name}"] for name in OUTPUTS)
```
